# Optimizing a Trainium2 kernel written in Bass

```python
import jax, jax.numpy as jnp
from jax import lax
import numpy as np

D_MODEL = 1024
BATCH = 1
SEQ = 512
DEPTH = 2

HEAD_DIM = 64
N_FOX_HEADS = 8
N_MOBA_HEADS = 8
FOX_WIDTH = N_FOX_HEADS * HEAD_DIM
MOBA_WIDTH = N_MOBA_HEADS * HEAD_DIM
ATTN_WIDTH = FOX_WIDTH + MOBA_WIDTH
IN_COLS = 3 * ATTN_WIDTH + N_FOX_HEADS
Q_BLOCK = 128
MOBA_BLOCK = 256
MOBA_TOPK = 3
MOBA_Q_CHUNK = 32
N_RWKV_HEADS = D_MODEL // HEAD_DIM
D_DECAY_LORA = 64
D_AAA_LORA = 64
D_GATE_LORA = 160
D_FF = -(-8 * D_MODEL // (3 * 256)) * 256
NORM_EPS = 1e-6
GN_EPS = HEAD_DIM * 1e-5
N_EVEN = (DEPTH + 1) // 2
N_ODD = DEPTH // 2

kernel_name = "fox_moba_rwkv7_adaln_hybrid"

F32 = jnp.float32

def rmsnorm(x, g):
    xf = x.astype(F32)
    y = xf * lax.rsqrt(jnp.mean(xf * xf, axis=-1, keepdims=True) + NORM_EPS)
    return y.astype(x.dtype) * g

def modulate(h, shift, scale):
    return h * (1.0 + scale[:, None, :]) + shift[:, None, :]

def split_heads(t, n_heads):
    b, s, _ = t.shape
    return t.reshape(b, s, n_heads, HEAD_DIM).transpose(0, 2, 1, 3)

def fox_attention(q, k, v, f_logit):
    b, h, s, dh = q.shape
    cum = jnp.cumsum(jax.nn.log_sigmoid(f_logit.astype(F32)), axis=-1)
    q = q * (dh ** -0.5)
    outs = []
    for i in range(s // Q_BLOCK):
        lo, hi = i * Q_BLOCK, (i + 1) * Q_BLOCK
        logits = jnp.einsum('bhqd,bhkd->bhqk', q[:, :, lo:hi], k[:, :, :hi]).astype(F32)
        logits = logits + cum[:, :, lo:hi, None] - cum[:, :, None, :hi]
        causal = jnp.arange(lo, hi)[:, None] >= jnp.arange(hi)[None, :]
        p = jax.nn.softmax(jnp.where(causal, logits, -jnp.inf), axis=-1)
        outs.append(jnp.einsum('bhqk,bhkd->bhqd', p.astype(v.dtype), v[:, :, :hi]))
    return jnp.concatenate(outs, axis=2)

def moba_attention(q, k, v):
    b, h, s, dh = q.shape
    nb = -(-s // MOBA_BLOCK)
    pad = nb * MOBA_BLOCK - s
    padw = ((0, 0), (0, 0), (0, pad), (0, 0))
    k_blocks = jnp.pad(k, padw).reshape(b, h, nb, MOBA_BLOCK, dh)
    v_blocks = jnp.pad(v, padw).reshape(b, h, nb, MOBA_BLOCK, dh)
    q = q * (dh ** -0.5)
    k_mean = jnp.mean(k_blocks.astype(F32), axis=3)
    q_blk = jnp.arange(s) // MOBA_BLOCK
    gate = jnp.einsum('bhsd,bhnd->bhsn', q.astype(F32), k_mean)
    fully_past = jnp.arange(nb)[None, :] < q_blk[:, None]
    gate = jnp.where(fully_past, gate, -jnp.inf)
    n_sel = min(MOBA_TOPK, nb)
    _, sel_idx = lax.top_k(gate, n_sel)
    sel_valid = jnp.arange(n_sel)[None, :] < q_blk[:, None]

    nc = s // MOBA_Q_CHUNK
    q_c = jnp.moveaxis(q.reshape(b, h, nc, MOBA_Q_CHUNK, dh), 2, 0)
    idx_c = jnp.moveaxis(sel_idx.reshape(b, h, nc, MOBA_Q_CHUNK, n_sel), 2, 0)
    valid_c = sel_valid.reshape(nc, MOBA_Q_CHUNK, n_sel)
    gather = jax.vmap(jax.vmap(lambda blocks, idx: blocks[idx]))

    def chunk(args):
        qq, ii, vv, ci = args
        qpos = ci * MOBA_Q_CHUNK + jnp.arange(MOBA_Q_CHUNK)
        own = (ci * MOBA_Q_CHUNK) // MOBA_BLOCK
        kg = gather(k_blocks, ii)
        vg = gather(v_blocks, ii)
        s_sel = jnp.einsum('bhqd,bhqnkd->bhqnk', qq, kg).astype(F32)
        s_sel = jnp.where(vv[None, None, :, :, None], s_sel, -jnp.inf)
        k_own = lax.dynamic_index_in_dim(k_blocks, own, axis=2, keepdims=False)
        v_own = lax.dynamic_index_in_dim(v_blocks, own, axis=2, keepdims=False)
        s_own = jnp.einsum('bhqd,bhkd->bhqk', qq, k_own).astype(F32)
        own_pos = own * MOBA_BLOCK + jnp.arange(MOBA_BLOCK)
        s_own = jnp.where(own_pos[None, :] <= qpos[:, None], s_own, -jnp.inf)
        logits = jnp.concatenate([s_sel.reshape(b, h, MOBA_Q_CHUNK, n_sel * MOBA_BLOCK), s_own], axis=-1)
        p = jax.nn.softmax(logits, axis=-1).astype(v.dtype)
        p_sel = p[..., :n_sel * MOBA_BLOCK].reshape(b, h, MOBA_Q_CHUNK, n_sel, MOBA_BLOCK)
        p_own = p[..., n_sel * MOBA_BLOCK:]
        return (jnp.einsum('bhqnk,bhqnkd->bhqd', p_sel, vg)
                + jnp.einsum('bhqk,bhkd->bhqd', p_own, v_own))

    out = lax.map(chunk, (q_c, idx_c, valid_c, jnp.arange(nc)))
    return jnp.moveaxis(out, 0, 2).reshape(b, h, s, dh)

def parallel_attention(h, w_in, b_f, w_out):
    b, s, _ = h.shape
    proj = h @ w_in
    qa, ka, va, qb, kb, vb = [proj[..., i * FOX_WIDTH:(i + 1) * FOX_WIDTH] for i in range(6)]
    f_logit = (proj[..., 3 * ATTN_WIDTH:] + b_f).transpose(0, 2, 1)
    o_a = fox_attention(split_heads(qa, N_FOX_HEADS), split_heads(ka, N_FOX_HEADS),
                        split_heads(va, N_FOX_HEADS), f_logit)
    o_b = moba_attention(split_heads(qb, N_MOBA_HEADS), split_heads(kb, N_MOBA_HEADS),
                         split_heads(vb, N_MOBA_HEADS))
    o = jnp.concatenate([o_a, o_b], axis=1)
    return o.transpose(0, 2, 1, 3).reshape(b, s, ATTN_WIDTH) @ w_out

def rwkv7_step(state, inp):
    r_t, w_t, k_t, v_t, a_t, b_t = inp
    sa = jnp.einsum('bhij,bhj->bhi', state, a_t)
    state = (state * w_t[:, :, None, :] + sa[..., None] * b_t[:, :, None, :]
             + v_t[..., None] * k_t[:, :, None, :])
    return state, jnp.einsum('bhij,bhj->bhi', state, r_t)

def rwkv7_time_mix(h, mu, w_r, w_k, w_v, w_o, w0, w1, w2, a0, a1, a2, g1, g2,
                   k_k, k_a, r_k, ln_w, ln_b):
    b, s, d = h.shape
    nh, n = N_RWKV_HEADS, HEAD_DIM
    xx = jnp.pad(h, ((0, 0), (1, 0), (0, 0)))[:, :-1] - h
    xr, xw, xk, xv, xa, xg = [h + xx * mu[i] for i in range(6)]
    r = xr @ w_r
    k = xk @ w_k
    v = xv @ w_v
    w_log = -jax.nn.softplus(-(w0 + jnp.tanh(xw @ w1) @ w2).astype(F32)) - 0.5
    decay = jnp.exp(-jnp.exp(w_log))
    a = jax.nn.sigmoid(a0 + (xa @ a1) @ a2)
    g = jax.nn.sigmoid(xg @ g1) @ g2
    kk = (k * k_k).reshape(b, s, nh, n).astype(F32)
    kk = kk / jnp.maximum(jnp.sqrt(jnp.sum(kk * kk, axis=-1, keepdims=True)), 1e-12)
    k = k * (1.0 + (a - 1.0) * k_a)
    heads = lambda t: t.reshape(b, s, nh, n).astype(F32)
    r_h, k_h, v_h, a_h, dec_h = heads(r), heads(k), heads(v), heads(a), heads(decay)
    xs = tuple(jnp.moveaxis(t, 1, 0) for t in (r_h, dec_h, k_h, v_h, -kk, kk * a_h))
    state0 = jnp.zeros((b, nh, n, n), F32)
    _, y = lax.scan(rwkv7_step, state0, xs)
    y = jnp.moveaxis(y, 0, 1)
    mean = jnp.mean(y, axis=-1, keepdims=True)
    var = jnp.mean(jnp.square(y - mean), axis=-1, keepdims=True)
    y = (y - mean) * lax.rsqrt(var + GN_EPS) * ln_w.reshape(nh, n).astype(F32) + ln_b.reshape(nh, n).astype(F32)
    bonus = jnp.sum(r_h * k_h * r_k.astype(F32), axis=-1, keepdims=True) * v_h
    out = (y + bonus).reshape(b, s, d).astype(h.dtype) * g
    return out @ w_o

def swiglu(h, w_in, w_out):
    gate, up = jnp.split(h @ w_in, 2, axis=-1)
    return (jax.nn.silu(gate) * up) @ w_out

def setup_inputs(seed: int = 0) -> dict:
    key = jax.random.key(seed)
    ks = iter(jax.random.split(key, 40))
    D = D_MODEL
    nrm = lambda shape, scale: jax.random.normal(next(ks), shape, F32) * scale
    uni = lambda shape, lo, hi: jax.random.uniform(next(ks), shape, F32, lo, hi)
    return {
        "x": nrm((BATCH, SEQ, D), 1.0),
        "c": nrm((BATCH, D), 1.0),
        "attn_w_in": nrm((N_EVEN, D, IN_COLS), D ** -0.5),
        "attn_b_f": uni((N_EVEN, N_FOX_HEADS), 1.0, 6.0),
        "attn_w_out": nrm((N_EVEN, ATTN_WIDTH, D), ATTN_WIDTH ** -0.5),
        "rwkv_mu": uni((N_ODD, 6, D), 0.0, 1.0),
        "rwkv_w_r": nrm((N_ODD, D, D), D ** -0.5),
        "rwkv_w_k": nrm((N_ODD, D, D), D ** -0.5),
        "rwkv_w_v": nrm((N_ODD, D, D), D ** -0.5),
        "rwkv_w_o": nrm((N_ODD, D, D), D ** -0.5),
        "rwkv_w0": uni((N_ODD, D), -6.0, -1.0),
        "rwkv_w1": nrm((N_ODD, D, D_DECAY_LORA), D ** -0.5),
        "rwkv_w2": nrm((N_ODD, D_DECAY_LORA, D), 0.5 * D_DECAY_LORA ** -0.5),
        "rwkv_a0": nrm((N_ODD, D), 0.1),
        "rwkv_a1": nrm((N_ODD, D, D_AAA_LORA), D ** -0.5),
        "rwkv_a2": nrm((N_ODD, D_AAA_LORA, D), 0.5 * D_AAA_LORA ** -0.5),
        "rwkv_g1": nrm((N_ODD, D, D_GATE_LORA), D ** -0.5),
        "rwkv_g2": nrm((N_ODD, D_GATE_LORA, D), D_GATE_LORA ** -0.5),
        "rwkv_k_k": 0.85 + nrm((N_ODD, D), 0.05),
        "rwkv_k_a": 1.0 + nrm((N_ODD, D), 0.05),
        "rwkv_r_k": nrm((N_ODD, N_RWKV_HEADS, HEAD_DIM), 0.1),
        "rwkv_ln_w": 1.0 + nrm((N_ODD, D), 0.05),
        "rwkv_ln_b": nrm((N_ODD, D), 0.02),
        "mod_w": nrm((DEPTH, D, 6 * D), 0.5 * D ** -0.5),
        "mod_b": nrm((DEPTH, 6 * D), 0.02),
        "norm_mix": 1.0 + nrm((DEPTH, D), 0.05),
        "norm_ffn": 1.0 + nrm((DEPTH, D), 0.05),
        "ffn_w_in": nrm((DEPTH, D, 2 * D_FF), D ** -0.5),
        "ffn_w_out": nrm((DEPTH, D_FF, D), D_FF ** -0.5),
        "norm_final": 1.0 + nrm((D,), 0.05),
    }

def reference(x, c, attn_w_in, attn_b_f, attn_w_out, rwkv_mu, rwkv_w_r, rwkv_w_k, rwkv_w_v,
              rwkv_w_o, rwkv_w0, rwkv_w1, rwkv_w2, rwkv_a0, rwkv_a1, rwkv_a2, rwkv_g1, rwkv_g2,
              rwkv_k_k, rwkv_k_a, rwkv_r_k, rwkv_ln_w, rwkv_ln_b, mod_w, mod_b, norm_mix,
              norm_ffn, ffn_w_in, ffn_w_out, norm_final):
    cond = jax.nn.silu(c)
    for i in range(DEPTH):
        mod = cond @ mod_w[i] + mod_b[i]
        sh_m, sc_m, gt_m, sh_f, sc_f, gt_f = jnp.split(mod, 6, axis=-1)
        h = modulate(rmsnorm(x, norm_mix[i]), sh_m, sc_m)
        j = i // 2
        if i % 2 == 0:
            y = parallel_attention(h, attn_w_in[j], attn_b_f[j], attn_w_out[j])
        else:
            y = rwkv7_time_mix(h, rwkv_mu[j], rwkv_w_r[j], rwkv_w_k[j], rwkv_w_v[j], rwkv_w_o[j],
                               rwkv_w0[j], rwkv_w1[j], rwkv_w2[j], rwkv_a0[j], rwkv_a1[j],
                               rwkv_a2[j], rwkv_g1[j], rwkv_g2[j], rwkv_k_k[j], rwkv_k_a[j],
                               rwkv_r_k[j], rwkv_ln_w[j], rwkv_ln_b[j])
        x = x + gt_m[:, None, :] * y
        h = modulate(rmsnorm(x, norm_ffn[i]), sh_f, sc_f)
        x = x + gt_f[:, None, :] * swiglu(h, ffn_w_in[i], ffn_w_out[i])
    return rmsnorm(x, norm_final)


_drawn_inputs = setup_inputs


def setup_inputs(seed=0):
    import zlib

    import numpy as np

    out = dict(_drawn_inputs(seed))
    spreads = {}
    factors = {'rwkv_w1': 7.696,
     'rwkv_w2': 8.0,
     'rwkv_a0': 8.0,
     'rwkv_k_k': 33.872,
     'rwkv_k_a': 4.277,
     'rwkv_ln_w': 30.835,
     'rwkv_ln_b': 64.0,
     'norm_mix': 3.336,
     'norm_ffn': 2.708}
    for name, (base, spread) in spreads.items():
        noise = np.random.default_rng([zlib.crc32(name.encode()), seed]).standard_normal(out[name].shape)
        drawn = base * np.exp(spread * noise) if base else spread * noise
        out[name] = __import__('jax').numpy.asarray(drawn.astype(out[name].dtype))
    for name, factor in factors.items():
        out[name] = (out[name] * factor).astype(out[name].dtype)
    return out
```

```python
from contextlib import ExitStack

import concourse.bass as bass
from concourse import mybir

F32 = mybir.dt.float32
F32R = mybir.dt.float32r
BF16 = mybir.dt.bfloat16
ALU = mybir.AluOpType
ACT = mybir.ActivationFunctionType
AX_X = mybir.AxisListType.X

P = 128
S = 512
D = 1024
KT = D // P
TT = S // P
HD = 64
NH = 16
NFOX = 8
FF = 2816
FT = FF // P
EPS = 1e-6
GN_EPS = HD * 1e-5
NEG = -1e30
DECAY = -0.6065306597126334
CH = 64
NC = S // CH
GL = 160
LOG_NORM = 6.931471805599453
RAW = 4
SPLIT = 2
NB = 4
OUT_PARTS = ((0, 8), (8, 7), (15, 7))

QKV, AO, FI0, FO0, RKV, WO, FI1, FO1, CHUNKS = 0, 24, 32, 76, 100, 124, 132, 176, 200
T_QKV, T_AO, T_FI0, T_FO0, T_RKV, T_WO, T_FI1, T_FO1 = 0, 24, 32, 76, 84, 108, 116, 160

H_MIX0, H_ATT, H_FFN0, H_R, H_K, H_V, H_WO, H_FFN1 = 0, 8, 16, 24, 32, 40, 48, 56
LAYERS = 2
LAST = 2 * LAYERS
CONSTS = 21
MASKS = 36
COL = (0, 128, 384, 768, 1280)
PT_BANK = (4, 5, 6, 6)
PT_OFF = (0, 0, 0, 256)

A_C, A_MODB, A_NMIX = 0, 8, 104
A_ROWS = 120
B_NFFN, B_NFIN, B_MU, B_W0, B_A0, B_KK, B_KA, B_RK, B_LNW, B_LNB = 0, 16, 24, 72, 80, 88, 96, 104, 112, 120


def rwkv_order():
    for p in range(KT + 1):
        steps = iter([(kind, p - 1, n) for n in range(NC) for kind in ("step", "out")] if p else [])
        own = []
        if p < KT:
            own = [("prep", p), ("tok", p)] + [("pairs", p, q) for q in range(8)] + [("intra", p), ("join", p, 0)]
            for l in range(1, 6):
                own += [("join", p, l), ("grow", p, l)]
        for seg in own:
            yield seg
            for _ in range(1):
                s = next(steps, None)
                if s:
                    yield s
        yield from steps
        if p < KT:
            yield ("wu", p)


def build(nc, a, out, dump=None):
    with ExitStack() as ctx:
        program(nc, a, out, ctx, dump)


def program(nc, a, out, ctx, dump):
    def sb(name, shape, dt=F32, scope=ctx):
        return scope.enter_context(nc.sbuf_tensor(name, shape, dt))

    def sem(name):
        return ctx.enter_context(nc.semaphore(name))

    bank = [ctx.enter_context(nc.psum_tensor(f"bank{i}", [P, S], F32)) for i in range(8)]

    x = sb("x", [P, KT, S])
    raw = sb("raw", [P, RAW, KT, P])
    w_hi = sb("w_hi", [P, SPLIT, KT, P], F32R)
    w_lo = sb("w_lo", [P, SPLIT, KT, P], F32R)
    ident = sb("ident", [P, P])
    ident_b = sb("ident_b", [P, P], BF16)
    causal = sb("causal", [P, P], BF16)
    ones = sb("ones", [P, P])
    cst = sb("cst", [P, 8])
    par_a = sb("par_a", [P, A_ROWS])
    par_b = sb("par_b", [P, P])
    rows_a = sb("rows_a", [A_ROWS, P])
    rows_b = sb("rows_b", [P, P])
    cond = sb("cond", [P, KT])
    mod_t = sb("mod_t", [P, 2, 6 * KT])
    gain = sb("gain", [P, 4, KT])
    fox_sel = sb("fox_sel", [P, NFOX])
    qkv_scale = sb("qkv_scale", [P, 24])
    ring = sb("ring", [P, 4, S])
    ssq = sb("ssq", [P, S])
    rstd = sb("rstd", [P, S])
    h_scope = ExitStack()
    h_hi = sb("h_hi", [P, KT, S], F32R, h_scope)
    h_lo = sb("h_lo", [P, KT, S], F32R, h_scope)
    mod_scope = ExitStack()
    mod_raw = sb("mod_raw", [P, 2, D], F32, mod_scope)
    mod_acc = sb("mod_acc", [P, D], F32, mod_scope)
    with ExitStack() as s0:
        x_tok = sb("x_tok", [P, TT, D], F32, s0)
        mod_first = sb("mod_first", [P, 2 * KT, D], F32, s0)
    with ExitStack() as s1:
        qkv = sb("qkv", [P, 24, S], F32, s1)
        prob = sb("prob", [P, 2, 1280], F32, s1)
        prob_t = sb("prob_t", [P, 2, 1280], F32, s1)
        decay_h = sb("decay_h", [P, 2, S], F32, s1)
        row_stat = sb("row_stat", [P, 2, 3, TT], F32, s1)
        with ExitStack() as s2:
            v_tok = sb("v_tok", [P, TT, D], F32, s2)
        with ExitStack() as s2:
            sb("start_up_tiles", [P, 2048], F32, s2)
            wf_raw = sb("wf_raw", [P, KT, NFOX], F32, s2)
            wf_hi = sb("wf_hi", [P, KT, P], F32R, s2)
            wf_lo = sb("wf_lo", [P, KT, P], F32R, s2)
            decay_l = sb("decay_l", [P, S], F32, s2)
            decay_r = sb("decay_r", [P, S], F32, s2)
            b_f = sb("b_f", [P, 1], F32, s2)
    with ExitStack() as s1:
        y_tok = sb("y_tok", [P, TT, D], F32, s1)
    with ExitStack() as s1:
        g_hi = sb("g_hi", [P, FT, S], F32R, s1)
        g_lo = sb("g_lo", [P, FT, S], F32R, s1)
    mod_scope.close()
    rw_scope = ExitStack()
    rkv = sb("rkv", [P, 3 * KT, S], F32, rw_scope)
    wa_mid = sb("wa_mid", [P, S], F32, rw_scope)
    g_mid = sb("g_mid", [P, 2, S], F32, rw_scope)
    wa2 = sb("wa2", [P, D], F32, rw_scope)
    levels = sb("levels", [P, 6, P], F32, rw_scope)
    before = sb("before", [P, 2, P], F32, rw_scope)
    heads2 = sb("heads2", [P, P], F32, rw_scope)
    restart = sb("restart", [P, S], F32, rw_scope)
    with ExitStack() as s1:
        h_f = sb("h_f", [P, KT, S + 4], F32, s1)
        xx = sb("xx", [P, KT, S], F32, s1)
        w1 = sb("w1", [P, KT, HD], F32, s1)
        a1 = sb("a1", [P, KT, HD], F32, s1)
        g1 = sb("g1", [P, KT, GL], F32, s1)
    with ExitStack() as s1:
        lt = sb("lt", [P, 8, 2, P], F32, s1)
        a_f = sb("a_f", [P, S], F32, s1)
        b_f32 = sb("b_feat", [P, S], F32, s1)
        a_tok = sb("a_tok", [P, TT, P], F32, s1)
        bkv_tok = sb("bkv_tok", [P, 2, 3, TT, P], F32, s1)
        u_tok = sb("u_tok", [P, 2, TT, P], F32, s1)
        w_f = sb("w_f", [P, 2, S], F32, s1)
        tmp = sb("tmp", [P, 3, S], F32, s1)
        state = sb("state", [P, P], F32, s1)
        state_t = sb("state_t", [P, P], F32, s1)
        bonus_w = sb("bonus_w", [P, P], F32, s1)
        chunk_decay = sb("chunk_decay", [P, 2, NC], F32, s1)
    with ExitStack() as s1:
        g2 = sb("g2", [P, 2, D], F32, s1)
    rw_scope.close()
    h_scope.close()
    with ExitStack() as s1:
        at = sb("at", [P, 2, 8, 2, P], F32, s1)
        inv = sb("inv", [P, 8, P], F32, s1)
        inv_t = sb("inv_t", [P, 8, P], F32, s1)
        join_t = sb("join_t", [P, 8, P], F32, s1)
        prod = sb("prod", [P, 8, P], F32, s1)

    s_rows = sem("s_rows")
    s_x_tok = sem("s_x_tok")
    s_mod_first = [sem(f"s_mod_first{i}") for i in range(8)]
    s_wf = sem("s_wf")
    s_raw = [sem(f"s_raw{i}") for i in range(RAW)]
    s_mod_raw = [sem(f"s_mod_raw{i}") for i in range(2)]
    s_hi = sem("s_hi")
    s_lo = sem("s_lo")
    s_mm = sem("s_mm")
    s_bank = sem("s_bank")
    s_const = sem("s_const")
    s_par_t = sem("s_par_t")
    s_par = sem("s_par")
    s_cond = sem("s_cond")
    s_xt = sem("s_xt")
    s_x0 = sem("s_x0")
    s_mod_used = sem("s_mod_used")
    s_mod0 = sem("s_mod0")
    s_mod_sum = sem("s_mod_sum")
    s_mod = sem("s_mod")
    s_gain = sem("s_gain")
    s_sq = sem("s_sq")
    s_ssq = sem("s_ssq")
    s_ssq0 = sem("s_ssq0")
    s_ssum = sem("s_ssum")
    s_ln = sem("s_ln")
    s_rstd = sem("s_rstd")
    s_u = sem("s_u")
    s_h_hi = sem("s_h_hi")
    s_h = sem("s_h")
    s_v_t = sem("s_v_t")
    s_v_tok = sem("s_v_tok")
    s_v_tokv = sem("s_v_tokv")
    s_wf_split = sem("s_wf_split")
    s_f = sem("s_f")
    s_fa = sem("s_fa")
    s_fv = sem("s_fv")
    s_fv0 = sem("s_fv0")
    s_wf_lo = sem("s_wf_lo")
    s_dh = sem("s_dh")
    s_score = sem("s_score")
    s_max = sem("s_max")
    s_exp = sem("s_exp")
    s_rinv = sem("s_rinv")
    s_norm = sem("s_norm")
    s_pt = sem("s_pt")
    s_pt_a = sem("s_pt_a")
    s_pt_v = sem("s_pt_v")
    s_pv = sem("s_pv")
    s_silu = sem("s_silu")
    s_g_hi = sem("s_g_hi")
    s_g = sem("s_g")
    s_y_t = sem("s_y_t")
    s_y = sem("s_y")
    s_out = sem("s_out")
    s_fin = sem("s_fin")

    r_lora_w = sem("r_lora_w")
    r_mix = sem("r_mix")
    r_lora = sem("r_lora")
    r_mid = sem("r_mid")
    r_hf = sem("r_hf")
    r_xx = sem("r_xx")
    r_hf0 = sem("r_hf0")
    r_mask = sem("r_mask")
    r_lora_mm = sem("r_lora_mm")
    r_sig = sem("r_sig")
    r_cum = sem("r_cum")
    r_cprev = sem("r_cprev")
    r_sqk = sem("r_sqk")
    r_ss = sem("r_ss")
    r_ssm = sem("r_ssm")
    r_rn = sem("r_rn")
    r_kk = sem("r_kk")
    r_b = sem("r_b")
    r_t = sem("r_t")
    r_k1 = sem("r_k1")
    r_prd = sem("r_prd")
    r_dec = sem("r_dec")
    r_prep = sem("r_prep")
    r_tm = sem("r_tm")
    r_tma = sem("r_tma")
    r_tmv = sem("r_tmv")
    r_pm = sem("r_pm")
    r_pe = sem("r_pe")
    r_xm = sem("r_xm")
    r_xv = sem("r_xv")
    r_m = sem("r_m")
    r_dt0 = sem("r_dt0")
    r_d0t = sem("r_d0t")
    r_d0 = sem("r_d0")
    r_zm = sem("r_zm")
    r_z = sem("r_z")
    r_dm = sem("r_dm")
    r_d = sem("r_d")
    r_wm = sem("r_wm")
    r_w = sem("r_w")
    r_um0 = sem("r_um0")
    r_u0 = sem("r_u0")
    r_um = sem("r_um")
    r_u = sem("r_u")
    r_kv = sem("r_kv")
    r_sm = sem("r_sm")
    r_ys = sem("r_ys")
    r_ym = sem("r_ym")
    r_s1 = sem("r_s1")
    r_s2 = sem("r_s2")
    r_y = sem("r_y")
    r_br = sem("r_br")
    r_bon = sem("r_bon")
    r_bwt = sem("r_bwt")
    r_mean = sem("r_mean")
    r_yc = sem("r_yc")
    r_ysq = sem("r_ysq")
    r_var = sem("r_var")
    r_gmm = sem("r_gmm")
    r_grs = sem("r_grs")
    r_yn = sem("r_yn")
    r_z1 = sem("r_z1")
    r_z2 = sem("r_z2")
    r_g2 = sem("r_g2")
    r_s0 = sem("r_s0")

    w_rkv = [a[f"rwkv_w_{n}"][0].rearrange("(k p) n -> p k n", p=P) for n in "rkv"]
    w_wo = a["rwkv_w_o"][0].rearrange("(k p) n -> p k n", p=P)
    w_in = a["attn_w_in"][0].rearrange("(k p) n -> p k n", p=P)
    w_ao = a["attn_w_out"][0].rearrange("(k p) n -> p k n", p=P)
    w_fi = [a["ffn_w_in"][l].rearrange("(k p) n -> p k n", p=P) for l in range(2)]
    w_fo = [a["ffn_w_out"][l].rearrange("(k p) n -> p k n", p=P) for l in range(2)]
    w_mod = [a["mod_w"][l].rearrange("(k p) n -> p k n", p=P) for l in range(2)]
    x_dram = a["x"][0].rearrange("(t p) d -> p t d", p=P)
    out_dram = out[0].rearrange("(t p) d -> p t d", p=P)

    score_of = lambda qt: bank[qt][:, 0:(qt + 1) * P]
    h_of = (lambda k: h_hi[:, k, :], lambda k: h_lo[:, k, :])
    g_of = (lambda k: g_hi[:, k, :], lambda k: g_lo[:, k, :])


    block = ctx.enter_context(nc.Block())

    @block.sync
    def _(sp):
        def load(base, per, i, j, src, tiles=KT):
            sp.wait_ge(s_lo, per * i + (base + j + 1))
            sp.dma_start(raw[:, j % RAW, 0:tiles, :], src).then_inc(s_raw[j % RAW], 16)

        def load_mod(layer, i, k, v):
            sp.wait_ge(s_mod_used, KT * i + (k + 1))
            sp.dma_start(mod_raw[:, k % 2, :], w_mod[layer][:, k, bass.ts(v, D)]).then_inc(s_mod_raw[k % 2], 16)

        sp.dma_start(x_tok[:, :, :], x_dram).then_inc(s_x_tok, 16)
        for n in range(8):
            v, k = n // 4, 2 * (n % 4)
            sp.dma_start(mod_first[:, 2 * n:2 * n + 2, :],
                         w_mod[0][:, k:k + 2, v * D:(v + 1) * D]).then_inc(s_mod_first[n], 16)

        def four(base, i, w):
            for j in range(4):
                load(base, 4, i, j, w[:, :, bass.ts(i * 4 + j, P)])

        with sp.Fori(0, 4) as i:
            for j in range(4):
                load(QKV, 4, i, j, w_in[:, :, bass.ts(i * 4 + j, P)])
                for k in (2 * j, 2 * j + 1):
                    load_mod(0, i, k, i + 2)
        with sp.Fori(4, 6) as i:
            four(QKV, i, w_in)

        def square(base, w):
            with sp.Fori(0, 2) as i:
                four(base, i, w)

        def swiglu(layer, base_in, base_out):
            def weights(i, j):
                for half in range(2):
                    load(base_in, 8, i, 2 * j + half, w_fi[layer][:, :, bass.ds((i * 4 + j + FT * half) * P, P)])

            with sp.Fori(0, 5) as i:
                for j in range(4):
                    weights(i, j)
                    if layer == 0:
                        load_mod(1, i + 4, 2 * j, i)
                        load_mod(1, i + 4, 2 * j + 1, i)
            weights(5, 0)
            weights(5, 1)
            if layer == 0:
                for k in range(KT):
                    load_mod(1, 9, k, 5)
            with sp.Fori(0, 2) as i:
                for j in range(4):
                    for c, (k0, kn) in enumerate(OUT_PARTS):
                        load(base_out, 12, i, 3 * j + c, w_fo[layer][:, k0:k0 + kn, bass.ts(i * 4 + j, P)], kn)

        square(AO, w_ao)
        swiglu(0, FI0, FO0)
        if LAYERS == 2:
            sp.wait_ge(s_mm, SPLIT + RKV)
            sp.dma_start(w1[:, :, :], a["rwkv_w1"][0].rearrange("(k p) n -> p k n", p=P)).then_inc(r_lora_w, 16)
            sp.dma_start(a1[:, :, :], a["rwkv_a1"][0].rearrange("(k p) n -> p k n", p=P)).then_inc(r_lora_w, 16)
            sp.dma_start(g1[:, :, :], a["rwkv_g1"][0].rearrange("(k p) n -> p k n", p=P)).then_inc(r_lora_w, 16)
            sp.dma_start(wa2[0:HD, :], a["rwkv_w2"][0]).then_inc(r_lora_w, 16)
            sp.dma_start(wa2[HD:P, :], a["rwkv_a2"][0]).then_inc(r_lora_w, 16)
            for n in range(3):
                with sp.Fori(0, 2) as i:
                    four(RKV + 8 * n, i, w_rkv[n])
            four(WO, 0, w_wo)
            sp.wait_ge(r_m, 6 * KT)
            sp.wait_ge(r_xm, KT)
            sp.dma_start(g2[:, 0, :], a["rwkv_g2"][0, 0:P, :]).then_inc(r_g2, 16)
            sp.dma_start(g2[0:GL - P, 1, :], a["rwkv_g2"][0, P:GL, :]).then_inc(r_g2, 16)
            four(WO, 1, w_wo)
            swiglu(1, FI1, FO1)
        for half in range(2):
            sp.wait_ge(s_y, 4 * half + 4)
            cols = slice(half * D // 2, (half + 1) * D // 2)
            sp.dma_start(out_dram[:, :, cols], y_tok[:, :, cols]).then_inc(s_out, 16)
        sp.wait_ge(s_out, 32)

    @block.gpsimd
    def _(pool):
        const = [0]

        def step(ins):
            const[0] += 1
            ins.then_inc(s_const, 1)
            pool.wait_ge(s_const, const[0])

        step(pool.memset(ident[:, :], 0.0))
        step(pool.affine_select(out=ident[:, :], in_=ident[:, :], pattern=[[-1, P]], compare_op=ALU.not_equal,
                                fill=1.0, base=0, channel_multiplier=1))
        step(pool.memset(ones[:, :], 1.0))
        step(pool.tensor_copy(ident_b[:, :], ident[:, :]))
        step(pool.memset(causal[:, :], 0.0))
        step(pool.affine_select(out=causal[:, :], in_=causal[:, :], pattern=[[-1, P]], compare_op=ALU.is_ge,
                                fill=NEG, base=0, channel_multiplier=1))
        step(pool.memset(cst[:, 0:1], EPS))
        step(pool.memset(cst[:, 1:2], 1.0))
        step(pool.memset(cst[:, 2:3], GN_EPS))
        step(pool.memset(cst[:, 3:4], LOG_NORM))
        step(pool.memset(qkv_scale[:, :], 1.0))
        step(pool.memset(qkv_scale[:, 0:4], HD ** -0.5))
        step(pool.memset(qkv_scale[:, 12:16], HD ** -0.5))
        step(pool.memset(wf_hi[:, :, :].bitcast(F32), 0.0))
        step(pool.memset(wf_lo[:, :, :].bitcast(F32), 0.0))
        step(pool.memset(fox_sel[:, :], 0.0))
        for row in (0, 32):
            step(pool.affine_select(out=fox_sel[:, :], in_=fox_sel[:, :], pattern=[[-1, NFOX]],
                                    compare_op=ALU.not_equal, fill=1.0, base=-row, channel_multiplier=1))
        step(pool.memset(decay_l[:, :], 0.0))
        step(pool.memset(decay_l[0:NFOX, :], -1.0))
        step(pool.memset(b_f[:, :], 0.0))
        pool.memset(cst[:, 4:5], 0.0).then_inc(s_lo, RAW)
        pool.memset(cst[:, 5:6], 0.0).then_inc(s_mm, SPLIT)
        pool.memset(cst[:, 6:7], 0.0).then_inc(s_bank, NB)
        pool.memset(cst[:, 7:8], 0.0).then_inc(s_mod_used, 2)
        assert const[0] == CONSTS

        def low_parts(lo, hi):
            with pool.Fori(lo // 4, hi // 4) as i:
                for j in range(4):
                    pool.wait_ge(s_hi, 4 * i + (j + 1))
                    pool.tensor_tensor(w_lo[:, j % SPLIT, :, :], raw[:, j % RAW, :, :],
                                       w_hi[:, j % SPLIT, :, :].bitcast(F32), ALU.subtract).then_inc(s_lo, 1)

        low_parts(0, RKV)
        if LAYERS == 2:
            pool.wait_ge(s_mm, SPLIT + RKV)
            mask = [0]

            def mstep(ins):
                mask[0] += 1
                ins.then_inc(r_mask, 1)
                pool.wait_ge(r_mask, mask[0])

            def blocks(dst, size):
                v = dst.rearrange("p (n b) -> p n b", b=size)
                mstep(pool.affine_select(out=v, in_=v, pattern=[[-size, P // size], [0, size]], compare_op=ALU.is_ge,
                                         fill=0.0, base=0, channel_multiplier=1))
                mstep(pool.affine_select(out=v, in_=v, pattern=[[size, P // size], [0, size]], compare_op=ALU.is_ge,
                                         fill=0.0, base=size - 1, channel_multiplier=-1))

            mstep(pool.memset(levels[:, :, :], 1.0))
            mstep(pool.memset(before[:, :, :], 1.0))
            mstep(pool.memset(heads2[:, :], 1.0))
            mstep(pool.memset(restart[:, :], 1.0))
            mstep(pool.memset(restart[:, :].rearrange("p (n c) -> p n c", c=CH)[:, :, 0:1], 0.0))
            for l in range(6):
                blocks(levels[:, l, :], 2 << l)
            blocks(heads2[:, :], HD)
            for l in range(5, 0, -1):
                mstep(pool.tensor_tensor(levels[:, l, :], levels[:, l, :], levels[:, l - 1, :], ALU.subtract))
            for l in range(6):
                mstep(pool.affine_select(out=levels[:, l, :], in_=levels[:, l, :], pattern=[[1, P]], compare_op=ALU.is_gt,
                                         fill=0.0, base=0, channel_multiplier=-1))
            for q, op in enumerate((ALU.is_gt, ALU.is_ge)):
                blocks(before[:, q, :], CH)
                mstep(pool.affine_select(out=before[:, q, :], in_=before[:, q, :], pattern=[[1, P]], compare_op=op,
                                         fill=0.0, base=0, channel_multiplier=-1))
            assert mask[0] == MASKS
            pool.wait_ge(r_hf0, 1)
            for k in range(KT):
                pool.wait_ge(r_hf, k + 1)
                pool.tensor_tensor(xx[:, k, :], h_f[:, k, 3:3 + S], h_f[:, k, 4:4 + S], ALU.subtract).then_inc(r_xx, 1)
            low_parts(RKV, WO)
            for seg in rwkv_order():
                kind, p = seg[0], seg[1]
                if kind == "prep":
                    pool.wait_ge(r_cum, p + 1)
                    pool.tensor_tensor(tmp[:, 0, :], ring[:, 2, :], ring[:, 0, :], ALU.subtract).then_inc(r_cprev, 1)
                    pool.wait_ge(r_kk, p + 1)
                    pool.tensor_tensor(tmp[:, 2, :], tmp[:, 1, :], ring[:, 1, :], ALU.mult).then_inc(r_b, 1)
                elif kind == "join":
                    l = seg[2]
                    if l == 0:
                        pool.wait_ge(r_pe, 16 * p + 16)
                    else:
                        pool.wait_ge(r_zm, 10 * p + 2 * (l - 1)) if l > 1 else pool.wait_ge(r_dt0, p + 1)
                    pool.tensor_tensor(join_t[:, :, :], lt[:, :, 0, :], levels[:, l, :].unsqueeze(1).broadcast_to((P, 8, P)),
                                       ALU.mult).then_inc(r_m, 1)
            low_parts(WO, CHUNKS)

    @block.scalar
    def _(act):
        def split(base, per, i, j):
            if isinstance(i, int) and base + per * i + j + 2 >= total:
                return
            act.wait_ge(s_raw[(j + 2) % RAW], 4 * per * i + 16 * (base // 4 + (j + 2) // 4 + 1))
            act.wait_ge(s_mm, per * i + (base + j + 3))
            act.activation(w_hi[:, j % SPLIT, :, :], raw[:, (j + 2) % RAW, :, :], ACT.Copy).then_inc(s_hi, 1)

        total = CHUNKS if LAYERS == 2 else FO0 + 24
        row = 0
        for src in (a["c"].rearrange("b (k p) -> (b k) p", p=P), a["mod_b"].rearrange("l (k p) -> (l k) p", p=P),
                    a["norm_mix"].rearrange("l (k p) -> (l k) p", p=P)):
            act.dma_start(rows_a[row:row + src.shape[0], :], src).then_inc(s_rows, 16)
            row += src.shape[0]
        row = 0
        for src in (a["norm_ffn"].rearrange("l (k p) -> (l k) p", p=P), a["norm_final"].rearrange("(k p) -> k p", p=P),
                    a["rwkv_mu"][0].rearrange("i (k p) -> (i k) p", p=P), a["rwkv_w0"].rearrange("l (k p) -> (l k) p", p=P),
                    a["rwkv_a0"].rearrange("l (k p) -> (l k) p", p=P), a["rwkv_k_k"].rearrange("l (k p) -> (l k) p", p=P),
                    a["rwkv_k_a"].rearrange("l (k p) -> (l k) p", p=P),
                    a["rwkv_r_k"][0].rearrange("(k g) j -> k (g j)", g=2),
                    a["rwkv_ln_w"].rearrange("l (k p) -> (l k) p", p=P), a["rwkv_ln_b"].rearrange("l (k p) -> (l k) p", p=P)):
            act.dma_start(rows_b[row:row + src.shape[0], :], src).then_inc(s_rows, 16)
            row += src.shape[0]
        act.dma_start(wf_raw[:, :, :], w_in[:, :, 24 * P:24 * P + NFOX]).then_inc(s_wf, 16)
        act.wait_ge(s_const, CONSTS)
        for r0 in (0, 32):
            act.dma_start(b_f[r0:r0 + NFOX, :], a["attn_b_f"].rearrange("l h -> h l")).then_inc(s_wf, 16)

        act.wait_ge(s_par, 1)
        act.activation(cond[:, :], par_a[:, A_C:A_C + KT], ACT.Silu).then_inc(s_cond, 1)
        act.wait_ge(s_mm, SPLIT)
        split(0, 4, 0, -2)
        split(0, 4, 0, -1)
        for k in range(KT):
            act.wait_ge(s_xt, k + 1)
            if k >= 2:
                act.wait_ge(s_ssq, k - 1)
            act.activation(ring[:, k % 2, :], bank[k % 4][:, :], ACT.Square).then_inc(s_sq, 1)
            act.activation(x[:, k, :], bank[k % 4][:, :], ACT.Copy).then_inc(s_x0, 1)
        act.wait_ge(s_wf, 48)
        for r0 in (0, 32):
            act.activation(wf_hi[:, :, r0:r0 + NFOX], wf_raw[:, :, :], ACT.Copy).then_inc(s_wf_split, 1)

        def norm_rstd(n):
            act.wait_ge(s_ssum, n + 1)
            act.activation(rstd[:, :], bank[7][:, :], ACT.Ln, bias=cst[:, 0:1], scale=1.0 / D).then_inc(s_ln, 1)
            act.wait_ge(s_ln, n + 1)
            act.activation(rstd[:, :], rstd[:, :], ACT.Exp, scale=-0.5).then_inc(s_rstd, 1)

        def norm_hi(n, h0, layer, v):
            norm_rstd(n)
            for k in range(KT):
                act.wait_ge(s_u, KT * n + k + 1)
                act.activation(h_hi[:, k, :], ring[:, k % 4, :], ACT.Identity,
                               bias=mod_t[:, layer, v * KT + k:v * KT + k + 1]).then_inc(s_h_hi, 1)

        norm_hi(0, H_MIX0, 0, 0)
        act.wait_ge(s_fv, 2)
        act.activation(ring[:, 2, :], ring[:, 1, :], ACT.Exp).then_inc(s_fa, 1)
        act.wait_ge(s_fa, 1)
        act.activation(ring[:, 3, :], ring[:, 2, :], ACT.Ln, bias=cst[:, 1:2]).then_inc(s_fa, 1)

        def four(base, i):
            for j in range(4):
                split(base, 4, i, j)

        with act.Fori(0, 6) as i:
            four(QKV, i)

        for n in range(0, 8, 2):
            act.wait_ge(s_v_t, n + 1)
            act.activation(v_tok[:, n // 2, (n % 2) * S:(n % 2 + 1) * S], bank[4 + n % 2][:, :], ACT.Copy).then_inc(s_v_tok, 1)
        for h in range(NH + 1):
            if h < NH:
                for qt in range(TT):
                    act.wait_ge(s_max, TT * h + qt + 1)
                    if h >= 2:
                        act.wait_ge(s_pt, h - 1)
                    act.activation(prob[:, h % 2, COL[qt]:COL[qt + 1]], score_of(qt), ACT.Exp,
                                   bias=row_stat[:, h % 2, 0, qt:qt + 1],
                                   accum_out=row_stat[:, h % 2, 1, qt:qt + 1]).then_inc(s_exp, 1)
            if h >= 1:
                g = h - 1
                act.wait_ge(s_pt, g + 1)
                if g >= 2:
                    act.wait_ge(s_pv, g - 1)
                act.activation(prob_t[:, g % 2, 0:S], bank[4][:, :], ACT.Copy).then_inc(s_pt_a, 1)
                if g % 2:
                    pair = g // 2
                    act.wait_ge(s_pv, g + 1)
                    act.activation(h_hi[:, pair, :], bank[7][:, :], ACT.Copy).then_inc(s_h_hi, 1)

        def square_x(n, t0, i, j):
            act.wait_ge(s_bank, 4 * i + (NB + t0 + j + 1))
            act.wait_ge(s_ssq, 4 * i + (KT * n + j - 1))
            act.activation(ring[:, j % 2, :], x[:, i * 4 + j, :], ACT.Square).then_inc(s_sq, 1)

        def square(base, t0, n):
            with act.Fori(0, 2) as i:
                for j in range(4):
                    split(base, 4, i, j)
                    square_x(n, t0, i, j)

        def swiglu(layer, base_in, base_out, t_in, t_out):
            def pairs(i, tiles):
                for j in range(tiles):
                    split(base_in, 8, i, 2 * j)
                    act.wait_ge(s_mm, 8 * i + (SPLIT + base_in + 2 * j + 1))
                    act.activation(ring[:, j % 2, :], bank[2 * j % 4][:, :], ACT.Silu).then_inc(s_silu, 1)
                    split(base_in, 8, i, 2 * j + 1)
                    act.wait_ge(s_bank, 8 * i + (NB + t_in + 2 * j + 2))
                    act.activation(g_hi[:, i * 4 + j, :], ring[:, 2 + j % 2, :], ACT.Copy).then_inc(s_g_hi, 1)

            with act.Fori(0, 5) as i:
                pairs(i, 4)
            pairs(5, 2)

            def out(i):
                for j in range(4):
                    for c in range(3):
                        split(base_out, 12, i, 3 * j + c)
                    square_x(2 + 2 * layer, t_out, i, j)

            with act.Fori(0, 1) as i:
                out(i)
            out(1)

        square(AO, T_AO, 1)
        norm_hi(1, H_FFN0, 0, 3)
        swiglu(0, FI0, FO0, T_FI0, T_FO0)
        if LAYERS == 2:
            norm_rstd(2)
            for k in range(KT):
                act.wait_ge(s_u, KT * 2 + k + 1)
                act.activation(h_f[:, k, 4:4 + S], ring[:, k % 4, :], ACT.Identity,
                               bias=mod_t[:, 1, k:k + 1]).then_inc(r_hf, 1)
            act.wait_ge(r_lora, 8)
            act.activation(wa_mid[0:HD, :], bank[0][0:HD, :], ACT.Tanh).then_inc(r_mid, 1)
            act.wait_ge(r_lora, 16)
            act.activation(wa_mid[HD:P, :], bank[1][HD:P, :], ACT.Copy).then_inc(r_mid, 1)
            act.wait_ge(r_lora, 24)
            act.activation(g_mid[:, 0, :], bank[2][:, :], ACT.Sigmoid).then_inc(r_mid, 1)
            act.activation(g_mid[0:GL - P, 1, :], bank[3][0:GL - P, :], ACT.Sigmoid).then_inc(r_mid, 1)
            for n in range(3):
                if n:
                    act.wait_ge(s_mm, SPLIT + RKV + 8 * n)
                for k in range(KT):
                    act.wait_ge(r_mix, 24 + 8 * n + k + 1)
                    act.activation(h_hi[:, k, :], ring[:, k % 4, :], ACT.Copy).then_inc(s_h_hi, 1)
                with act.Fori(0, 2) as i:
                    four(RKV + 8 * n, i)
            par = lambda b, p: par_b[:, b + p:b + p + 1]
            for seg in rwkv_order():
                kind, p = seg[0], seg[1]
                kp = rkv[:, KT + p, :]
                if kind == "prep":
                    act.wait_ge(r_lora_mm, 2 * p + 2)
                    act.activation(ring[:, 0, :], bank[0][:, :], ACT.Sigmoid, bias=par(B_W0, p)).then_inc(r_sig, 1)
                    act.activation(ring[:, 1, :], bank[1][:, :], ACT.Sigmoid, bias=par(B_A0, p)).then_inc(r_sig, 1)
                    act.activation(ring[:, 3, :], kp, ACT.Square, scale=par(B_KK, p)).then_inc(r_sqk, 1)
                    act.wait_ge(r_ssm, p + 1)
                    act.activation(ring[:, 3, :], ring[:, 3, :], ACT.Ln, scale=2.0 ** 20).then_inc(r_rn, 1)
                    act.wait_ge(r_rn, 2 * p + 1)
                    act.activation(ring[:, 3, :], ring[:, 3, :], ACT.Exp, scale=-0.5, bias=cst[:, 3:4]).then_inc(r_rn, 1)
                    act.wait_ge(r_cprev, p + 1)
                    act.activation(ring[:, 0, :], ring[:, 2, :], ACT.Exp, scale=DECAY).then_inc(r_dec, 1)
                    act.activation(ring[:, 2, :], ring[:, 2, :], ACT.Exp, scale=-DECAY).then_inc(r_dec, 1)
                    act.activation(tmp[:, 0, :], tmp[:, 0, :], ACT.Exp, scale=DECAY).then_inc(r_dec, 1)
                elif kind == "tok":
                    act.wait_ge(r_tm, p + 1)
                    act.activation(a_tok[:, :, :], bank[0][:, :], ACT.Copy).then_inc(r_tma, 1)
                    act.activation(bkv_tok[:, p % 2, 0, :, :], bank[1][:, :], ACT.Copy).then_inc(r_tma, 1)
                elif kind == "intra":
                    act.wait_ge(r_xm, p + 1)
                    act.activation(u_tok[:, p % 2, :, :], bank[4][:, :], ACT.Copy).then_inc(r_xv, 1)
                elif kind == "join" and seg[2] == 0:
                    act.wait_ge(r_d0t, p + 1)
                    for g in range(2):
                        act.activation(inv[:, 4 * g:4 * g + 4, :], bank[g][:, :], ACT.Copy).then_inc(r_d0, 1)
                elif kind == "join":
                    for g in range(2):
                        act.wait_ge(r_zm, 2 * (5 * p + seg[2] - 1) + g + 1)
                        act.activation(prod[:, 4 * g:4 * g + 4, :], bank[g][:, :], ACT.Copy).then_inc(r_z, 1)
                elif kind == "wu":
                    act.wait_ge(r_wm, p + 1)
                    act.activation(w_f[:, p % 2, :], bank[0][:, :], ACT.Copy).then_inc(r_w, 1)
                    act.wait_ge(r_um0, p + 1)
                    act.activation(u_tok[:, p % 2, :, :], bank[1][:, :], ACT.Copy).then_inc(r_u0, 1)
                elif kind == "out":
                    n = seg[2]
                    act.wait_ge(r_ym, NC * p + n + 1)
                    act.activation(kp[:, n * CH:(n + 1) * CH], bank[6][:, 256:256 + CH], ACT.Copy).then_inc(r_y, 1)
            for p in range(KT + 1):
                if p < KT:
                    act.wait_ge(r_yc, p + 1)
                    if p >= 2:
                        act.wait_ge(r_yn, p - 1)
                    act.activation(ring[:, p % 2, :], rkv[:, KT + p, :], ACT.Square).then_inc(r_ysq, 1)
                    act.wait_ge(r_var, p + 1)
                    act.activation(ring[:, p % 2, :], bank[2 + p % 2][:, :], ACT.Ln, scale=1.0 / HD,
                                   bias=cst[:, 2:3]).then_inc(r_grs, 1)
                    act.wait_ge(r_grs, 2 * p + 1)
                    act.activation(ring[:, p % 2, :], ring[:, p % 2, :], ACT.Exp, scale=-0.5).then_inc(r_grs, 1)
                if p >= 1:
                    act.wait_ge(r_z2, p)
                    act.activation(h_hi[:, p - 1, :], ring[:, 2 + (p - 1) % 2, :], ACT.Copy).then_inc(s_h_hi, 1)
            square(WO, T_WO, 3)
            norm_hi(3, H_FFN1, 1, 3)
            swiglu(1, FI1, FO1, T_FI1, T_FO1)
        norm_rstd(LAST)
        for k in range(KT):
            act.wait_ge(s_y_t, k + 1)
            act.activation(y_tok[:, :, k * P:(k + 1) * P], bank[k % 4][:, :].rearrange("p (t f) -> p t f", t=TT),
                           ACT.Copy).then_inc(s_y, 1)

    @block.vector
    def _(dve):
        def gate_col(layer, v, k):
            return mod_t[:, layer, v * KT + k:v * KT + k + 1]

        dve.wait_ge(s_par_t, 1)
        dve.tensor_copy(par_a[:, :], bank[4][:, 0:A_ROWS]).then_inc(s_par, 1)
        dve.tensor_copy(par_b[:, :], bank[5][:, 0:P]).then_inc(s_par, 1)
        dve.memset(ssq[:, :], 0.0).then_inc(s_ssq0, 1)
        dve.memset(decay_r[:, :], 1.0).then_inc(s_fv0, 1)
        dve.wait_ge(s_cond, 1)
        dve.wait_ge(s_par, 2)
        dve.wait_ge(s_ssq0, 1)
        for v in range(2):
            for k in range(KT):
                n = KT * v + k
                dve.wait_ge(s_mod_first[n // 2], 16)
                if k == 0:
                    dve.tensor_scalar(mod_first[:, n, :], mod_first[:, n, :], cond[:, 0:1], None, ALU.mult).then_inc(s_mod0, 1)
                else:
                    dve.wait_ge(s_mod0, n)
                    dve.scalar_tensor_tensor(out=mod_first[:, KT * v, :], in0=mod_first[:, n, :], scalar=cond[:, k:k + 1],
                                             in1=mod_first[:, KT * v, :], op0=ALU.mult, op1=ALU.add).then_inc(s_mod0, 1)
                if v == 0:
                    dve.wait_ge(s_sq, k + 1)
                    if k >= 1:
                        dve.wait_ge(s_ssq, k)
                    dve.tensor_tensor(ssq[:, :], ssq[:, :], ring[:, k % 2, :], ALU.add).then_inc(s_ssq, 1)

        def mod_chunk(i, k):
            dve.wait_ge(s_mod_raw[k % 2], 64 * i + 16 * (k // 2 + 1))
            if k == 0:
                dve.wait_ge(s_mod_sum, i + 2)
                dve.tensor_scalar(mod_acc[:, :], mod_raw[:, 0, :], cond[:, 0:1], None, ALU.mult).then_inc(s_mod_used, 1)
            else:
                dve.wait_ge(s_mod_used, 8 * i + (2 + k))
                dve.scalar_tensor_tensor(out=mod_acc[:, :], in0=mod_raw[:, k % 2, :], scalar=cond[:, k:k + 1],
                                         in1=mod_acc[:, :], op0=ALU.mult, op1=ALU.add).then_inc(s_mod_used, 1)

        def mod_finish(layer, v, group):
            dve.wait_ge(s_mod_sum, group + 1)
            dve.tensor_tensor(mod_t[:, layer, bass.ts(v, KT)], bank[7][:, 0:KT],
                              par_a[:, bass.ds(v * KT + (A_MODB + 6 * KT * layer), KT)], ALU.add).then_inc(s_mod, 1)

        def set_gain(n, layer, v, norm):
            dve.scalar_tensor_tensor(out=gain[:, n, :], in0=mod_t[:, layer, v * KT:(v + 1) * KT], scalar=1.0, in1=norm,
                                     op0=ALU.add, op1=ALU.mult).then_inc(s_gain, 1)

        mod_finish(0, 0, 0)
        mod_finish(0, 1, 1)
        dve.wait_ge(s_mod, 2)
        set_gain(0, 0, 1, par_a[:, A_NMIX:A_NMIX + KT])
        dve.wait_ge(s_x0, KT)
        dve.wait_ge(s_wf_split, 2)
        for r0 in (0, 32):
            dve.tensor_tensor(wf_lo[:, :, r0:r0 + NFOX], wf_raw[:, :, :], wf_hi[:, :, r0:r0 + NFOX].bitcast(F32),
                              ALU.subtract).then_inc(s_wf_lo, 1)

        def norm_u(n, k, gcol):
            dve.scalar_tensor_tensor(out=ring[:, k % 4, :], in0=x[:, k, :], scalar=gcol, in1=rstd[:, :],
                                     op0=ALU.mult, op1=ALU.mult).then_inc(s_u, 1)

        def norm_split(n, h0, layer, v):
            dve.wait_ge(s_gain, n + 1)
            dve.wait_ge(s_rstd, n + 1)
            for k in range(KT + 1):
                if k < KT:
                    if k >= 4:
                        dve.wait_ge(s_h_hi, h0 + k - 3)
                    norm_u(n, k, gain[:, n, k:k + 1])
                if k >= 1:
                    q = k - 1
                    dve.wait_ge(s_u, KT * n + q + 1)
                    dve.wait_ge(s_h_hi, h0 + q + 1)
                    dve.scalar_tensor_tensor(out=h_lo[:, q, :], in0=ring[:, q % 4, :], scalar=gate_col(layer, v, q),
                                             in1=h_hi[:, q, :].bitcast(F32), op0=ALU.add, op1=ALU.subtract).then_inc(s_h, 1)

        norm_split(0, H_MIX0, 0, 0)
        dve.wait_ge(s_f, 1)
        dve.tensor_scalar(ring[:, 0, :], bank[6][:, :], b_f[:, 0:1], None, ALU.add).then_inc(s_fv, 1)
        dve.wait_ge(s_fv, 1)
        dve.scalar_tensor_tensor(out=ring[:, 1, :], in0=ring[:, 0, :], scalar=-1.0, in1=ring[:, 0, :],
                                 op0=ALU.mult, op1=ALU.min).then_inc(s_fv, 1)
        dve.wait_ge(s_fa, 2)
        dve.scalar_tensor_tensor(out=ring[:, 1, :], in0=ring[:, 0, :], scalar=0.0, in1=ring[:, 3, :],
                                 op0=ALU.min, op1=ALU.subtract).then_inc(s_fv, 1)
        dve.wait_ge(s_fv, 3)
        dve.wait_ge(s_fv0, 1)
        dve.tensor_tensor_scan(ring[:, 2, :], decay_r[:, :], ring[:, 1, :], 0.0, ALU.mult, ALU.add).then_inc(s_fv, 1)
        dve.wait_ge(s_fv, 4)
        dve.tensor_copy(decay_l[32:32 + NFOX, :], ring[32:32 + NFOX, 2, :]).then_inc(s_fv, 1)
        dve.tensor_copy(decay_r[0:NFOX, :], ring[0:NFOX, 2, :]).then_inc(s_fv, 1)
        dve.wait_ge(s_fv, 6)

        def select_decay(h):
            dve.tensor_scalar(decay_h[:, h % 2, :], decay_l[:, :], fox_sel[:, h:h + 1], None, ALU.mult).then_inc(s_dh, 1)

        select_decay(0)
        select_decay(1)

        def evict_qkv(i, j):
            dve.wait_ge(s_mm, 4 * i + (SPLIT + QKV + j + 1))
            dve.tensor_scalar(qkv[:, i * 4 + j, :], bank[j][:, :], qkv_scale[:, bass.ds(i * 4 + j, 1)], None,
                              ALU.mult).then_inc(s_bank, 1)

        with dve.Fori(0, 4) as i:
            for j in range(4):
                mod_chunk(i, 2 * j)
                mod_chunk(i, 2 * j + 1)
                evict_qkv(i, j)
            mod_finish(0, i + 2, i + 2)
        with dve.Fori(4, 6) as i:
            for j in range(4):
                evict_qkv(i, j)

        for n in range(1, 8, 2):
            dve.wait_ge(s_v_t, n + 1)
            dve.tensor_copy(v_tok[:, n // 2, (n % 2) * S:(n % 2 + 1) * S], bank[4 + n % 2][:, :]).then_inc(s_v_tokv, 1)
        dve.wait_ge(s_mod, 6)
        set_gain(1, 0, 4, par_b[:, B_NFFN:B_NFFN + KT])
        for h in range(NH + 1):
            g = h - 1
            for qt in range(TT):
                if g >= 0:
                    dve.wait_ge(s_exp, TT * g + qt + 1)
                    dve.reciprocal(row_stat[:, g % 2, 2, qt:qt + 1], row_stat[:, g % 2, 1, qt:qt + 1]).then_inc(s_rinv, 1)
                if h < NH:
                    dve.wait_ge(s_score, TT * h + qt + 1)
                    dve.tensor_reduce(row_stat[:, h % 2, 0, qt:qt + 1], score_of(qt), AX_X, ALU.max,
                                      negate=True).then_inc(s_max, 1)
                if g >= 0:
                    dve.wait_ge(s_rinv, TT * g + qt + 1)
                    dve.tensor_scalar(prob[:, g % 2, COL[qt]:COL[qt + 1]], prob[:, g % 2, COL[qt]:COL[qt + 1]],
                                      row_stat[:, g % 2, 2, qt:qt + 1], None, ALU.mult).then_inc(s_norm, 1)
            if h < NFOX - 2:
                select_decay(h + 2)
            if g >= 0:
                dve.wait_ge(s_pt, g + 1)
                if g >= 2:
                    dve.wait_ge(s_pv, g - 1)
                dve.tensor_copy(prob_t[:, g % 2, S:S + 384], bank[5][:, 0:384]).then_inc(s_pt_v, 1)
                dve.tensor_copy(prob_t[:, g % 2, S + 384:1280], bank[6][:, 0:384]).then_inc(s_pt_v, 1)
                if g % 2:
                    pair = g // 2
                    dve.wait_ge(s_h_hi, H_ATT + pair + 1)
                    dve.tensor_tensor(h_lo[:, pair, :], bank[7][:, :], h_hi[:, pair, :].bitcast(F32),
                                      ALU.subtract).then_inc(s_h, 1)

        def residual(base, per, last, layer, v, n, t0, i, j):
            dve.wait_ge(s_mm, per * i + (SPLIT + base + last + 1))
            dve.scalar_tensor_tensor(out=x[:, i * 4 + j, :], in0=bank[j][:, :],
                                     scalar=mod_t[:, layer, bass.ds(i * 4 + (v * KT + j), 1)], in1=x[:, i * 4 + j, :],
                                     op0=ALU.mult, op1=ALU.add).then_inc(s_bank, 1)
            dve.wait_ge(s_sq, 4 * i + (KT * n + j + 1))
            dve.wait_ge(s_ssq, 4 * i + (KT * n + j))
            dve.tensor_tensor(ssq[:, :], ssq[:, :], ring[:, j % 2, :], ALU.add).then_inc(s_ssq, 1)

        def clear_ssq(n):
            dve.wait_ge(s_ssum, n)
            dve.memset(ssq[:, :], 0.0).then_inc(s_ssq0, 1)
            dve.wait_ge(s_ssq0, n + 1)

        def square(base, layer, t0, n):
            clear_ssq(n)
            with dve.Fori(0, 2) as i:
                for j in range(4):
                    residual(base, 4, j, layer, 2, n, t0, i, j)

        def swiglu(layer, base_in, base_out, t_in):
            def pairs(i, tiles):
                for j in range(tiles):
                    at = FT * layer + j + 1
                    if layer == 0:
                        per = KT // tiles
                        for k in range(per * j, per * j + per):
                            mod_chunk(i + 4, k)
                    dve.wait_ge(s_silu, 4 * i + at)
                    dve.wait_ge(s_mm, 8 * i + (SPLIT + base_in + 2 * j + 2))
                    dve.tensor_tensor(ring[:, 2 + j % 2, :], ring[:, j % 2, :], bank[(2 * j + 1) % 4][:, :],
                                      ALU.mult).then_inc(s_bank, 2)
                    dve.wait_ge(s_g_hi, 4 * i + at)
                    dve.tensor_tensor(g_lo[:, i * 4 + j, :], ring[:, 2 + j % 2, :], g_hi[:, i * 4 + j, :].bitcast(F32),
                                      ALU.subtract).then_inc(s_g, 1)
                if layer == 0:
                    mod_finish(1, i, i + 6)

            with dve.Fori(0, 5) as i:
                pairs(i, 4)
            pairs(5, 2)
            n = 2 + 2 * layer
            clear_ssq(n)
            with dve.Fori(0, 2) as i:
                for j in range(4):
                    residual(base_out, 12, 3 * j + 2, layer, 5, n, 0, i, j)

        square(AO, 0, T_AO, 1)
        norm_split(1, H_FFN0, 0, 3)
        swiglu(0, FI0, FO0, T_FI0)
        dve.wait_ge(s_mod, 12)
        set_gain(2, 1, 1, par_a[:, A_NMIX + KT:A_NMIX + 2 * KT])
        set_gain(3, 1, 4, par_b[:, B_NFFN + KT:B_NFFN + 2 * KT])
        if LAYERS == 2:
            dve.wait_ge(s_mm, SPLIT + RKV)
            dve.memset(h_f[:, :, 3:4], 0.0).then_inc(r_hf0, 1)
            dve.wait_ge(s_gain, 4)
            dve.wait_ge(s_rstd, 3)
            for k in range(KT):
                if k >= 4:
                    dve.wait_ge(r_hf, k - 3)
                norm_u(2, k, gain[:, 2, k:k + 1])
            m = 0
            for n, mu in enumerate((1, 4, 5, 0, 2, 3)):
                for k in range(KT + 1):
                    if k < KT:
                        dve.wait_ge(r_xx, k + 1)
                        if m < 4:
                            dve.wait_ge(r_hf, KT)
                        elif m < 28:
                            dve.wait_ge(r_lora, m - 3)
                        else:
                            dve.wait_ge(s_h_hi, H_R + m - 27)
                        dve.scalar_tensor_tensor(out=ring[:, m % 4, :], in0=xx[:, k, :],
                                                 scalar=par_b[:, B_MU + 8 * mu + k:B_MU + 8 * mu + k + 1],
                                                 in1=h_f[:, k, 4:4 + S], op0=ALU.mult, op1=ALU.add).then_inc(r_mix, 1)
                        m += 1
                    if n >= 3 and k >= 1:
                        q = 8 * (n - 3) + k
                        dve.wait_ge(r_mix, 24 + q)
                        dve.wait_ge(s_h_hi, H_R + q)
                        dve.tensor_tensor(h_lo[:, k - 1, :], ring[:, (k - 1) % 4, :], h_hi[:, k - 1, :].bitcast(F32),
                                          ALU.subtract).then_inc(s_h, 1)
                if n >= 3:
                    with dve.Fori(0, 2) as i:
                        for j in range(4):
                            dve.wait_ge(s_mm, 4 * i + (SPLIT + RKV + 8 * (n - 3) + j + 1))
                            dve.tensor_copy(rkv[:, i * 4 + (8 * (n - 3) + j), :], bank[j][:, :]).then_inc(s_bank, 1)
            dve.wait_ge(r_mask, MASKS)
            for seg in rwkv_order():
                kind, p = seg[0], seg[1]
                rp, kp, vp = rkv[:, p, :], rkv[:, KT + p, :], rkv[:, 2 * KT + p, :]
                par = lambda b: par_b[:, b + p:b + p + 1]
                if kind == "prep":
                    dve.tensor_scalar(bonus_w[:, :], heads2[:, :], par(B_RK), None, ALU.mult).then_inc(r_bwt, 1)
                    dve.wait_ge(r_sig, 2 * p + 1)
                    dve.tensor_tensor_scan(ring[:, 2, :], restart[:, :], ring[:, 0, :], 0.0, ALU.mult, ALU.add).then_inc(r_cum, 1)
                    dve.wait_ge(r_ss, p + 1)
                    dve.tensor_scalar(ring[:, 3, :], bank[2][:, :], 1e-24, None, ALU.max).then_inc(r_ssm, 1)
                    dve.wait_ge(r_rn, 2 * p + 2)
                    dve.scalar_tensor_tensor(out=tmp[:, 1, :], in0=kp, scalar=par(B_KK), in1=ring[:, 3, :],
                                             op0=ALU.mult, op1=ALU.mult).then_inc(r_kk, 1)
                    dve.wait_ge(r_b, p + 1)
                    dve.tensor_scalar(ring[:, 1, :], ring[:, 1, :], -1.0, par(B_KA), ALU.add, ALU.mult).then_inc(r_t, 1)
                    dve.wait_ge(r_t, p + 1)
                    dve.scalar_tensor_tensor(out=kp, in0=ring[:, 1, :], scalar=1.0, in1=kp, op0=ALU.add,
                                             op1=ALU.mult).then_inc(r_k1, 1)
                    dve.wait_ge(r_k1, p + 1)
                    dve.wait_ge(r_kk, p + 1)
                    dve.tensor_tensor(ring[:, 3, :], rp, kp, ALU.mult).then_inc(r_prd, 1)
                    dve.wait_ge(r_dec, 3 * p + 3)
                    dve.scalar_tensor_tensor(out=a_f[:, :], in0=tmp[:, 1, :], scalar=-1.0, in1=tmp[:, 0, :], op0=ALU.mult,
                                             op1=ALU.mult).then_inc(r_prep, 1)
                    dve.tensor_tensor(b_f32[:, :], tmp[:, 2, :], ring[:, 2, :], ALU.mult).then_inc(r_prep, 1)
                    dve.wait_ge(r_prd, p + 1)
                    dve.tensor_tensor(kp, kp, ring[:, 2, :], ALU.mult).then_inc(r_prep, 1)
                    dve.tensor_tensor(rp, rp, ring[:, 0, :], ALU.mult).then_inc(r_prep, 1)
                    dve.tensor_copy(chunk_decay[:, p % 2, :],
                                    ring[:, 0, :].rearrange("p (n c) -> p n c", c=CH)[:, :, CH - 1]).then_inc(r_prep, 1)
                elif kind == "tok":
                    dve.wait_ge(r_tm, p + 1)
                    for q in (1, 2):
                        dve.tensor_copy(bkv_tok[:, p % 2, q, :, :], bank[1 + q][:, :]).then_inc(r_tmv, 1)
                    dve.wait_ge(r_br, p + 1)
                    dve.tensor_tensor(vp, vp, bank[5][:, :], ALU.mult).then_inc(r_bon, 1)
                elif kind == "pairs":
                    q = seg[2]
                    dve.wait_ge(r_pm, 8 * p + q + 1)
                    for half, dst in enumerate((lt[:, q, :, :], at[:, p % 2, q, :, :])):
                        dve.tensor_tensor(dst, bank[q % 4][:, 256 * half:256 * half + 256].rearrange("p (a t) -> p a t", a=2),
                                          before[:, half, :].unsqueeze(1).broadcast_to((P, 2, P)), ALU.mult).then_inc(r_pe, 1)
                elif kind == "join" and seg[2] == 0:
                    dve.wait_ge(r_m, 6 * p + 1)
                    dve.tensor_tensor(inv_t[:, :, :], join_t[:, :, :], ident[:, :].unsqueeze(1).broadcast_to((P, 8, P)),
                                      ALU.add).then_inc(r_dt0, 1)
                elif kind == "join":
                    l = seg[2]
                    for g in range(2):
                        at_ = 10 * p + 2 * (l - 1) + g + 1
                        dve.wait_ge(r_dm, at_)
                        half = slice(4 * g, 4 * g + 4)
                        dve.tensor_tensor(inv_t[:, half, :], inv_t[:, half, :],
                                          bank[4 + g][:, :].rearrange("p (q t) -> p q t", q=4), ALU.add).then_inc(r_d, 1)
                        if l < 5:
                            dve.tensor_tensor(inv[:, half, :], inv[:, half, :],
                                              bank[2 + g][:, :].rearrange("p (q t) -> p q t", q=4), ALU.add).then_inc(r_d, 1)
                elif kind == "step":
                    n = seg[2]
                    c, rows = n // 2, slice(CH * (n % 2), CH * (n % 2) + CH)
                    if n == 0:
                        dve.memset(state[:, :], 0.0).then_inc(r_s0, 1)
                    dve.wait_ge(r_um, NC * p + n + 1)
                    dve.tensor_tensor(u_tok[rows, p % 2, c, :], bank[6][rows, 0:P], u_tok[rows, p % 2, c, :],
                                      ALU.add).then_inc(r_u, 1)
                elif kind == "out":
                    n = seg[2]
                    dve.wait_ge(r_sm, NC * p + n + 1)
                    dve.tensor_tensor(state_t[:, :], bank[7][:, 0:P], state[:, :], ALU.add).then_inc(r_s1, 1)
                    dve.wait_ge(r_s1, NC * p + n + 1)
                    dve.wait_ge(r_ys, NC * p + n + 1)
                    dve.scalar_tensor_tensor(out=state[:, :], in0=state_t[:, :], scalar=chunk_decay[:, p % 2, n:n + 1],
                                             in1=heads2[:, :], op0=ALU.mult, op1=ALU.mult).then_inc(r_s2, 1)
            for p in range(KT + 1):
                if p < KT:
                    yp = rkv[:, KT + p, :]
                    dve.wait_ge(r_mean, p + 1)
                    dve.scalar_tensor_tensor(out=yp, in0=bank[p % 2][:, :], scalar=-1.0 / HD, in1=yp, op0=ALU.mult,
                                             op1=ALU.add).then_inc(r_yc, 1)
                if p >= 1:
                    q = p - 1
                    yp = rkv[:, KT + q, :]
                    dve.wait_ge(r_grs, 2 * q + 2)
                    dve.scalar_tensor_tensor(out=yp, in0=yp, scalar=par_b[:, B_LNW + q:B_LNW + q + 1], in1=ring[:, q % 2, :],
                                             op0=ALU.mult, op1=ALU.mult).then_inc(r_yn, 1)
                    dve.wait_ge(r_yn, q + 1)
                    dve.scalar_tensor_tensor(out=yp, in0=yp, scalar=par_b[:, B_LNB + q:B_LNB + q + 1],
                                             in1=rkv[:, 2 * KT + q, :], op0=ALU.add, op1=ALU.add).then_inc(r_z1, 1)
                    dve.wait_ge(r_z1, q + 1)
                    dve.wait_ge(r_gmm, q + 1)
                    dve.tensor_tensor(ring[:, 2 + q % 2, :], yp, bank[4 + q % 2][:, :], ALU.mult).then_inc(r_z2, 1)
                    dve.wait_ge(s_h_hi, H_WO + q + 1)
                    dve.tensor_tensor(h_lo[:, q, :], ring[:, 2 + q % 2, :], h_hi[:, q, :].bitcast(F32),
                                      ALU.subtract).then_inc(s_h, 1)
            square(WO, 1, T_WO, 3)
            norm_split(3, H_FFN1, 1, 3)
            swiglu(1, FI1, FO1, T_FI1)
        dve.wait_ge(s_rstd, LAST + 1)
        for k in range(KT):
            if k >= 4:
                dve.wait_ge(s_y_t, k - 3)
            norm_u(LAST, k, par_b[:, B_NFIN + k:B_NFIN + k + 1])

    @block.tensor
    def _(pe):
        def multiply(base, per, i, j, psum, rhs, tiles=KT, k0=0, first=True, last=True, ready=None):
            pe.wait_ge(s_lo, per * i + (base + j + 1 + RAW))
            for t in range(tiles):
                if ready is not None:
                    pe.wait_ge(ready[0], ready[1] + k0 + t + 1)
                hi, lo = rhs[0](k0 + t), rhs[1](k0 + t)
                for q, (w, r) in enumerate(((w_hi, hi), (w_hi, lo), (w_lo, hi))):
                    mm = pe.matmul(psum[:, :], w[:, j % SPLIT, t, :], r, start=first and t == 0 and q == 0,
                                   stop=last and t == tiles - 1 and q == 2)
            mm.then_inc(s_mm, 1)

        def mod_sum(acc, group):
            pe.wait_ge(s_mod, group)
            for c in range(KT):
                mm = pe.matmul(bank[7][:, c:c + 1], acc[:, c * P:(c + 1) * P], ones[:, 0:1], start=True, stop=True)
            mm.then_inc(s_mod_sum, 1)

        def norm_sum(n):
            pe.wait_ge(s_ssq, KT * (n + 1))
            pe.matmul(bank[7][:, :], ones[:, :], ssq[:, :], start=True, stop=True).then_inc(s_ssum, 1)

        pe.wait_ge(s_const, CONSTS)
        pe.wait_ge(s_rows, 16 * 13)
        pe.transpose(bank[4][:, 0:A_ROWS], rows_a[:, :], ident[0:A_ROWS, 0:A_ROWS])
        pe.transpose(bank[5][:, 0:P], rows_b[:, :], ident[:, :]).then_inc(s_par_t, 1)
        pe.wait_ge(s_x_tok, 16)
        for k in range(KT):
            if k >= 4:
                pe.wait_ge(s_x0, k - 3)
                pe.wait_ge(s_sq, k - 3)
            for t in range(TT):
                mm = pe.transpose(bank[k % 4][:, t * P:(t + 1) * P], x_tok[:, t, k * P:(k + 1) * P], ident[:, :])
            mm.then_inc(s_xt, 1)
        pe.wait_ge(s_mod0, KT)
        for c in range(KT):
            mm = pe.matmul(bank[7][:, c:c + 1], mod_first[:, 0, c * P:(c + 1) * P], ones[:, 0:1], start=True, stop=True)
        mm.then_inc(s_mod_sum, 1)
        pe.wait_ge(s_mod0, 2 * KT)
        mod_sum(mod_first[:, KT, :], 1)
        pe.wait_ge(s_mod, 2)
        norm_sum(0)
        pe.wait_ge(s_wf_lo, 2)
        for k in range(KT):
            pe.wait_ge(s_h, H_MIX0 + k + 1)
            for q, (w, r) in enumerate(((wf_hi, h_hi), (wf_hi, h_lo), (wf_lo, h_hi))):
                mm = pe.matmul(bank[6][:, :], w[:, k, :], r[:, k, :], start=k == 0 and q == 0, stop=k == KT - 1 and q == 2)
        mm.then_inc(s_f, 1)

        def four(base, t0, i, ready=None):
            for j in range(4):
                pe.wait_ge(s_bank, 4 * i + (t0 + j + 1))
                multiply(base, 4, i, j, bank[j], h_of, ready=ready if j == 0 else None)

        with pe.Fori(0, 4) as i:
            four(QKV, T_QKV, i)
            pe.wait_ge(s_mod_used, 8 * i + 10)
            mod_sum(mod_acc, i + 2)
        with pe.Fori(4, 6) as i:
            four(QKV, T_QKV, i)

        pe.wait_ge(s_bank, NB + T_QKV + 24)
        for n in range(8):
            if n >= 2:
                pe.wait_ge(s_v_tok if n % 2 == 0 else s_v_tokv, n // 2)
            for f in range(4):
                mm = pe.transpose(bank[4 + n % 2][:, f * P:(f + 1) * P], qkv[:, 8 + 12 * (n % 2) + f, (n // 2) * P:(n // 2 + 1) * P],
                                  ident[:, :])
            mm.then_inc(s_v_t, 1)
        pe.wait_ge(s_v_tok, 4)
        pe.wait_ge(s_v_tokv, 4)
        pe.wait_ge(s_mod, 6)
        pe.wait_ge(s_fv, 6)
        for h in range(NH + 1):
            if h < NH:
                pair, rows = (h % NFOX) // 2, slice(HD * (h % 2), HD * (h % 2) + HD)
                q0 = pair + 12 * (h // NFOX)
                for qt in range(TT):
                    if h >= 1:
                        pe.wait_ge(s_exp, TT * (h - 1) + qt + 1)
                    cols = slice(qt * P, (qt + 1) * P)
                    psum = score_of(qt)
                    pe.matmul(psum, qkv[rows, q0, cols], qkv[rows, q0 + 4, 0:(qt + 1) * P], start=True, stop=False)
                    if h < NFOX:
                        pe.wait_ge(s_dh, h + 1)
                        pe.matmul(psum, decay_h[:, h % 2, cols], decay_r[:, 0:(qt + 1) * P], start=False, stop=False)
                    pe.matmul(psum[:, qt * P:(qt + 1) * P], ident_b[:, :], causal[:, :], start=False,
                              stop=True).then_inc(s_score, 1)
            if h >= 1:
                g = h - 1
                if g >= 1:
                    pe.wait_ge(s_pt_a, g)
                    pe.wait_ge(s_pt_v, 2 * g)
                for qt in range(TT):
                    pe.wait_ge(s_norm, TT * g + qt + 1)
                    for kt in range(qt + 1):
                        dst = bank[PT_BANK[kt]][:, PT_OFF[kt] + (qt - kt) * P:PT_OFF[kt] + (qt - kt + 1) * P]
                        mm = pe.transpose(dst, prob[:, g % 2, COL[qt] + kt * P:COL[qt] + (kt + 1) * P], ident[:, :])
                mm.then_inc(s_pt, 1)
                pair = g // 2
                if g % 2 == 0 and pair >= 1:
                    pe.wait_ge(s_h, H_ATT + pair)
                pe.wait_ge(s_pt_a, g + 1)
                pe.wait_ge(s_pt_v, 2 * g + 2)
                rows = slice(HD * (g % 2), HD * (g % 2) + HD)
                for kt in range(TT):
                    o = (0, S, S + 384, S + 640)[kt]
                    mm = pe.matmul(bank[7][rows, kt * P:S], v_tok[:, kt, g * HD:(g + 1) * HD],
                                   prob_t[:, g % 2, o:o + S - kt * P], start=kt == 0, stop=kt == TT - 1)
                mm.then_inc(s_pv, 1)

        def square(base, t0, h0):
            with pe.Fori(0, 2) as i:
                four(base, t0, i, ready=(s_h, h0))

        def swiglu(layer, base_in, base_out, t_in, t_out, h0):
            def pairs(i, tiles):
                for j in range(2 * tiles):
                    pe.wait_ge(s_bank, 8 * i + (t_in + j + 1))
                    multiply(base_in, 8, i, j, bank[j % 4], h_of, ready=(s_h, h0) if j == 0 else None)
                if layer == 0:
                    pe.wait_ge(s_mod_used, 8 * i + 42)
                    mod_sum(mod_acc, i + 6)

            with pe.Fori(0, 5) as i:
                pairs(i, 4)
            pairs(5, 2)
            with pe.Fori(0, 2) as i:
                for j in range(4):
                    pe.wait_ge(s_bank, 4 * i + (t_out + j + 1))
                    for c, (k0, kn) in enumerate(OUT_PARTS):
                        multiply(base_out, 12, i, 3 * j + c, bank[j], g_of, kn, k0, c == 0, c == 2,
                                 ready=(s_g, FT * layer) if j == 0 else None)

        square(AO, T_AO, H_ATT)
        norm_sum(1)
        swiglu(0, FI0, FO0, T_FI0, T_FO0, H_FFN0)
        norm_sum(2)
        if LAYERS == 2:
            pe.wait_ge(s_bank, NB + T_RKV)
            pe.wait_ge(r_lora_w, 80)
            for m in range(24):
                k, x_mix = m % KT, ring[:, m % 4, :]
                pe.wait_ge(r_mix, m + 1)
                if m < 8:
                    mm = pe.matmul(bank[0][0:HD, :], w1[:, k, :], x_mix, start=k == 0, stop=k == KT - 1)
                elif m < 16:
                    mm = pe.matmul(bank[1][HD:P, :], a1[:, k, :], x_mix, start=k == 0, stop=k == KT - 1)
                else:
                    pe.matmul(bank[2][:, :], g1[:, k, 0:P], x_mix, start=k == 0, stop=k == KT - 1)
                    mm = pe.matmul(bank[3][0:GL - P, :], g1[:, k, P:GL], x_mix, start=k == 0, stop=k == KT - 1)
                mm.then_inc(r_lora, 1)
            pe.wait_ge(r_mid, 4)
            for n in range(3):
                with pe.Fori(0, 2) as i:
                    four(RKV + 8 * n, T_RKV + 8 * n, i, ready=(s_h, H_R + 8 * n))
            pe.wait_ge(s_bank, NB + T_WO)
            pe.wait_ge(r_mask, MASKS)
            for seg in rwkv_order():
                kind, p = seg[0], seg[1]
                rp, kp, vp = rkv[:, p, :], rkv[:, KT + p, :], rkv[:, 2 * KT + p, :]
                if kind == "prep":
                    if p:
                        pe.wait_ge(r_w, p)
                        pe.wait_ge(r_u0, p)
                        pe.wait_ge(r_d, 18 * p)
                    cols = slice(p * P, (p + 1) * P)
                    pe.matmul(bank[0][:, :], wa2[0:HD, cols], wa_mid[0:HD, :], start=True, stop=True).then_inc(r_lora_mm, 1)
                    pe.matmul(bank[1][:, :], wa2[HD:P, cols], wa_mid[HD:P, :], start=True, stop=True).then_inc(r_lora_mm, 1)
                    pe.wait_ge(r_sqk, p + 1)
                    pe.matmul(bank[2][:, :], heads2[:, :], ring[:, 3, :], start=True, stop=True).then_inc(r_ss, 1)
                elif kind == "tok":
                    pe.wait_ge(r_prd, p + 1)
                    pe.wait_ge(r_bwt, p + 1)
                    pe.matmul(bank[5][:, :], bonus_w[:, :], ring[:, 3, :], start=True, stop=True).then_inc(r_br, 1)
                    pe.wait_ge(r_prep, 5 * p + 4)
                    for q, src in enumerate((a_f[:, :], b_f32[:, :], kp, vp)):
                        for t in range(TT):
                            mm = pe.transpose(bank[q][:, t * P:(t + 1) * P], src[:, t * P:(t + 1) * P], ident[:, :])
                    mm.then_inc(r_tm, 1)
                elif kind == "pairs":
                    q = seg[2]
                    c, rows = q // 2, slice(HD * (q % 2), HD * (q % 2) + HD)
                    if q == 0:
                        pe.wait_ge(r_tma, 2 * p + 2)
                        pe.wait_ge(r_tmv, 2 * p + 2)
                    if q >= 4:
                        pe.wait_ge(r_pe, 16 * p + 2 * (q - 4) + 2)
                    t = slice(c * P, (c + 1) * P)
                    for o, (left, right) in enumerate(((b_f32, a_f[rows, t]), (kp, a_f[rows, t]), (b_f32, rp[rows, t]),
                                                       (kp, rp[rows, t]))):
                        mm = pe.matmul(bank[q % 4][:, o * P:(o + 1) * P], left[rows, t], right, start=True, stop=True)
                    mm.then_inc(r_pm, 1)
                elif kind == "intra":
                    pe.wait_ge(r_pe, 16 * p + 16)
                    for q in range(8):
                        c, cols = q // 2, slice(HD * (q % 2), HD * (q % 2) + HD)
                        mm = pe.matmul(bank[4][:, q * HD:(q + 1) * HD], lt[:, q, 1, :], bkv_tok[:, p % 2, 2, c, cols],
                                       start=True, stop=True)
                    mm.then_inc(r_xm, 1)
                elif kind == "join" and seg[2] == 0:
                    pe.wait_ge(r_dt0, p + 1)
                    for q in range(8):
                        mm = pe.transpose(bank[q // 4][:, q % 4 * P:(q % 4 + 1) * P], inv_t[:, q, :], ident[:, :])
                    mm.then_inc(r_d0t, 1)
                elif kind == "join":
                    l = seg[2]
                    pe.wait_ge(r_m, 6 * p + l + 1)
                    if l == 1:
                        pe.wait_ge(r_d0, 2 * p + 2)
                    else:
                        pe.wait_ge(r_d, 18 * p + 4 * (l - 1))
                    for q in range(8):
                        mm = pe.matmul(bank[q // 4][:, q % 4 * P:(q % 4 + 1) * P], join_t[:, q, :], inv[:, q, :], start=True, stop=True)
                        if q % 4 == 3:
                            mm.then_inc(r_zm, 1)
                elif kind == "grow":
                    l = seg[2]
                    for g in range(2):
                        pe.wait_ge(r_z, 10 * p + 2 * (l - 1) + g + 1)
                        if l == 1:
                            pe.wait_ge(r_xv, p + 1)
                        for q in range(4 * g, 4 * g + 4):
                            t = slice(q % 4 * P, (q % 4 + 1) * P)
                            if l < 5:
                                pe.matmul(bank[2 + g][:, t], inv_t[:, q, :], prod[:, q, :], start=True, stop=True)
                            mm = pe.matmul(bank[4 + g][:, t], prod[:, q, :], inv_t[:, q, :], start=True, stop=True)
                        mm.then_inc(r_dm, 1)
                elif kind == "wu":
                    pe.wait_ge(r_d, 18 * p + 18)
                    for q in range(8):
                        c, rows = q // 2, slice(HD * (q % 2), HD * (q % 2) + HD)
                        mm = pe.matmul(bank[0][rows, c * P:(c + 1) * P], a_tok[:, c, rows], inv_t[:, q, :], start=True, stop=True)
                    mm.then_inc(r_wm, 1)
                    for q in range(8):
                        c, cols = q // 2, slice(HD * (q % 2), HD * (q % 2) + HD)
                        mm = pe.matmul(bank[1][:, q * HD:(q + 1) * HD], inv_t[:, q, :], u_tok[:, p % 2, c, cols], start=True, stop=True)
                    mm.then_inc(r_um0, 1)
                elif kind == "step":
                    n = seg[2]
                    at_, c, lo = NC * p + n, n // 2, CH * (n % 2)
                    rows = slice(lo, lo + CH)
                    if n == 0:
                        pe.wait_ge(r_s0, p + 1)
                        pe.wait_ge(r_w, p + 1)
                        pe.wait_ge(r_u0, p + 1)
                    if at_:
                        pe.wait_ge(r_s2, at_)
                        pe.wait_ge(r_y, at_)
                    pe.matmul(bank[6][rows, 0:P], w_f[:, p % 2, c * P + lo:c * P + lo + CH], state[:, :], start=True,
                              stop=True).then_inc(r_um, 1)
                    pe.matmul(bank[7][:, 0:P], bkv_tok[rows, p % 2, 1, c, :], bkv_tok[rows, p % 2, 2, c, :], start=True, stop=False)
                elif kind == "out":
                    n = seg[2]
                    at_, c, lo = NC * p + n, n // 2, CH * (n % 2)
                    rows, toks = slice(lo, lo + CH), slice(n * CH, (n + 1) * CH)
                    pe.wait_ge(r_u, at_ + 1)
                    pe.matmul(bank[7][:, 0:P], bkv_tok[rows, p % 2, 0, c, :], u_tok[rows, p % 2, c, :], start=False,
                              stop=True).then_inc(r_sm, 1)
                    y = bank[6][:, 256:256 + CH]
                    pe.matmul(y, state[:, :], rp[:, toks], start=True, stop=False).then_inc(r_ys, 1)
                    for hd in range(2):
                        f = slice(HD * hd, HD * hd + HD)
                        q = 2 * c + hd
                        pe.matmul(y[f, :], u_tok[rows, p % 2, c, f], at[rows, p % 2, q, 0, rows], start=False, stop=False)
                        mm = pe.matmul(y[f, :], bkv_tok[rows, p % 2, 2, c, f], at[rows, p % 2, q, 1, rows], start=False, stop=True)
                    mm.then_inc(r_ym, 1)
            pe.wait_ge(r_g2, 32)
            pe.wait_ge(r_y, NC * KT)
            for p in range(KT + 1):
                if p < KT:
                    if p >= 2:
                        pe.wait_ge(r_z2, p - 1)
                    pe.matmul(bank[p % 2][:, :], heads2[:, :], rkv[:, KT + p, :], start=True, stop=True).then_inc(r_mean, 1)
                    pe.matmul(bank[4 + p % 2][:, :], g2[:, 0, p * P:(p + 1) * P], g_mid[:, 0, :], start=True, stop=False)
                    pe.matmul(bank[4 + p % 2][:, :], g2[0:GL - P, 1, p * P:(p + 1) * P], g_mid[0:GL - P, 1, :], start=False,
                              stop=True).then_inc(r_gmm, 1)
                    pe.wait_ge(r_ysq, p + 1)
                    pe.matmul(bank[2 + p % 2][:, :], heads2[:, :], ring[:, p % 2, :], start=True, stop=True).then_inc(r_var, 1)
            square(WO, T_WO, H_WO)
            norm_sum(3)
            swiglu(1, FI1, FO1, T_FI1, T_FO1, H_FFN1)
            norm_sum(4)
        for k in range(KT):
            pe.wait_ge(s_u, KT * LAST + k + 1)
            if k >= 4:
                pe.wait_ge(s_y, k - 3)
            for t in range(TT):
                mm = pe.transpose(bank[k % 4][:, t * P:(t + 1) * P], ring[:, k % 4, t * P:(t + 1) * P], ident[:, :])
            mm.then_inc(s_y_t, 1)


_INS = ["x", "c", "attn_w_in", "attn_b_f", "attn_w_out", "rwkv_mu", "rwkv_w_r", "rwkv_w_k", "rwkv_w_v", "rwkv_w_o",
        "rwkv_w0", "rwkv_w1", "rwkv_w2", "rwkv_a0", "rwkv_a1", "rwkv_a2", "rwkv_g1", "rwkv_g2", "rwkv_k_k", "rwkv_k_a",
        "rwkv_r_k", "rwkv_ln_w", "rwkv_ln_b", "mod_w", "mod_b", "norm_mix", "norm_ffn", "ffn_w_in", "ffn_w_out",
        "norm_final"]


def kernel(**inputs):
    import numpy as np
    import concourse.bacc as bacc
    from concourse.bass_utils import run_bass_kernel_spmd

    nc = bacc.Bacc("TRN2", target_bir_lowering=False, num_devices=1)
    arrays, aps = {}, {}
    for name in _INS:
        arr = np.ascontiguousarray(inputs[name])
        arrays[f"in_{name}"] = arr
        aps[name] = nc.dram_tensor(f"in_{name}", arr.shape, mybir.dt.from_np(arr.dtype), kind="ExternalInput").ap()
    out = nc.dram_tensor("out", (1, S, D), F32, kind="ExternalOutput").ap()
    build(nc, aps, out)
    return run_bass_kernel_spmd(nc, [arrays], core_ids=[0]).results[0]["out"]
```

```python
from contextlib import ExitStack

import concourse.bass as bass
from concourse import mybir

F32 = mybir.dt.float32
F32R = mybir.dt.float32r
BF16 = mybir.dt.bfloat16
ALU = mybir.AluOpType
ACT = mybir.ActivationFunctionType
AX_X = mybir.AxisListType.X

P = 128
S = 512
D = 1024
KT = D // P
TT = S // P
HD = 64
NH = 16
NFOX = 8
FF = 2816
FT = FF // P
EPS = 1e-6
GN_EPS = HD * 1e-5
NEG = -1e30
DECAY = -0.6065306597126334
CH = 64
NC = S // CH
GL = 160
LOG_NORM = 6.931471805599453
RAW = 4
SPLIT = 2
NB = 4
OUT_PARTS = ((0, 8), (8, 7), (15, 7))

QKV, AO, FI0, FO0, RKV, WO, FI1, FO1, CHUNKS = 0, 24, 32, 76, 100, 124, 132, 176, 200
T_QKV, T_AO, T_FI0, T_FO0, T_RKV, T_WO, T_FI1, T_FO1 = 0, 24, 32, 76, 84, 108, 116, 160

H_MIX0, H_ATT, H_FFN0, H_R, H_K, H_V, H_WO, H_FFN1 = 0, 8, 16, 24, 32, 40, 48, 56
LAYERS = 2
LAST = 2 * LAYERS
CONSTS = 21
MASKS = 37
COL = (0, 128, 384, 768, 1280)
PT_BANK = (4, 5, 6, 6)
PT_OFF = (0, 0, 0, 256)

A_C, A_MODB, A_NMIX = 0, 8, 104
A_ROWS = 120
B_NFFN, B_NFIN, B_MU, B_W0, B_A0, B_KK, B_KA, B_RK, B_LNW, B_LNB = 0, 16, 24, 72, 80, 88, 96, 104, 112, 120

PAIR_BANK = (4, 5, 1, 2)
PREP = ("prep_lora", "prep_sig", "prep_cum", "prep_prev", "prep_ln", "prep_norm", "prep_decay", "prep_key", "prep_a",
        "prep_b", "prep_r", "prep_k", "prep_bonus")


def rwkv_order():
    for part in PREP:
        yield (part, 0)
    for p in range(KT + 1):
        steps = iter([(kind, p - 1, n) for n in range(NC) for kind in ("step", "out")] if p else [])
        prep = iter([(part, p + 1) for part in PREP] if p + 1 < KT else [])
        own = []
        if p < KT:
            own = [(("tok_bk", p), 0, 0), (("w_back", p - 1), 0, 0), (("tok_av", p), 0, 0)]
            own += [(("pairs", p, g), int(g >= 2), 0) for g in range(4)]
            own += [(("intra", p, 0), 1, 0), (("intra", p, 1), 1, 1), (("first", p), 1, 1), (("join", p, 1), 1, 1),
                    (("grow", p, 1), 1, 2)]
            for l in range(2, 6):
                own += [(("join", p, l), 0, 0), (("turn", p, l - 1), 1, 1)]
                own += [(("grow" if l < 5 else "grow_t", p, l), 1 if l < 5 else 2, 1)]
        for seg, count, more in own:
            if seg[1] >= 0:
                yield seg
            for _ in range(count):
                yield from (s for s in [next(steps, None)] if s)
            for _ in range(more):
                yield from (s for s in [next(prep, None)] if s)
        yield from prep
        if p == KT:
            yield ("w_back", p - 1)
        yield from steps
        if p < KT:
            yield ("wu", p)


def build(nc, a, out):
    with ExitStack() as ctx:
        program(nc, a, out, ctx)


def program(nc, a, out, ctx):
    def sb(name, shape, dt=F32, scope=ctx):
        return scope.enter_context(nc.sbuf_tensor(name, shape, dt))

    def sem(name):
        return ctx.enter_context(nc.semaphore(name))

    bank = [ctx.enter_context(nc.psum_tensor(f"bank{i}", [P, S], F32)) for i in range(8)]

    x = sb("x", [P, KT, S])
    raw = sb("raw", [P, RAW, KT, P])
    w_hi = sb("w_hi", [P, SPLIT, KT, P], F32R)
    w_lo = sb("w_lo", [P, SPLIT, KT, P], F32R)
    ident = sb("ident", [P, P])
    ident_b = sb("ident_b", [P, P], BF16)
    causal = sb("causal", [P, P], BF16)
    ones = sb("ones", [P, P])
    cst = sb("cst", [P, 8])
    par_a = sb("par_a", [P, A_ROWS])
    par_b = sb("par_b", [P, P])
    rows_a = sb("rows_a", [A_ROWS, P])
    rows_b = sb("rows_b", [P, P])
    cond = sb("cond", [P, KT])
    mod_t = sb("mod_t", [P, 2, 6 * KT])
    gain = sb("gain", [P, 4, KT])
    fox_sel = sb("fox_sel", [P, NFOX])
    qkv_scale = sb("qkv_scale", [P, 24])
    ring = sb("ring", [P, 4, S])
    ssq = sb("ssq", [P, S])
    rstd = sb("rstd", [P, S])
    h_scope = ExitStack()
    h_hi = sb("h_hi", [P, KT, S], F32R, h_scope)
    h_lo = sb("h_lo", [P, KT, S], F32R, h_scope)
    mod_scope = ExitStack()
    mod_raw = sb("mod_raw", [P, 2, D], F32, mod_scope)
    mod_acc = sb("mod_acc", [P, D], F32, mod_scope)
    with ExitStack() as s0:
        x_tok = sb("x_tok", [P, TT, D], F32, s0)
        mod_first = sb("mod_first", [P, 2 * KT, D], F32, s0)
    with ExitStack() as s1:
        qkv = sb("qkv", [P, 24, S], F32, s1)
        prob = sb("prob", [P, 2, 1280], F32, s1)
        prob_t = sb("prob_t", [P, 2, 1280], F32, s1)
        decay_h = sb("decay_h", [P, 2, S], F32, s1)
        row_stat = sb("row_stat", [P, 2, 3, TT], F32, s1)
        with ExitStack() as s2:
            v_tok = sb("v_tok", [P, TT, D], F32, s2)
        with ExitStack() as s2:
            sb("start_up_tiles", [P, 2048], F32, s2)
            wf_raw = sb("wf_raw", [P, KT, NFOX], F32, s2)
            wf_hi = sb("wf_hi", [P, KT, P], F32R, s2)
            wf_lo = sb("wf_lo", [P, KT, P], F32R, s2)
            decay_l = sb("decay_l", [P, S], F32, s2)
            decay_r = sb("decay_r", [P, S], F32, s2)
            b_f = sb("b_f", [P, 1], F32, s2)
    with ExitStack() as s1:
        y_tok = sb("y_tok", [P, TT, D], F32, s1)
    with ExitStack() as s1:
        g_hi = sb("g_hi", [P, FT, S], F32R, s1)
        g_lo = sb("g_lo", [P, FT, S], F32R, s1)
    mod_scope.close()
    rw_scope = ExitStack()
    rkv = sb("rkv", [P, 3 * KT, S], F32, rw_scope)
    wa_mid = sb("wa_mid", [P, S], F32, rw_scope)
    g_mid = sb("g_mid", [P, 2, S], F32, rw_scope)
    wa2 = sb("wa2", [P, D], F32, rw_scope)
    levels = sb("levels", [P, 6, P], F32, rw_scope)
    before = sb("before", [P, 2, CH], F32, rw_scope)
    heads2 = sb("heads2", [P, P], F32, rw_scope)
    restart = sb("restart", [P, S], F32, rw_scope)
    with ExitStack() as s1:
        h_f = sb("h_f", [P, KT, S + 4], F32, s1)
        xx = sb("xx", [P, KT, S], F32, s1)
        w1 = sb("w1", [P, KT, HD], F32, s1)
        a1 = sb("a1", [P, KT, HD], F32, s1)
        g1 = sb("g1", [P, KT, GL], F32, s1)
    rkv_flat = rkv[:, :, :].rearrange("p k s -> p (k s)")
    with ExitStack() as s1:
        ax_tok = sb("ax_tok", [P, TT, 2, P], F32, s1)
        w_tok = sb("w_tok", [P, TT, P], F32, s1)
        bk_f = sb("bk_f", [P, TT, 4, CH], F32, s1)
        ar_f = sb("ar_f", [P, 2, S], F32, s1)
        bk_tok = sb("bk_tok", [P, 2, NC, P], F32, s1)
        uv = sb("uv", [P, 2, 2, TT, P], F32, s1)
        u0 = sb("u0", [P, TT, P], F32, s1)
        w_f = sb("w_f", [P, S], F32, s1)
        inv = sb("inv", [P, 8, P], F32, s1)
        key = sb("key", [P, S], F32, s1)
        state = sb("state", [P, 2, P], F32, s1)
        state_t = sb("state_t", [P, P], F32, s1)
        bonus_w = sb("bonus_w", [P, P], F32, s1)
        bonus = sb("bonus", [P, S], F32, s1)
        chunk_decay = sb("chunk_decay", [P, 3, NC], F32, s1)
    with ExitStack() as s1:
        g2 = sb("g2", [P, 2, D], F32, s1)
    rw_scope.close()
    h_scope.close()
    with ExitStack() as s1:
        ar = sb("ar", [P, 2, 2, NC, 2, CH], F32, s1)
        inv_t = sb("inv_t", [P, 8, P], F32, s1)
        prod = sb("prod", [P, 8, P], F32, s1)
        join_t = sb("join_t", [P, 2, 8, P], F32, s1)

    s_rows = sem("s_rows")
    s_x_tok = sem("s_x_tok")
    s_mod_first = [sem(f"s_mod_first{i}") for i in range(8)]
    s_wf = sem("s_wf")
    s_raw = [sem(f"s_raw{i}") for i in range(RAW)]
    s_mod_raw = [sem(f"s_mod_raw{i}") for i in range(2)]
    s_hi = sem("s_hi")
    s_lo = sem("s_lo")
    s_mm = sem("s_mm")
    s_bank = sem("s_bank")
    s_const = sem("s_const")
    s_par_t = sem("s_par_t")
    s_par = sem("s_par")
    s_cond = sem("s_cond")
    s_xt = sem("s_xt")
    s_x0 = sem("s_x0")
    s_mod_used = sem("s_mod_used")
    s_mod0 = sem("s_mod0")
    s_mod_sum = sem("s_mod_sum")
    s_mod = sem("s_mod")
    s_gain = sem("s_gain")
    s_sq = sem("s_sq")
    s_ssq = sem("s_ssq")
    s_ssq0 = sem("s_ssq0")
    s_ssum = sem("s_ssum")
    s_ln = sem("s_ln")
    s_rstd = sem("s_rstd")
    s_u = sem("s_u")
    s_h_hi = sem("s_h_hi")
    s_h = sem("s_h")
    s_v_t = sem("s_v_t")
    s_v_tok = sem("s_v_tok")
    s_v_tokv = sem("s_v_tokv")
    s_wf_split = sem("s_wf_split")
    s_f = sem("s_f")
    s_fa = sem("s_fa")
    s_fv = sem("s_fv")
    s_fv0 = sem("s_fv0")
    s_wf_lo = sem("s_wf_lo")
    s_dh = sem("s_dh")
    s_score = sem("s_score")
    s_max = sem("s_max")
    s_exp = sem("s_exp")
    s_rinv = sem("s_rinv")
    s_norm = sem("s_norm")
    s_pt = sem("s_pt")
    s_pt_a = sem("s_pt_a")
    s_pt_v = sem("s_pt_v")
    s_pv = sem("s_pv")
    s_silu = sem("s_silu")
    s_g_hi = sem("s_g_hi")
    s_g = sem("s_g")
    s_y_t = sem("s_y_t")
    s_y = sem("s_y")
    s_out = sem("s_out")
    s_fin = sem("s_fin")

    r_lora_w = sem("r_lora_w")
    r_mix = sem("r_mix")
    r_lora = sem("r_lora")
    r_mid = sem("r_mid")
    r_hf = sem("r_hf")
    r_xx = sem("r_xx")
    r_hf0 = sem("r_hf0")
    r_mask = sem("r_mask")
    r_zero = sem("r_zero")
    r_lora_mm = sem("r_lora_mm")
    r_sig = sem("r_sig")
    r_cum = sem("r_cum")
    r_cprev = sem("r_cprev")
    r_sqk = sem("r_sqk")
    r_ss = sem("r_ss")
    r_ssm = sem("r_ssm")
    r_rn = sem("r_rn")
    r_dec = sem("r_dec")
    r_kk = sem("r_kk")
    r_b = sem("r_b")
    r_t = sem("r_t")
    r_k1 = sem("r_k1")
    r_prd = sem("r_prd")
    r_bwt = sem("r_bwt")
    r_feat = sem("r_feat")
    r_rt = sem("r_rt")
    r_br = sem("r_br")
    r_brc = sem("r_brc")
    r_bon = sem("r_bon")
    r_tm = sem("r_tm")
    r_tma = sem("r_tma")
    r_tmv = sem("r_tmv")
    r_pm = sem("r_pm")
    r_pe = sem("r_pe")
    r_xm = sem("r_xm")
    r_xv = sem("r_xv")
    r_m = sem("r_m")
    r_l0 = sem("r_l0")
    r_i0 = sem("r_i0")
    r_i0m = sem("r_i0m")
    r_i0c = sem("r_i0c")
    r_zm = sem("r_zm")
    r_zb = sem("r_zb")
    r_gm = sem("r_gm")
    r_inv = sem("r_inv")
    r_tt = sem("r_tt")
    r_tta = sem("r_tta")
    r_ttv = sem("r_ttv")
    r_lm = sem("r_lm")
    r_last = sem("r_last")
    r_wm = sem("r_wm")
    r_wt = sem("r_wt")
    r_wtm = sem("r_wtm")
    r_w = sem("r_w")
    r_u0 = sem("r_u0")
    r_s0 = sem("r_s0")
    r_um = sem("r_um")
    r_u = sem("r_u")
    r_sm = sem("r_sm")
    r_s1 = sem("r_s1")
    r_s2 = sem("r_s2")
    r_ym = sem("r_ym")
    r_y = sem("r_y")
    r_mean = sem("r_mean")
    r_yc = sem("r_yc")
    r_ysq = sem("r_ysq")
    r_var = sem("r_var")
    r_gmm = sem("r_gmm")
    r_grs = sem("r_grs")
    r_yn = sem("r_yn")
    r_z1 = sem("r_z1")
    r_z2 = sem("r_z2")
    r_g2 = sem("r_g2")

    w_rkv = [a[f"rwkv_w_{n}"][0].rearrange("(k p) n -> p k n", p=P) for n in "rkv"]
    w_wo = a["rwkv_w_o"][0].rearrange("(k p) n -> p k n", p=P)
    w_in = a["attn_w_in"][0].rearrange("(k p) n -> p k n", p=P)
    w_ao = a["attn_w_out"][0].rearrange("(k p) n -> p k n", p=P)
    w_fi = [a["ffn_w_in"][l].rearrange("(k p) n -> p k n", p=P) for l in range(2)]
    w_fo = [a["ffn_w_out"][l].rearrange("(k p) n -> p k n", p=P) for l in range(2)]
    w_mod = [a["mod_w"][l].rearrange("(k p) n -> p k n", p=P) for l in range(2)]
    x_dram = a["x"][0].rearrange("(t p) d -> p t d", p=P)
    out_dram = out[0].rearrange("(t p) d -> p t d", p=P)

    score_of = lambda qt: bank[qt][:, 0:(qt + 1) * P]
    h_of = (lambda k: h_hi[:, k, :], lambda k: h_lo[:, k, :])
    g_of = (lambda k: g_hi[:, k, :], lambda k: g_lo[:, k, :])


    block = ctx.enter_context(nc.Block())

    @block.sync
    def _(sp):
        def load(base, per, i, j, src, tiles=KT):
            sp.wait_ge(s_lo, per * i + (base + j + 1))
            sp.dma_start(raw[:, j % RAW, 0:tiles, :], src).then_inc(s_raw[j % RAW], 16)

        def load_mod(layer, i, k, v):
            sp.wait_ge(s_mod_used, KT * i + (k + 1))
            sp.dma_start(mod_raw[:, k % 2, :], w_mod[layer][:, k, bass.ts(v, D)]).then_inc(s_mod_raw[k % 2], 16)

        sp.dma_start(x_tok[:, :, :], x_dram).then_inc(s_x_tok, 16)
        for n in range(8):
            v, k = n // 4, 2 * (n % 4)
            sp.dma_start(mod_first[:, 2 * n:2 * n + 2, :],
                         w_mod[0][:, k:k + 2, v * D:(v + 1) * D]).then_inc(s_mod_first[n], 16)

        def four(base, i, w):
            for j in range(4):
                load(base, 4, i, j, w[:, :, bass.ts(i * 4 + j, P)])

        with sp.Fori(0, 4) as i:
            for j in range(4):
                load(QKV, 4, i, j, w_in[:, :, bass.ts(i * 4 + j, P)])
                for k in (2 * j, 2 * j + 1):
                    load_mod(0, i, k, i + 2)
        with sp.Fori(4, 6) as i:
            four(QKV, i, w_in)

        def square(base, w):
            with sp.Fori(0, 2) as i:
                four(base, i, w)

        def swiglu(layer, base_in, base_out):
            def weights(i, j):
                for half in range(2):
                    load(base_in, 8, i, 2 * j + half, w_fi[layer][:, :, bass.ds((i * 4 + j + FT * half) * P, P)])

            with sp.Fori(0, 5) as i:
                for j in range(4):
                    weights(i, j)
                    if layer == 0:
                        load_mod(1, i + 4, 2 * j, i)
                        load_mod(1, i + 4, 2 * j + 1, i)
            weights(5, 0)
            weights(5, 1)
            if layer == 0:
                for k in range(KT):
                    load_mod(1, 9, k, 5)
            with sp.Fori(0, 2) as i:
                for j in range(4):
                    for c, (k0, kn) in enumerate(OUT_PARTS):
                        load(base_out, 12, i, 3 * j + c, w_fo[layer][:, k0:k0 + kn, bass.ts(i * 4 + j, P)], kn)

        square(AO, w_ao)
        swiglu(0, FI0, FO0)
        if LAYERS == 2:
            sp.wait_ge(s_mm, SPLIT + RKV)
            sp.dma_start(w1[:, :, :], a["rwkv_w1"][0].rearrange("(k p) n -> p k n", p=P)).then_inc(r_lora_w, 16)
            sp.dma_start(a1[:, :, :], a["rwkv_a1"][0].rearrange("(k p) n -> p k n", p=P)).then_inc(r_lora_w, 16)
            sp.dma_start(g1[:, :, :], a["rwkv_g1"][0].rearrange("(k p) n -> p k n", p=P)).then_inc(r_lora_w, 16)
            sp.dma_start(wa2[0:HD, :], a["rwkv_w2"][0]).then_inc(r_lora_w, 16)
            sp.dma_start(wa2[HD:P, :], a["rwkv_a2"][0]).then_inc(r_lora_w, 16)
            for n in range(3):
                with sp.Fori(0, 2) as i:
                    four(RKV + 8 * n, i, w_rkv[n])
            four(WO, 0, w_wo)
            sp.wait_ge(r_w, KT)
            sp.wait_ge(r_u0, 2 * KT)
            sp.dma_start(g2[:, 0, :], a["rwkv_g2"][0, 0:P, :]).then_inc(r_g2, 16)
            sp.dma_start(g2[0:GL - P, 1, :], a["rwkv_g2"][0, P:GL, :]).then_inc(r_g2, 16)
            four(WO, 1, w_wo)
            swiglu(1, FI1, FO1)
        for half in range(2):
            sp.wait_ge(s_y, 4 * half + 4)
            cols = slice(half * D // 2, (half + 1) * D // 2)
            sp.dma_start(out_dram[:, :, cols], y_tok[:, :, cols]).then_inc(s_out, 16)
        sp.wait_ge(s_out, 32)

    @block.gpsimd
    def _(pool):
        const = [0]

        def step(ins):
            const[0] += 1
            ins.then_inc(s_const, 1)
            pool.wait_ge(s_const, const[0])

        step(pool.memset(ident[:, :], 0.0))
        step(pool.affine_select(out=ident[:, :], in_=ident[:, :], pattern=[[-1, P]], compare_op=ALU.not_equal,
                                fill=1.0, base=0, channel_multiplier=1))
        step(pool.memset(ones[:, :], 1.0))
        step(pool.tensor_copy(ident_b[:, :], ident[:, :]))
        step(pool.memset(causal[:, :], 0.0))
        step(pool.affine_select(out=causal[:, :], in_=causal[:, :], pattern=[[-1, P]], compare_op=ALU.is_ge,
                                fill=NEG, base=0, channel_multiplier=1))
        step(pool.memset(cst[:, 0:1], EPS))
        step(pool.memset(cst[:, 1:2], 1.0))
        step(pool.memset(cst[:, 2:3], GN_EPS))
        step(pool.memset(cst[:, 3:4], LOG_NORM))
        step(pool.memset(qkv_scale[:, :], 1.0))
        step(pool.memset(qkv_scale[:, 0:4], HD ** -0.5))
        step(pool.memset(qkv_scale[:, 12:16], HD ** -0.5))
        step(pool.memset(wf_hi[:, :, :].bitcast(F32), 0.0))
        step(pool.memset(wf_lo[:, :, :].bitcast(F32), 0.0))
        step(pool.memset(fox_sel[:, :], 0.0))
        for row in (0, 32):
            step(pool.affine_select(out=fox_sel[:, :], in_=fox_sel[:, :], pattern=[[-1, NFOX]],
                                    compare_op=ALU.not_equal, fill=1.0, base=-row, channel_multiplier=1))
        step(pool.memset(decay_l[:, :], 0.0))
        step(pool.memset(decay_l[0:NFOX, :], -1.0))
        step(pool.memset(b_f[:, :], 0.0))
        pool.memset(cst[:, 4:5], 0.0).then_inc(s_lo, RAW)
        pool.memset(cst[:, 5:6], 0.0).then_inc(s_mm, SPLIT)
        pool.memset(cst[:, 6:7], 0.0).then_inc(s_bank, NB)
        pool.memset(cst[:, 7:8], 0.0).then_inc(s_mod_used, 2)
        assert const[0] == CONSTS

        def low_parts(lo, hi):
            with pool.Fori(lo // 4, hi // 4) as i:
                for j in range(4):
                    pool.wait_ge(s_hi, 4 * i + (j + 1))
                    pool.tensor_tensor(w_lo[:, j % SPLIT, :, :], raw[:, j % RAW, :, :],
                                       w_hi[:, j % SPLIT, :, :].bitcast(F32), ALU.subtract).then_inc(s_lo, 1)

        low_parts(0, RKV)
        if LAYERS == 2:
            pool.wait_ge(s_mm, SPLIT + RKV)
            mask = [0]

            def mstep(ins):
                mask[0] += 1
                ins.then_inc(r_mask, 1)
                pool.wait_ge(r_mask, mask[0])

            def blocks(dst, size):
                v = dst.rearrange("p (n b) -> p n b", b=size)
                mstep(pool.affine_select(out=v, in_=v, pattern=[[-size, P // size], [0, size]], compare_op=ALU.is_ge,
                                         fill=0.0, base=0, channel_multiplier=1))
                mstep(pool.affine_select(out=v, in_=v, pattern=[[size, P // size], [0, size]], compare_op=ALU.is_ge,
                                         fill=0.0, base=size - 1, channel_multiplier=-1))

            mstep(pool.memset(levels[:, :, :], 1.0))
            mstep(pool.memset(join_t[:, 0, 0:2, :], 1.0))
            mstep(pool.memset(heads2[:, :], 1.0))
            mstep(pool.memset(restart[:, :], 1.0))
            mstep(pool.memset(restart[:, :].rearrange("p (n c) -> p n c", c=CH)[:, :, 0:1], 0.0))
            for l in range(6):
                blocks(levels[:, l, :], 2 << l)
            blocks(heads2[:, :], HD)
            for l in range(5, 0, -1):
                mstep(pool.tensor_tensor(levels[:, l, :], levels[:, l, :], levels[:, l - 1, :], ALU.subtract))
            for l in range(6):
                mstep(pool.affine_select(out=levels[:, l, :], in_=levels[:, l, :], pattern=[[1, P]], compare_op=ALU.is_gt,
                                         fill=0.0, base=0, channel_multiplier=-1))
            for q, op in enumerate((ALU.is_gt, ALU.is_ge)):
                blocks(join_t[:, 0, q, :], CH)
                mstep(pool.affine_select(out=join_t[:, 0, q, :], in_=join_t[:, 0, q, :], pattern=[[1, P]], compare_op=op,
                                         fill=0.0, base=0, channel_multiplier=-1))
            mstep(pool.tensor_tensor(before[:, :, :], join_t[:, 0, 0:2, 0:CH], join_t[:, 0, 0:2, CH:P], ALU.add))
            assert mask[0] == MASKS
            pool.wait_ge(r_hf0, 1)
            for k in range(KT):
                pool.wait_ge(r_hf, k + 1)
                pool.tensor_tensor(xx[:, k, :], h_f[:, k, 3:3 + S], h_f[:, k, 4:4 + S], ALU.subtract).then_inc(r_xx, 1)
            low_parts(RKV, WO)
            pool.wait_ge(s_mm, SPLIT + WO)
            pool.memset(inv_t[:, :, :], 0.0).then_inc(r_zero, 1)
            pool.memset(join_t[:, :, :, :], 0.0).then_inc(r_zero, 1)
            pool.wait_ge(r_zero, 2)
            for seg in rwkv_order():
                kind, p = seg[0], seg[1]

                def level_part(l, e, src, dst):
                    rows = slice(CH * e, CH * e + CH)
                    n = dst.shape[1] // TT
                    pool.tensor_tensor(dst[rows, :, rows].rearrange("s (h c) t -> s h c t", h=n), src[rows, :, e::2, 0, :],
                                       levels[rows, l, rows].unsqueeze(1).unsqueeze(1).broadcast_to((CH, n, TT, CH)),
                                       ALU.mult).then_inc(r_m, 1)

                if kind == "prep_prev":
                    pool.wait_ge(r_cum, p + 1)
                    pool.tensor_tensor(rstd[:, :], ring[:, 2, :], ring[:, 0, :], ALU.subtract).then_inc(r_cprev, 1)
                    pool.wait_ge(r_cprev, p + 1)
                elif kind == "prep_a":
                    pool.wait_ge(r_kk, p + 1)
                    pool.tensor_tensor(ssq[:, :], key[:, :], ring[:, 1, :], ALU.mult).then_inc(r_b, 1)
                    pool.wait_ge(r_b, p + 1)
                elif kind == "prep_k":
                    pool.wait_ge(r_feat, 5 * p + 3)
                    pool.tensor_copy(rkv[:, p, :], ar_f[:, 1, :]).then_inc(r_rt, 1)
                    pool.wait_ge(r_rt, p + 1)
                elif kind == "first":
                    for hd in range(2):
                        pool.wait_ge(r_pe, 4 * p + 2 * hd + 2)
                        if p and hd == 0:
                            pool.wait_ge(r_wm, 2 * p)
                        level_part(0, 1, ar[:, p % 2, hd:hd + 1, :, :, :], inv_t[:, 4 * hd:4 * hd + 4, :])
                        pool.wait_ge(r_m, 12 * p + hd + 1)
                if kind == "first" or kind == "join" and seg[2] < 5:
                    l = seg[2] + 1 if kind == "join" else 1
                    if 5 * p + l > 2:
                        pool.wait_ge(r_zm, 10 * p + 2 * (l - 2))
                    for e in range(2):
                        level_part(l, e, ar[:, p % 2, :, :, :, :], join_t[:, (p + l) % 2, :, :])
                        pool.wait_ge(r_m, 12 * p + 2 * l + e + 1)
                    if l == 2:
                        pool.wait_ge(r_brc, p + 1)
                        pool.wait_ge(r_tm, 4 * p + 4)
                        pool.tensor_tensor(rkv[:, 2 * KT + p, :], rkv[:, 2 * KT + p, :], bonus[:, :], ALU.mult).then_inc(r_bon, 1)
                        pool.wait_ge(r_bon, p + 1)
            low_parts(WO, CHUNKS)

    @block.scalar
    def _(act):
        def split(base, per, i, j):
            if isinstance(i, int) and base + per * i + j + 2 >= total:
                return
            act.wait_ge(s_raw[(j + 2) % RAW], 4 * per * i + 16 * (base // 4 + (j + 2) // 4 + 1))
            act.wait_ge(s_mm, per * i + (base + j + 3))
            act.activation(w_hi[:, j % SPLIT, :, :], raw[:, (j + 2) % RAW, :, :], ACT.Copy).then_inc(s_hi, 1)

        total = CHUNKS if LAYERS == 2 else FO0 + 24
        row = 0
        for src in (a["c"].rearrange("b (k p) -> (b k) p", p=P), a["mod_b"].rearrange("l (k p) -> (l k) p", p=P),
                    a["norm_mix"].rearrange("l (k p) -> (l k) p", p=P)):
            act.dma_start(rows_a[row:row + src.shape[0], :], src).then_inc(s_rows, 16)
            row += src.shape[0]
        row = 0
        for src in (a["norm_ffn"].rearrange("l (k p) -> (l k) p", p=P), a["norm_final"].rearrange("(k p) -> k p", p=P),
                    a["rwkv_mu"][0].rearrange("i (k p) -> (i k) p", p=P), a["rwkv_w0"].rearrange("l (k p) -> (l k) p", p=P),
                    a["rwkv_a0"].rearrange("l (k p) -> (l k) p", p=P), a["rwkv_k_k"].rearrange("l (k p) -> (l k) p", p=P),
                    a["rwkv_k_a"].rearrange("l (k p) -> (l k) p", p=P),
                    a["rwkv_r_k"][0].rearrange("(k g) j -> k (g j)", g=2),
                    a["rwkv_ln_w"].rearrange("l (k p) -> (l k) p", p=P), a["rwkv_ln_b"].rearrange("l (k p) -> (l k) p", p=P)):
            act.dma_start(rows_b[row:row + src.shape[0], :], src).then_inc(s_rows, 16)
            row += src.shape[0]
        act.dma_start(wf_raw[:, :, :], w_in[:, :, 24 * P:24 * P + NFOX]).then_inc(s_wf, 16)
        act.wait_ge(s_const, CONSTS)
        for r0 in (0, 32):
            act.dma_start(b_f[r0:r0 + NFOX, :], a["attn_b_f"].rearrange("l h -> h l")).then_inc(s_wf, 16)

        act.wait_ge(s_par, 1)
        act.activation(cond[:, :], par_a[:, A_C:A_C + KT], ACT.Silu).then_inc(s_cond, 1)
        act.wait_ge(s_mm, SPLIT)
        split(0, 4, 0, -2)
        split(0, 4, 0, -1)
        for k in range(KT):
            act.wait_ge(s_xt, k + 1)
            if k >= 2:
                act.wait_ge(s_ssq, k - 1)
            act.activation(ring[:, k % 2, :], bank[k % 4][:, :], ACT.Square).then_inc(s_sq, 1)
            act.activation(x[:, k, :], bank[k % 4][:, :], ACT.Copy).then_inc(s_x0, 1)
        act.wait_ge(s_wf, 48)
        for r0 in (0, 32):
            act.activation(wf_hi[:, :, r0:r0 + NFOX], wf_raw[:, :, :], ACT.Copy).then_inc(s_wf_split, 1)

        def norm_rstd(n):
            act.wait_ge(s_ssum, n + 1)
            act.activation(rstd[:, :], bank[7][:, :], ACT.Ln, bias=cst[:, 0:1], scale=1.0 / D).then_inc(s_ln, 1)
            act.wait_ge(s_ln, n + 1)
            act.activation(rstd[:, :], rstd[:, :], ACT.Exp, scale=-0.5).then_inc(s_rstd, 1)

        def norm_hi(n, h0, layer, v):
            norm_rstd(n)
            for k in range(KT):
                act.wait_ge(s_u, KT * n + k + 1)
                act.activation(h_hi[:, k, :], ring[:, k % 4, :], ACT.Identity,
                               bias=mod_t[:, layer, v * KT + k:v * KT + k + 1]).then_inc(s_h_hi, 1)

        norm_hi(0, H_MIX0, 0, 0)
        act.wait_ge(s_fv, 2)
        act.activation(ring[:, 2, :], ring[:, 1, :], ACT.Exp).then_inc(s_fa, 1)
        act.wait_ge(s_fa, 1)
        act.activation(ring[:, 3, :], ring[:, 2, :], ACT.Ln, bias=cst[:, 1:2]).then_inc(s_fa, 1)

        def four(base, i):
            for j in range(4):
                split(base, 4, i, j)

        with act.Fori(0, 6) as i:
            four(QKV, i)

        for n in range(0, 8, 2):
            act.wait_ge(s_v_t, n + 1)
            act.activation(v_tok[:, n // 2, (n % 2) * S:(n % 2 + 1) * S], bank[4 + n % 2][:, :], ACT.Copy).then_inc(s_v_tok, 1)
        for h in range(NH + 1):
            if h < NH:
                for qt in range(TT):
                    act.wait_ge(s_max, TT * h + qt + 1)
                    if h >= 2:
                        act.wait_ge(s_pt, h - 1)
                    act.activation(prob[:, h % 2, COL[qt]:COL[qt + 1]], score_of(qt), ACT.Exp,
                                   bias=row_stat[:, h % 2, 0, qt:qt + 1],
                                   accum_out=row_stat[:, h % 2, 1, qt:qt + 1]).then_inc(s_exp, 1)
            if h >= 1:
                g = h - 1
                act.wait_ge(s_pt, g + 1)
                if g >= 2:
                    act.wait_ge(s_pv, g - 1)
                act.activation(prob_t[:, g % 2, 0:S], bank[4][:, :], ACT.Copy).then_inc(s_pt_a, 1)
                if g % 2:
                    pair = g // 2
                    act.wait_ge(s_pv, g + 1)
                    act.activation(h_hi[:, pair, :], bank[7][:, :], ACT.Copy).then_inc(s_h_hi, 1)

        def square_x(n, t0, i, j):
            act.wait_ge(s_bank, 4 * i + (NB + t0 + j + 1))
            act.wait_ge(s_ssq, 4 * i + (KT * n + j - 1))
            act.activation(ring[:, j % 2, :], x[:, i * 4 + j, :], ACT.Square).then_inc(s_sq, 1)

        def square(base, t0, n):
            with act.Fori(0, 2) as i:
                for j in range(4):
                    split(base, 4, i, j)
                    square_x(n, t0, i, j)

        def swiglu(layer, base_in, base_out, t_in, t_out):
            def pairs(i, tiles):
                for j in range(tiles):
                    split(base_in, 8, i, 2 * j)
                    act.wait_ge(s_mm, 8 * i + (SPLIT + base_in + 2 * j + 1))
                    act.activation(ring[:, j % 2, :], bank[2 * j % 4][:, :], ACT.Silu).then_inc(s_silu, 1)
                    split(base_in, 8, i, 2 * j + 1)
                    act.wait_ge(s_bank, 8 * i + (NB + t_in + 2 * j + 2))
                    act.activation(g_hi[:, i * 4 + j, :], ring[:, 2 + j % 2, :], ACT.Copy).then_inc(s_g_hi, 1)

            with act.Fori(0, 5) as i:
                pairs(i, 4)
            pairs(5, 2)

            def out(i):
                for j in range(4):
                    for c in range(3):
                        split(base_out, 12, i, 3 * j + c)
                    square_x(2 + 2 * layer, t_out, i, j)

            with act.Fori(0, 1) as i:
                out(i)
            out(1)

        square(AO, T_AO, 1)
        norm_hi(1, H_FFN0, 0, 3)
        swiglu(0, FI0, FO0, T_FI0, T_FO0)
        if LAYERS == 2:
            norm_rstd(2)
            for k in range(KT):
                act.wait_ge(s_u, KT * 2 + k + 1)
                act.activation(h_f[:, k, 4:4 + S], ring[:, k % 4, :], ACT.Identity,
                               bias=mod_t[:, 1, k:k + 1]).then_inc(r_hf, 1)
            act.wait_ge(r_lora, 8)
            act.activation(wa_mid[0:HD, :], bank[0][0:HD, :], ACT.Tanh).then_inc(r_mid, 1)
            act.wait_ge(r_lora, 16)
            act.activation(wa_mid[HD:P, :], bank[1][HD:P, :], ACT.Copy).then_inc(r_mid, 1)
            act.wait_ge(r_lora, 24)
            act.activation(g_mid[:, 0, :], bank[2][:, :], ACT.Sigmoid).then_inc(r_mid, 1)
            act.activation(g_mid[0:GL - P, 1, :], bank[3][0:GL - P, :], ACT.Sigmoid).then_inc(r_mid, 1)
            for n in range(3):
                if n:
                    act.wait_ge(s_mm, SPLIT + RKV + 8 * n)
                for k in range(KT):
                    act.wait_ge(r_mix, 24 + 8 * n + k + 1)
                    act.activation(h_hi[:, k, :], ring[:, k % 4, :], ACT.Copy).then_inc(s_h_hi, 1)
                with act.Fori(0, 2) as i:
                    four(RKV + 8 * n, i)
            par = lambda b, p: par_b[:, b + p:b + p + 1]
            for seg in rwkv_order():
                kind, p = seg[0], seg[1]
                kp = rkv[:, KT + p, :]
                if kind == "prep_lora":
                    if p:
                        act.wait_ge(r_feat, 5 * p)
                        act.wait_ge(r_br, p)
                    act.activation(ring[:, 3, :], kp, ACT.Square, scale=par(B_KK, p)).then_inc(r_sqk, 1)
                elif kind == "prep_sig":
                    act.wait_ge(r_lora_mm, 2 * p + 2)
                    act.activation(ring[:, 0, :], bank[0][:, :], ACT.Sigmoid, bias=par(B_W0, p)).then_inc(r_sig, 1)
                    act.activation(ring[:, 1, :], bank[1][:, :], ACT.Sigmoid, bias=par(B_A0, p)).then_inc(r_sig, 1)
                elif kind == "prep_ln":
                    act.wait_ge(r_ssm, p + 1)
                    act.activation(ring[:, 3, :], ring[:, 3, :], ACT.Ln, scale=2.0 ** 20).then_inc(r_rn, 1)
                elif kind == "prep_norm":
                    act.wait_ge(r_rn, 2 * p + 1)
                    act.activation(ring[:, 3, :], ring[:, 3, :], ACT.Exp, scale=-0.5, bias=cst[:, 3:4]).then_inc(r_rn, 1)
                elif kind == "prep_decay":
                    act.wait_ge(r_cprev, p + 1)
                    act.activation(ring[:, 0, :], ring[:, 2, :], ACT.Exp, scale=DECAY).then_inc(r_dec, 1)
                    act.activation(ring[:, 2, :], ring[:, 2, :], ACT.Exp, scale=-DECAY).then_inc(r_dec, 1)
                elif kind == "prep_key":
                    act.activation(rstd[:, :], rstd[:, :], ACT.Exp, scale=DECAY).then_inc(r_dec, 1)
                elif kind == "prep_bonus":
                    act.wait_ge(r_br, p + 1)
                    if p:
                        act.wait_ge(r_bon, p)
                    act.activation(bonus[:, :], bank[0][:, :], ACT.Copy).then_inc(r_brc, 1)
                elif kind == "tok_bk":
                    act.wait_ge(r_tm, 4 * p + 1)
                    act.activation(bk_tok[:, p % 2, 0:4, :], bank[4][:, :], ACT.Copy).then_inc(r_tma, 1)
                elif kind == "tok_av":
                    act.wait_ge(r_tm, 4 * p + 3)
                    act.activation(ax_tok[:, :, 0, :], bank[2][:, :].rearrange("p (c f) -> p c f", c=TT), ACT.Copy).then_inc(r_tma, 1)
                    act.wait_ge(r_tm, 4 * p + 4)
                    act.activation(uv[CH:P, p % 2, 0, :, :], bank[3][CH:P, :], ACT.Copy).then_inc(r_tma, 1)
                    act.activation(uv[0:CH, p % 2, 1, :, :], bank[3][0:CH, :], ACT.Copy).then_inc(r_tma, 1)
                elif kind == "intra":
                    e = seg[2]
                    rows = slice(CH * e, CH * e + CH)
                    act.wait_ge(r_xm, 2 * p + e + 1)
                    act.activation(ax_tok[rows, :, 1, :], bank[(3, 5)[e]][rows, :].rearrange("p (c f) -> p c f", c=TT),
                                   ACT.Copy).then_inc(r_xv, 1)
                elif kind == "first":
                    for g in range(2):
                        act.wait_ge(r_i0m, 2 * p + g + 1)
                        act.activation(inv[:, 4 * g:4 * g + 4, :], bank[4 + g][:, :], ACT.Copy).then_inc(r_i0c, 1)
                elif kind == "join":
                    for g in range(2):
                        act.wait_ge(r_zm, 2 * (5 * p + seg[2] - 1) + g + 1)
                        act.activation(prod[:, 4 * g:4 * g + 4, :], bank[2 + g][:, :], ACT.Copy).then_inc(r_zb, 1)
                elif kind == "turn":
                    act.wait_ge(r_tt, 8 * p + 2 * seg[2])
                    act.activation(inv_t[:, 4:8, :], bank[5][:, :], ACT.Copy).then_inc(r_tta, 1)
                elif kind == "wu":
                    for hd in range(2):
                        act.wait_ge(r_wm, 2 * p + hd + 1)
                        act.activation(w_tok[:, :, HD * hd:HD * hd + HD],
                                       bank[2 + hd][:, :].rearrange("p (c a f) -> p c a f", c=TT, a=2)[:, :, 0, :],
                                       ACT.Copy).then_inc(r_wt, 1)
                    for hd in range(2):
                        act.activation(u0[:, :, HD * hd:HD * hd + HD],
                                       bank[2 + hd][:, :].rearrange("p (c a f) -> p c a f", c=TT, a=2)[:, :, 1, :],
                                       ACT.Copy).then_inc(r_u0, 1)
                elif kind == "w_back":
                    act.wait_ge(r_wtm, p + 1)
                    act.activation(w_f[:, :], bank[1][:, :], ACT.Copy).then_inc(r_w, 1)
                elif kind == "out":
                    n = seg[2]
                    act.wait_ge(r_ym, NC * p + n + 1)
                    act.activation(kp[:, n * CH:(n + 1) * CH], bank[6][:, 256:256 + CH], ACT.Copy).then_inc(r_y, 1)
            for p in range(KT + 1):
                if p < KT:
                    act.wait_ge(r_yc, p + 1)
                    if p >= 2:
                        act.wait_ge(r_yn, p - 1)
                    act.activation(ring[:, p % 2, :], rkv[:, KT + p, :], ACT.Square).then_inc(r_ysq, 1)
                    act.wait_ge(r_var, p + 1)
                    act.activation(ring[:, p % 2, :], bank[2 + p % 2][:, :], ACT.Ln, scale=1.0 / HD,
                                   bias=cst[:, 2:3]).then_inc(r_grs, 1)
                    act.wait_ge(r_grs, 2 * p + 1)
                    act.activation(ring[:, p % 2, :], ring[:, p % 2, :], ACT.Exp, scale=-0.5).then_inc(r_grs, 1)
                if p >= 1:
                    act.wait_ge(r_z2, p)
                    act.activation(h_hi[:, p - 1, :], ring[:, 2 + (p - 1) % 2, :], ACT.Copy).then_inc(s_h_hi, 1)
            square(WO, T_WO, 3)
            norm_hi(3, H_FFN1, 1, 3)
            swiglu(1, FI1, FO1, T_FI1, T_FO1)
        norm_rstd(LAST)
        for k in range(KT):
            act.wait_ge(s_y_t, k + 1)
            act.activation(y_tok[:, :, k * P:(k + 1) * P], bank[k % 4][:, :].rearrange("p (t f) -> p t f", t=TT),
                           ACT.Copy).then_inc(s_y, 1)

    @block.vector
    def _(dve):
        def gate_col(layer, v, k):
            return mod_t[:, layer, v * KT + k:v * KT + k + 1]

        dve.wait_ge(s_par_t, 1)
        dve.tensor_copy(par_a[:, :], bank[4][:, 0:A_ROWS]).then_inc(s_par, 1)
        dve.tensor_copy(par_b[:, :], bank[5][:, 0:P]).then_inc(s_par, 1)
        dve.memset(ssq[:, :], 0.0).then_inc(s_ssq0, 1)
        dve.memset(decay_r[:, :], 1.0).then_inc(s_fv0, 1)
        dve.wait_ge(s_cond, 1)
        dve.wait_ge(s_par, 2)
        dve.wait_ge(s_ssq0, 1)
        for v in range(2):
            for k in range(KT):
                n = KT * v + k
                dve.wait_ge(s_mod_first[n // 2], 16)
                if k == 0:
                    dve.tensor_scalar(mod_first[:, n, :], mod_first[:, n, :], cond[:, 0:1], None, ALU.mult).then_inc(s_mod0, 1)
                else:
                    dve.wait_ge(s_mod0, n)
                    dve.scalar_tensor_tensor(out=mod_first[:, KT * v, :], in0=mod_first[:, n, :], scalar=cond[:, k:k + 1],
                                             in1=mod_first[:, KT * v, :], op0=ALU.mult, op1=ALU.add).then_inc(s_mod0, 1)
                if v == 0:
                    dve.wait_ge(s_sq, k + 1)
                    if k >= 1:
                        dve.wait_ge(s_ssq, k)
                    dve.tensor_tensor(ssq[:, :], ssq[:, :], ring[:, k % 2, :], ALU.add).then_inc(s_ssq, 1)

        def mod_chunk(i, k):
            dve.wait_ge(s_mod_raw[k % 2], 64 * i + 16 * (k // 2 + 1))
            if k == 0:
                dve.wait_ge(s_mod_sum, i + 2)
                dve.tensor_scalar(mod_acc[:, :], mod_raw[:, 0, :], cond[:, 0:1], None, ALU.mult).then_inc(s_mod_used, 1)
            else:
                dve.wait_ge(s_mod_used, 8 * i + (2 + k))
                dve.scalar_tensor_tensor(out=mod_acc[:, :], in0=mod_raw[:, k % 2, :], scalar=cond[:, k:k + 1],
                                         in1=mod_acc[:, :], op0=ALU.mult, op1=ALU.add).then_inc(s_mod_used, 1)

        def mod_finish(layer, v, group):
            dve.wait_ge(s_mod_sum, group + 1)
            dve.tensor_tensor(mod_t[:, layer, bass.ts(v, KT)], bank[7][:, 0:KT],
                              par_a[:, bass.ds(v * KT + (A_MODB + 6 * KT * layer), KT)], ALU.add).then_inc(s_mod, 1)

        def set_gain(n, layer, v, norm):
            dve.scalar_tensor_tensor(out=gain[:, n, :], in0=mod_t[:, layer, v * KT:(v + 1) * KT], scalar=1.0, in1=norm,
                                     op0=ALU.add, op1=ALU.mult).then_inc(s_gain, 1)

        mod_finish(0, 0, 0)
        mod_finish(0, 1, 1)
        dve.wait_ge(s_mod, 2)
        set_gain(0, 0, 1, par_a[:, A_NMIX:A_NMIX + KT])
        dve.wait_ge(s_x0, KT)
        dve.wait_ge(s_wf_split, 2)
        for r0 in (0, 32):
            dve.tensor_tensor(wf_lo[:, :, r0:r0 + NFOX], wf_raw[:, :, :], wf_hi[:, :, r0:r0 + NFOX].bitcast(F32),
                              ALU.subtract).then_inc(s_wf_lo, 1)

        def norm_u(n, k, gcol):
            dve.scalar_tensor_tensor(out=ring[:, k % 4, :], in0=x[:, k, :], scalar=gcol, in1=rstd[:, :],
                                     op0=ALU.mult, op1=ALU.mult).then_inc(s_u, 1)

        def norm_split(n, h0, layer, v):
            dve.wait_ge(s_gain, n + 1)
            dve.wait_ge(s_rstd, n + 1)
            for k in range(KT + 1):
                if k < KT:
                    if k >= 4:
                        dve.wait_ge(s_h_hi, h0 + k - 3)
                    norm_u(n, k, gain[:, n, k:k + 1])
                if k >= 1:
                    q = k - 1
                    dve.wait_ge(s_u, KT * n + q + 1)
                    dve.wait_ge(s_h_hi, h0 + q + 1)
                    dve.scalar_tensor_tensor(out=h_lo[:, q, :], in0=ring[:, q % 4, :], scalar=gate_col(layer, v, q),
                                             in1=h_hi[:, q, :].bitcast(F32), op0=ALU.add, op1=ALU.subtract).then_inc(s_h, 1)

        norm_split(0, H_MIX0, 0, 0)
        dve.wait_ge(s_f, 1)
        dve.tensor_scalar(ring[:, 0, :], bank[6][:, :], b_f[:, 0:1], None, ALU.add).then_inc(s_fv, 1)
        dve.wait_ge(s_fv, 1)
        dve.scalar_tensor_tensor(out=ring[:, 1, :], in0=ring[:, 0, :], scalar=-1.0, in1=ring[:, 0, :],
                                 op0=ALU.mult, op1=ALU.min).then_inc(s_fv, 1)
        dve.wait_ge(s_fa, 2)
        dve.scalar_tensor_tensor(out=ring[:, 1, :], in0=ring[:, 0, :], scalar=0.0, in1=ring[:, 3, :],
                                 op0=ALU.min, op1=ALU.subtract).then_inc(s_fv, 1)
        dve.wait_ge(s_fv, 3)
        dve.wait_ge(s_fv0, 1)
        dve.tensor_tensor_scan(ring[:, 2, :], decay_r[:, :], ring[:, 1, :], 0.0, ALU.mult, ALU.add).then_inc(s_fv, 1)
        dve.wait_ge(s_fv, 4)
        dve.tensor_copy(decay_l[32:32 + NFOX, :], ring[32:32 + NFOX, 2, :]).then_inc(s_fv, 1)
        dve.tensor_copy(decay_r[0:NFOX, :], ring[0:NFOX, 2, :]).then_inc(s_fv, 1)
        dve.wait_ge(s_fv, 6)

        def select_decay(h):
            dve.tensor_scalar(decay_h[:, h % 2, :], decay_l[:, :], fox_sel[:, h:h + 1], None, ALU.mult).then_inc(s_dh, 1)

        select_decay(0)
        select_decay(1)

        def evict_qkv(i, j):
            dve.wait_ge(s_mm, 4 * i + (SPLIT + QKV + j + 1))
            dve.tensor_scalar(qkv[:, i * 4 + j, :], bank[j][:, :], qkv_scale[:, bass.ds(i * 4 + j, 1)], None,
                              ALU.mult).then_inc(s_bank, 1)

        with dve.Fori(0, 4) as i:
            for j in range(4):
                mod_chunk(i, 2 * j)
                mod_chunk(i, 2 * j + 1)
                evict_qkv(i, j)
            mod_finish(0, i + 2, i + 2)
        with dve.Fori(4, 6) as i:
            for j in range(4):
                evict_qkv(i, j)

        for n in range(1, 8, 2):
            dve.wait_ge(s_v_t, n + 1)
            dve.tensor_copy(v_tok[:, n // 2, (n % 2) * S:(n % 2 + 1) * S], bank[4 + n % 2][:, :]).then_inc(s_v_tokv, 1)
        dve.wait_ge(s_mod, 6)
        set_gain(1, 0, 4, par_b[:, B_NFFN:B_NFFN + KT])
        for h in range(NH + 1):
            g = h - 1
            for qt in range(TT):
                if g >= 0:
                    dve.wait_ge(s_exp, TT * g + qt + 1)
                    dve.reciprocal(row_stat[:, g % 2, 2, qt:qt + 1], row_stat[:, g % 2, 1, qt:qt + 1]).then_inc(s_rinv, 1)
                if h < NH:
                    dve.wait_ge(s_score, TT * h + qt + 1)
                    dve.tensor_reduce(row_stat[:, h % 2, 0, qt:qt + 1], score_of(qt), AX_X, ALU.max,
                                      negate=True).then_inc(s_max, 1)
                if g >= 0:
                    dve.wait_ge(s_rinv, TT * g + qt + 1)
                    dve.tensor_scalar(prob[:, g % 2, COL[qt]:COL[qt + 1]], prob[:, g % 2, COL[qt]:COL[qt + 1]],
                                      row_stat[:, g % 2, 2, qt:qt + 1], None, ALU.mult).then_inc(s_norm, 1)
            if h < NFOX - 2:
                select_decay(h + 2)
            if g >= 0:
                dve.wait_ge(s_pt, g + 1)
                if g >= 2:
                    dve.wait_ge(s_pv, g - 1)
                dve.tensor_copy(prob_t[:, g % 2, S:S + 384], bank[5][:, 0:384]).then_inc(s_pt_v, 1)
                dve.tensor_copy(prob_t[:, g % 2, S + 384:1280], bank[6][:, 0:384]).then_inc(s_pt_v, 1)
                if g % 2:
                    pair = g // 2
                    dve.wait_ge(s_h_hi, H_ATT + pair + 1)
                    dve.tensor_tensor(h_lo[:, pair, :], bank[7][:, :], h_hi[:, pair, :].bitcast(F32),
                                      ALU.subtract).then_inc(s_h, 1)

        def residual(base, per, last, layer, v, n, t0, i, j):
            dve.wait_ge(s_mm, per * i + (SPLIT + base + last + 1))
            dve.scalar_tensor_tensor(out=x[:, i * 4 + j, :], in0=bank[j][:, :],
                                     scalar=mod_t[:, layer, bass.ds(i * 4 + (v * KT + j), 1)], in1=x[:, i * 4 + j, :],
                                     op0=ALU.mult, op1=ALU.add).then_inc(s_bank, 1)
            dve.wait_ge(s_sq, 4 * i + (KT * n + j + 1))
            dve.wait_ge(s_ssq, 4 * i + (KT * n + j))
            dve.tensor_tensor(ssq[:, :], ssq[:, :], ring[:, j % 2, :], ALU.add).then_inc(s_ssq, 1)

        def clear_ssq(n):
            dve.wait_ge(s_ssum, n)
            dve.memset(ssq[:, :], 0.0).then_inc(s_ssq0, 1)
            dve.wait_ge(s_ssq0, n + 1)

        def square(base, layer, t0, n):
            clear_ssq(n)
            with dve.Fori(0, 2) as i:
                for j in range(4):
                    residual(base, 4, j, layer, 2, n, t0, i, j)

        def swiglu(layer, base_in, base_out, t_in):
            def pairs(i, tiles):
                for j in range(tiles):
                    at = FT * layer + j + 1
                    if layer == 0:
                        per = KT // tiles
                        for k in range(per * j, per * j + per):
                            mod_chunk(i + 4, k)
                    dve.wait_ge(s_silu, 4 * i + at)
                    dve.wait_ge(s_mm, 8 * i + (SPLIT + base_in + 2 * j + 2))
                    dve.tensor_tensor(ring[:, 2 + j % 2, :], ring[:, j % 2, :], bank[(2 * j + 1) % 4][:, :],
                                      ALU.mult).then_inc(s_bank, 2)
                    dve.wait_ge(s_g_hi, 4 * i + at)
                    dve.tensor_tensor(g_lo[:, i * 4 + j, :], ring[:, 2 + j % 2, :], g_hi[:, i * 4 + j, :].bitcast(F32),
                                      ALU.subtract).then_inc(s_g, 1)
                if layer == 0:
                    mod_finish(1, i, i + 6)

            with dve.Fori(0, 5) as i:
                pairs(i, 4)
            pairs(5, 2)
            n = 2 + 2 * layer
            clear_ssq(n)
            with dve.Fori(0, 2) as i:
                for j in range(4):
                    residual(base_out, 12, 3 * j + 2, layer, 5, n, 0, i, j)

        square(AO, 0, T_AO, 1)
        norm_split(1, H_FFN0, 0, 3)
        swiglu(0, FI0, FO0, T_FI0)
        dve.wait_ge(s_mod, 12)
        set_gain(2, 1, 1, par_a[:, A_NMIX + KT:A_NMIX + 2 * KT])
        set_gain(3, 1, 4, par_b[:, B_NFFN + KT:B_NFFN + 2 * KT])
        if LAYERS == 2:
            dve.wait_ge(s_mm, SPLIT + RKV)
            dve.memset(h_f[:, :, 3:4], 0.0).then_inc(r_hf0, 1)
            dve.wait_ge(s_gain, 4)
            dve.wait_ge(s_rstd, 3)
            for k in range(KT):
                if k >= 4:
                    dve.wait_ge(r_hf, k - 3)
                norm_u(2, k, gain[:, 2, k:k + 1])
            m = 0
            for n, mu in enumerate((1, 4, 5, 0, 2, 3)):
                for k in range(KT + 1):
                    if k < KT:
                        dve.wait_ge(r_xx, k + 1)
                        if m < 4:
                            dve.wait_ge(r_hf, KT)
                        elif m < 28:
                            dve.wait_ge(r_lora, m - 3)
                        else:
                            dve.wait_ge(s_h_hi, H_R + m - 27)
                        dve.scalar_tensor_tensor(out=ring[:, m % 4, :], in0=xx[:, k, :],
                                                 scalar=par_b[:, B_MU + 8 * mu + k:B_MU + 8 * mu + k + 1],
                                                 in1=h_f[:, k, 4:4 + S], op0=ALU.mult, op1=ALU.add).then_inc(r_mix, 1)
                        m += 1
                    if n >= 3 and k >= 1:
                        q = 8 * (n - 3) + k
                        dve.wait_ge(r_mix, 24 + q)
                        dve.wait_ge(s_h_hi, H_R + q)
                        dve.tensor_tensor(h_lo[:, k - 1, :], ring[:, (k - 1) % 4, :], h_hi[:, k - 1, :].bitcast(F32),
                                          ALU.subtract).then_inc(s_h, 1)
                if n >= 3:
                    with dve.Fori(0, 2) as i:
                        for j in range(4):
                            dve.wait_ge(s_mm, 4 * i + (SPLIT + RKV + 8 * (n - 3) + j + 1))
                            dve.tensor_copy(rkv[:, i * 4 + (8 * (n - 3) + j), :], bank[j][:, :]).then_inc(s_bank, 1)
            dve.wait_ge(r_mask, MASKS)
            for seg in rwkv_order():
                kind, p = seg[0], seg[1]
                rp, kp, vp = rkv[:, p, :], rkv[:, KT + p, :], rkv[:, 2 * KT + p, :]
                par = lambda b: par_b[:, b + p:b + p + 1]
                if kind == "prep_cum":
                    dve.wait_ge(r_sig, 2 * p + 1)
                    dve.tensor_tensor_scan(ring[:, 2, :], restart[:, :], ring[:, 0, :], 0.0, ALU.mult, ALU.add).then_inc(r_cum, 1)
                elif kind == "prep_prev":
                    dve.wait_ge(r_ss, p + 1)
                    dve.tensor_scalar(ring[:, 3, :], bank[0][:, :], 1e-24, None, ALU.max).then_inc(r_ssm, 1)
                elif kind == "prep_key":
                    dve.wait_ge(r_rn, 2 * p + 2)
                    dve.scalar_tensor_tensor(out=key[:, :], in0=kp, scalar=par(B_KK), in1=ring[:, 3, :],
                                             op0=ALU.mult, op1=ALU.mult).then_inc(r_kk, 1)
                    dve.tensor_scalar(bonus_w[:, :], heads2[:, :], par(B_RK), None, ALU.mult).then_inc(r_bwt, 1)
                elif kind == "prep_a":
                    dve.wait_ge(r_kk, p + 1)
                    dve.wait_ge(r_dec, 3 * p + 3)
                    dve.scalar_tensor_tensor(out=ar_f[:, 0, :], in0=key[:, :], scalar=-1.0, in1=rstd[:, :], op0=ALU.mult,
                                             op1=ALU.mult).then_inc(r_feat, 1)
                elif kind in ("prep_b", "prep_r", "prep_k"):
                    bk = lambda slots: bk_f[:, :, slots, :]
                    by_chunk = lambda t: t.rearrange("p (c e t) -> p c e t", e=2, t=CH)
                if kind == "prep_b":
                    dve.wait_ge(r_b, p + 1)
                    dve.tensor_scalar(ring[:, 1, :], ring[:, 1, :], -1.0, par(B_KA), ALU.add, ALU.mult).then_inc(r_t, 1)
                    dve.tensor_tensor(bk(slice(0, 4, 3)), by_chunk(ssq[:, :]), by_chunk(ring[:, 2, :]), ALU.mult).then_inc(r_feat, 1)
                    dve.wait_ge(r_t, p + 1)
                    dve.scalar_tensor_tensor(out=kp, in0=ring[:, 1, :], scalar=1.0, in1=kp, op0=ALU.add,
                                             op1=ALU.mult).then_inc(r_k1, 1)
                elif kind == "prep_r":
                    dve.wait_ge(r_k1, p + 1)
                    dve.tensor_tensor(ring[:, 3, :], rp, kp, ALU.mult).then_inc(r_prd, 1)
                    dve.tensor_tensor(ar_f[:, 1, :], rp, ring[:, 0, :], ALU.mult).then_inc(r_feat, 1)
                elif kind == "prep_k":
                    dve.tensor_tensor(bk(slice(1, 3)), by_chunk(kp), by_chunk(ring[:, 2, :]), ALU.mult).then_inc(r_feat, 1)
                    dve.tensor_copy(chunk_decay[:, p % 3, :],
                                    ring[:, 0, :].rearrange("p (n c) -> p n c", c=CH)[:, :, CH - 1]).then_inc(r_feat, 1)
                elif kind == "tok_bk":
                    dve.wait_ge(r_tm, 4 * p + 2)
                    dve.tensor_copy(bk_tok[:, p % 2, 4:8, :], bank[5][:, :]).then_inc(r_tmv, 1)
                elif kind == "pairs":
                    g = seg[2]
                    dve.wait_ge(r_pm, 4 * p + g + 1)
                    dve.tensor_tensor(ar[:, p % 2, g // 2, 4 * (g % 2):4 * (g % 2) + 4, :, :],
                                      bank[PAIR_BANK[g]][:, :].rearrange("p (n a t) -> p n a t", n=4, a=2),
                                      before[:, :, :].unsqueeze(1).broadcast_to((P, 4, 2, CH)), ALU.mult).then_inc(r_pe, 1)
                elif kind == "first":
                    if p:
                        dve.wait_ge(r_wm, 2 * p)
                    else:
                        dve.wait_ge(r_zero, 2)
                    for hd in range(2):
                        half = slice(4 * hd, 4 * hd + 4)
                        dve.wait_ge(r_pe, 4 * p + 2 * hd + 2)
                        even = slice(0, CH)
                        dve.tensor_tensor(inv_t[even, half, even], ar[even, p % 2, hd, 0::2, 0, :],
                                          levels[even, 0, even].unsqueeze(1).broadcast_to((CH, TT, CH)),
                                          ALU.mult).then_inc(r_l0, 1)
                        dve.wait_ge(r_l0, 2 * p + hd + 1)
                        dve.wait_ge(r_m, 12 * p + hd + 1)
                        dve.tensor_tensor(inv_t[:, half, :], inv_t[:, half, :], ident[:, :].unsqueeze(1).broadcast_to((P, 4, P)),
                                          ALU.add).then_inc(r_i0, 1)
                elif kind == "grow":
                    for g in range(2):
                        half = slice(4 * g, 4 * g + 4)
                        dve.wait_ge(r_gm, 8 * p + 2 * (seg[2] - 1) + g + 1)
                        dve.tensor_tensor(inv[:, half, :], inv[:, half, :],
                                          bank[4 + g][:, :].rearrange("p (q t) -> p q t", q=4), ALU.add).then_inc(r_inv, 1)
                elif kind == "turn":
                    dve.wait_ge(r_tt, 8 * p + 2 * seg[2] - 1)
                    dve.tensor_copy(inv_t[:, 0:4, :], bank[4][:, :]).then_inc(r_ttv, 1)
                elif kind == "grow_t":
                    for g in range(2):
                        half = slice(4 * g, 4 * g + 4)
                        dve.wait_ge(r_lm, 2 * p + g + 1)
                        dve.tensor_tensor(inv_t[:, half, :], inv_t[:, half, :],
                                          bank[4 + g][:, :].rearrange("p (q t) -> p q t", q=4), ALU.add).then_inc(r_last, 1)
                elif kind == "wu":
                    if p:
                        dve.wait_ge(r_s2, NC * p)
                    dve.memset(state[:, 0, :], 0.0).then_inc(r_s0, 1)
                elif kind == "step":
                    n = seg[2]
                    c, e, rows = n // 2, n % 2, slice(CH * (n % 2), CH * (n % 2) + CH)
                    dve.wait_ge(r_um, NC * p + n + 1)
                    dve.tensor_tensor(uv[rows, p % 2, e, (c + e) % TT, :], bank[6][rows, 0:P], u0[rows, c, :],
                                      ALU.add).then_inc(r_u, 1)
                elif kind == "out":
                    n = seg[2]
                    dve.wait_ge(r_sm, NC * p + n + 1)
                    dve.tensor_tensor(state_t[:, :], bank[7][:, 0:P], state[:, n % 2, :], ALU.add).then_inc(r_s1, 1)
                    dve.wait_ge(r_s1, NC * p + n + 1)
                    dve.scalar_tensor_tensor(out=state[:, (n + 1) % 2, :], in0=state_t[:, :],
                                             scalar=chunk_decay[:, p % 3, n:n + 1], in1=heads2[:, :], op0=ALU.mult,
                                             op1=ALU.mult).then_inc(r_s2, 1)
            for p in range(KT + 1):
                if p < KT:
                    yp = rkv[:, KT + p, :]
                    dve.wait_ge(r_mean, p + 1)
                    dve.scalar_tensor_tensor(out=yp, in0=bank[p % 2][:, :], scalar=-1.0 / HD, in1=yp, op0=ALU.mult,
                                             op1=ALU.add).then_inc(r_yc, 1)
                if p >= 1:
                    q = p - 1
                    yp = rkv[:, KT + q, :]
                    dve.wait_ge(r_grs, 2 * q + 2)
                    dve.scalar_tensor_tensor(out=yp, in0=yp, scalar=par_b[:, B_LNW + q:B_LNW + q + 1], in1=ring[:, q % 2, :],
                                             op0=ALU.mult, op1=ALU.mult).then_inc(r_yn, 1)
                    dve.wait_ge(r_yn, q + 1)
                    dve.scalar_tensor_tensor(out=yp, in0=yp, scalar=par_b[:, B_LNB + q:B_LNB + q + 1],
                                             in1=rkv[:, 2 * KT + q, :], op0=ALU.add, op1=ALU.add).then_inc(r_z1, 1)
                    dve.wait_ge(r_z1, q + 1)
                    dve.wait_ge(r_gmm, q + 1)
                    dve.tensor_tensor(ring[:, 2 + q % 2, :], yp, bank[4 + q % 2][:, :], ALU.mult).then_inc(r_z2, 1)
                    dve.wait_ge(s_h_hi, H_WO + q + 1)
                    dve.tensor_tensor(h_lo[:, q, :], ring[:, 2 + q % 2, :], h_hi[:, q, :].bitcast(F32),
                                      ALU.subtract).then_inc(s_h, 1)
            square(WO, 1, T_WO, 3)
            norm_split(3, H_FFN1, 1, 3)
            swiglu(1, FI1, FO1, T_FI1)
        dve.wait_ge(s_rstd, LAST + 1)
        for k in range(KT):
            if k >= 4:
                dve.wait_ge(s_y_t, k - 3)
            norm_u(LAST, k, par_b[:, B_NFIN + k:B_NFIN + k + 1])

    @block.tensor
    def _(pe):
        def multiply(base, per, i, j, psum, rhs, tiles=KT, k0=0, first=True, last=True, ready=None):
            pe.wait_ge(s_lo, per * i + (base + j + 1 + RAW))
            for t in range(tiles):
                if ready is not None:
                    pe.wait_ge(ready[0], ready[1] + k0 + t + 1)
                hi, lo = rhs[0](k0 + t), rhs[1](k0 + t)
                for q, (w, r) in enumerate(((w_hi, hi), (w_hi, lo), (w_lo, hi))):
                    mm = pe.matmul(psum[:, :], w[:, j % SPLIT, t, :], r, start=first and t == 0 and q == 0,
                                   stop=last and t == tiles - 1 and q == 2)
            mm.then_inc(s_mm, 1)

        def mod_sum(acc, group):
            pe.wait_ge(s_mod, group)
            for c in range(KT):
                mm = pe.matmul(bank[7][:, c:c + 1], acc[:, c * P:(c + 1) * P], ones[:, 0:1], start=True, stop=True)
            mm.then_inc(s_mod_sum, 1)

        def norm_sum(n):
            pe.wait_ge(s_ssq, KT * (n + 1))
            pe.matmul(bank[7][:, :], ones[:, :], ssq[:, :], start=True, stop=True).then_inc(s_ssum, 1)

        pe.wait_ge(s_const, CONSTS)
        pe.wait_ge(s_rows, 16 * 13)
        pe.transpose(bank[4][:, 0:A_ROWS], rows_a[:, :], ident[0:A_ROWS, 0:A_ROWS])
        pe.transpose(bank[5][:, 0:P], rows_b[:, :], ident[:, :]).then_inc(s_par_t, 1)
        pe.wait_ge(s_x_tok, 16)
        for k in range(KT):
            if k >= 4:
                pe.wait_ge(s_x0, k - 3)
                pe.wait_ge(s_sq, k - 3)
            for t in range(TT):
                mm = pe.transpose(bank[k % 4][:, t * P:(t + 1) * P], x_tok[:, t, k * P:(k + 1) * P], ident[:, :])
            mm.then_inc(s_xt, 1)
        pe.wait_ge(s_mod0, KT)
        for c in range(KT):
            mm = pe.matmul(bank[7][:, c:c + 1], mod_first[:, 0, c * P:(c + 1) * P], ones[:, 0:1], start=True, stop=True)
        mm.then_inc(s_mod_sum, 1)
        pe.wait_ge(s_mod0, 2 * KT)
        mod_sum(mod_first[:, KT, :], 1)
        pe.wait_ge(s_mod, 2)
        norm_sum(0)
        pe.wait_ge(s_wf_lo, 2)
        for k in range(KT):
            pe.wait_ge(s_h, H_MIX0 + k + 1)
            for q, (w, r) in enumerate(((wf_hi, h_hi), (wf_hi, h_lo), (wf_lo, h_hi))):
                mm = pe.matmul(bank[6][:, :], w[:, k, :], r[:, k, :], start=k == 0 and q == 0, stop=k == KT - 1 and q == 2)
        mm.then_inc(s_f, 1)

        def four(base, t0, i, ready=None):
            for j in range(4):
                pe.wait_ge(s_bank, 4 * i + (t0 + j + 1))
                multiply(base, 4, i, j, bank[j], h_of, ready=ready if j == 0 else None)

        with pe.Fori(0, 4) as i:
            four(QKV, T_QKV, i)
            pe.wait_ge(s_mod_used, 8 * i + 10)
            mod_sum(mod_acc, i + 2)
        with pe.Fori(4, 6) as i:
            four(QKV, T_QKV, i)

        pe.wait_ge(s_bank, NB + T_QKV + 24)
        for n in range(8):
            if n >= 2:
                pe.wait_ge(s_v_tok if n % 2 == 0 else s_v_tokv, n // 2)
            for f in range(4):
                mm = pe.transpose(bank[4 + n % 2][:, f * P:(f + 1) * P], qkv[:, 8 + 12 * (n % 2) + f, (n // 2) * P:(n // 2 + 1) * P],
                                  ident[:, :])
            mm.then_inc(s_v_t, 1)
        pe.wait_ge(s_v_tok, 4)
        pe.wait_ge(s_v_tokv, 4)
        pe.wait_ge(s_mod, 6)
        pe.wait_ge(s_fv, 6)
        for h in range(NH + 1):
            if h < NH:
                pair, rows = (h % NFOX) // 2, slice(HD * (h % 2), HD * (h % 2) + HD)
                q0 = pair + 12 * (h // NFOX)
                for qt in range(TT):
                    if h >= 1:
                        pe.wait_ge(s_exp, TT * (h - 1) + qt + 1)
                    cols = slice(qt * P, (qt + 1) * P)
                    psum = score_of(qt)
                    pe.matmul(psum, qkv[rows, q0, cols], qkv[rows, q0 + 4, 0:(qt + 1) * P], start=True, stop=False)
                    if h < NFOX:
                        pe.wait_ge(s_dh, h + 1)
                        pe.matmul(psum, decay_h[:, h % 2, cols], decay_r[:, 0:(qt + 1) * P], start=False, stop=False)
                    pe.matmul(psum[:, qt * P:(qt + 1) * P], ident_b[:, :], causal[:, :], start=False,
                              stop=True).then_inc(s_score, 1)
            if h >= 1:
                g = h - 1
                if g >= 1:
                    pe.wait_ge(s_pt_a, g)
                    pe.wait_ge(s_pt_v, 2 * g)
                for qt in range(TT):
                    pe.wait_ge(s_norm, TT * g + qt + 1)
                    for kt in range(qt + 1):
                        dst = bank[PT_BANK[kt]][:, PT_OFF[kt] + (qt - kt) * P:PT_OFF[kt] + (qt - kt + 1) * P]
                        mm = pe.transpose(dst, prob[:, g % 2, COL[qt] + kt * P:COL[qt] + (kt + 1) * P], ident[:, :])
                mm.then_inc(s_pt, 1)
                pair = g // 2
                if g % 2 == 0 and pair >= 1:
                    pe.wait_ge(s_h, H_ATT + pair)
                pe.wait_ge(s_pt_a, g + 1)
                pe.wait_ge(s_pt_v, 2 * g + 2)
                rows = slice(HD * (g % 2), HD * (g % 2) + HD)
                for kt in range(TT):
                    o = (0, S, S + 384, S + 640)[kt]
                    mm = pe.matmul(bank[7][rows, kt * P:S], v_tok[:, kt, g * HD:(g + 1) * HD],
                                   prob_t[:, g % 2, o:o + S - kt * P], start=kt == 0, stop=kt == TT - 1)
                mm.then_inc(s_pv, 1)

        def square(base, t0, h0):
            with pe.Fori(0, 2) as i:
                four(base, t0, i, ready=(s_h, h0))

        def swiglu(layer, base_in, base_out, t_in, t_out, h0):
            def pairs(i, tiles):
                for j in range(2 * tiles):
                    pe.wait_ge(s_bank, 8 * i + (t_in + j + 1))
                    multiply(base_in, 8, i, j, bank[j % 4], h_of, ready=(s_h, h0) if j == 0 else None)
                if layer == 0:
                    pe.wait_ge(s_mod_used, 8 * i + 42)
                    mod_sum(mod_acc, i + 6)

            with pe.Fori(0, 5) as i:
                pairs(i, 4)
            pairs(5, 2)
            with pe.Fori(0, 2) as i:
                for j in range(4):
                    pe.wait_ge(s_bank, 4 * i + (t_out + j + 1))
                    for c, (k0, kn) in enumerate(OUT_PARTS):
                        multiply(base_out, 12, i, 3 * j + c, bank[j], g_of, kn, k0, c == 0, c == 2,
                                 ready=(s_g, FT * layer) if j == 0 else None)

        square(AO, T_AO, H_ATT)
        norm_sum(1)
        swiglu(0, FI0, FO0, T_FI0, T_FO0, H_FFN0)
        norm_sum(2)
        if LAYERS == 2:
            pe.wait_ge(s_bank, NB + T_RKV)
            pe.wait_ge(r_lora_w, 80)
            for m in range(24):
                k, x_mix = m % KT, ring[:, m % 4, :]
                pe.wait_ge(r_mix, m + 1)
                if m < 8:
                    mm = pe.matmul(bank[0][0:HD, :], w1[:, k, :], x_mix, start=k == 0, stop=k == KT - 1)
                elif m < 16:
                    mm = pe.matmul(bank[1][HD:P, :], a1[:, k, :], x_mix, start=k == 0, stop=k == KT - 1)
                else:
                    pe.matmul(bank[2][:, :], g1[:, k, 0:P], x_mix, start=k == 0, stop=k == KT - 1)
                    mm = pe.matmul(bank[3][0:GL - P, :], g1[:, k, P:GL], x_mix, start=k == 0, stop=k == KT - 1)
                mm.then_inc(r_lora, 1)
            pe.wait_ge(r_mid, 4)
            for n in range(3):
                with pe.Fori(0, 2) as i:
                    four(RKV + 8 * n, T_RKV + 8 * n, i, ready=(s_h, H_R + 8 * n))
            pe.wait_ge(s_bank, NB + T_WO)
            pe.wait_ge(r_mask, MASKS)
            for seg in rwkv_order():
                kind, p = seg[0], seg[1]
                rp, vp = rkv[:, p, :], rkv[:, 2 * KT + p, :]
                blocks = [(hd, c, 4 * hd + c) for hd in range(2) for c in range(TT)]
                if kind == "prep_lora":
                    if p:
                        pe.wait_ge(r_pe, 4 * p)
                        pe.wait_ge(r_brc, p)
                    cols = slice(p * P, (p + 1) * P)
                    pe.matmul(bank[0][:, :], wa2[0:HD, cols], wa_mid[0:HD, :], start=True, stop=True).then_inc(r_lora_mm, 1)
                    pe.matmul(bank[1][:, :], wa2[HD:P, cols], wa_mid[HD:P, :], start=True, stop=True).then_inc(r_lora_mm, 1)
                elif kind == "prep_cum":
                    pe.wait_ge(r_sqk, p + 1)
                    pe.wait_ge(r_sig, 2 * p + 1)
                    pe.matmul(bank[0][:, :], heads2[:, :], ring[:, 3, :], start=True, stop=True).then_inc(r_ss, 1)
                elif kind == "prep_k":
                    pe.wait_ge(r_bwt, p + 1)
                    pe.wait_ge(r_prd, p + 1)
                    pe.matmul(bank[0][:, :], bonus_w[:, :], ring[:, 3, :], start=True, stop=True).then_inc(r_br, 1)
                elif kind == "tok_bk":
                    pe.wait_ge(r_feat, 5 * p + 4)
                    if p:
                        pe.wait_ge(r_last, 2 * p)
                    for g, b in enumerate((4, 5)):
                        for n in range(4):
                            mm = pe.transpose(bank[b][:, n * P:(n + 1) * P],
                                              bk_f[:, 2 * g + n // 2, 2 * (n % 2):2 * (n % 2) + 2, :], ident[:, :])
                        mm.then_inc(r_tm, 1)
                elif kind == "tok_av":
                    if p:
                        pe.wait_ge(r_u0, 2 * p)
                    for c in range(TT):
                        mm = pe.transpose(bank[2][:, c * P:(c + 1) * P], ar_f[:, 0, c * P:(c + 1) * P], ident[:, :])
                    mm.then_inc(r_tm, 1)
                    for c in range(TT):
                        t = (2 * KT + p) * S + c * P - CH
                        pe.transpose(bank[3][:, c * P:(c + 1) * P], rkv_flat[:, t:t + P], ident[:, :])
                    mm = pe.transpose(bank[3][0:CH, 0:P], vp[:, S - CH:S], ident[:, :])
                    mm.then_inc(r_tm, 1)
                elif kind == "pairs":
                    g = seg[2]
                    if g == 0:
                        pe.wait_ge(r_tma, 4 * p + 1)
                    elif g == 1:
                        pe.wait_ge(r_tmv, p + 1)
                    elif g == 2 and p:
                        pe.wait_ge(r_w, p)
                    elif g == 3:
                        pe.wait_ge(r_tma, 4 * p + 2)
                    rows = slice(HD * (g // 2), HD * (g // 2) + HD)
                    for m in range(4):
                        n = 4 * (g % 2) + m
                        mm = pe.matmul(bank[PAIR_BANK[g]][:, m * P:(m + 1) * P],
                                       bk_f[rows, n // 2, 2 * (n % 2):2 * (n % 2) + 2, :],
                                       ar_f[rows, :, n * CH:(n + 1) * CH], start=True, stop=True)
                    mm.then_inc(r_pm, 1)
                elif kind == "intra":
                    e = seg[2]
                    pe.wait_ge(r_pe, 4 * p + 4)
                    if e == 0:
                        pe.wait_ge(r_tma, 4 * p + 4)
                    rows, krows = slice(CH * e, CH * e + CH), slice(CH * (1 - e), CH * (1 - e) + CH)
                    for hd, c, _ in blocks:
                        f = slice(HD * hd, HD * hd + HD)
                        mm = pe.matmul(bank[(3, 5)[e]][rows, c * P + HD * hd:c * P + HD * hd + HD],
                                       ar[krows, p % 2, hd, 2 * c + e, 0, :], uv[krows, p % 2, e, (c + e) % TT, f],
                                       start=True, stop=True)
                    mm.then_inc(r_xm, 1)
                elif kind == "first":
                    for g in range(2):
                        pe.wait_ge(r_i0, 2 * p + g + 1)
                        if g == 1:
                            pe.wait_ge(r_xv, 2 * p + 2)
                        for q in range(4 * g, 4 * g + 4):
                            mm = pe.transpose(bank[4 + g][:, q % 4 * P:(q % 4 + 1) * P], inv_t[:, q, :], ident[:, :])
                        mm.then_inc(r_i0m, 1)
                elif kind == "join":
                    l = seg[2]
                    pe.wait_ge(r_m, 12 * p + 2 * l + 2)
                    for g in range(2):
                        if l == 1:
                            pe.wait_ge(r_i0c, 2 * p + g + 1)
                        else:
                            pe.wait_ge(r_inv, 8 * p + 2 * (l - 2) + g + 1)
                        for q in range(4 * g, 4 * g + 4):
                            mm = pe.matmul(bank[2 + g][:, q % 4 * P:(q % 4 + 1) * P], join_t[:, (p + l) % 2, q, :], inv[:, q, :],
                                           start=True, stop=True)
                        mm.then_inc(r_zm, 1)
                elif kind in ("grow", "grow_t"):
                    l = seg[2]
                    for g in range(2):
                        pe.wait_ge(r_zb, 2 * (5 * p + l - 1) + g + 1)
                        if l > 1:
                            pe.wait_ge((r_ttv, r_tta)[g], 4 * p + l - 1)
                        for q in range(4 * g, 4 * g + 4):
                            left, right = (inv_t, prod) if l < 5 else (prod, inv_t)
                            mm = pe.matmul(bank[4 + g][:, q % 4 * P:(q % 4 + 1) * P], left[:, q, :], right[:, q, :],
                                           start=True, stop=True)
                        mm.then_inc(r_gm if l < 5 else r_lm, 1)
                elif kind == "turn":
                    for g in range(2):
                        pe.wait_ge(r_inv, 8 * p + 2 * (seg[2] - 1) + g + 1)
                        for q in range(4 * g, 4 * g + 4):
                            mm = pe.transpose(bank[4 + g][:, q % 4 * P:(q % 4 + 1) * P], inv[:, q, :], ident[:, :])
                        mm.then_inc(r_tt, 1)
                elif kind == "wu":
                    pe.wait_ge(r_xv, 2 * p + 2)
                    for hd in range(2):
                        pe.wait_ge(r_last, 2 * p + hd + 1)
                        for c in range(TT):
                            mm = pe.matmul(bank[2 + hd][:, c * P:(c + 1) * P], inv_t[:, 4 * hd + c, :],
                                           ax_tok[:, c, :, HD * hd:HD * hd + HD], start=True, stop=True)
                        mm.then_inc(r_wm, 1)
                elif kind == "w_back":
                    pe.wait_ge(r_wt, 2 * p + 2)
                    for c in range(TT):
                        mm = pe.transpose(bank[1][:, c * P:(c + 1) * P], w_tok[:, c, :], ident[:, :])
                    mm.then_inc(r_wtm, 1)
                elif kind == "step":
                    n = seg[2]
                    at_, rows = NC * p + n, slice(CH * (n % 2), CH * (n % 2) + CH)
                    if n == 0:
                        pe.wait_ge(r_s0, p + 1)
                        pe.wait_ge(r_w, p + 1)
                        pe.wait_ge(r_u0, 2 * p + 2)
                    if at_:
                        pe.wait_ge(r_s2, at_)
                        pe.wait_ge(r_y, at_)
                    pe.matmul(bank[6][rows, 0:P], w_f[:, n * CH:(n + 1) * CH], state[:, n % 2, :], start=True,
                              stop=True).then_inc(r_um, 1)
                elif kind == "out":
                    n = seg[2]
                    c, e, toks = n // 2, n % 2, slice(n * CH, (n + 1) * CH)
                    pe.wait_ge(r_u, NC * p + n + 1)
                    pe.matmul(bank[7][:, 0:P], bk_tok[:, p % 2, n, :], uv[:, p % 2, e, (c + e) % TT, :], start=True,
                              stop=True).then_inc(r_sm, 1)
                    pe.wait_ge(r_rt, p + 1)
                    y = bank[6][:, 256:256 + CH]
                    pe.matmul(y, state[:, n % 2, :], rp[:, toks], start=True, stop=False)
                    for hd in range(2):
                        f = slice(HD * hd, HD * hd + HD)
                        mm = pe.matmul(y[f, :], uv[:, p % 2, e, (c + e) % TT, f], ar[:, p % 2, hd, n, 1, :], start=False, stop=True)
                    mm.then_inc(r_ym, 1)
            pe.wait_ge(r_g2, 32)
            pe.wait_ge(r_y, NC * KT)
            for p in range(KT + 1):
                if p < KT:
                    if p >= 2:
                        pe.wait_ge(r_z2, p - 1)
                    pe.matmul(bank[p % 2][:, :], heads2[:, :], rkv[:, KT + p, :], start=True, stop=True).then_inc(r_mean, 1)
                    pe.matmul(bank[4 + p % 2][:, :], g2[:, 0, p * P:(p + 1) * P], g_mid[:, 0, :], start=True, stop=False)
                    pe.matmul(bank[4 + p % 2][:, :], g2[0:GL - P, 1, p * P:(p + 1) * P], g_mid[0:GL - P, 1, :], start=False,
                              stop=True).then_inc(r_gmm, 1)
                    pe.wait_ge(r_ysq, p + 1)
                    pe.matmul(bank[2 + p % 2][:, :], heads2[:, :], ring[:, p % 2, :], start=True, stop=True).then_inc(r_var, 1)
            square(WO, T_WO, H_WO)
            norm_sum(3)
            swiglu(1, FI1, FO1, T_FI1, T_FO1, H_FFN1)
            norm_sum(4)
        for k in range(KT):
            pe.wait_ge(s_u, KT * LAST + k + 1)
            if k >= 4:
                pe.wait_ge(s_y, k - 3)
            for t in range(TT):
                mm = pe.transpose(bank[k % 4][:, t * P:(t + 1) * P], ring[:, k % 4, t * P:(t + 1) * P], ident[:, :])
            mm.then_inc(s_y_t, 1)


_INS = ["x", "c", "attn_w_in", "attn_b_f", "attn_w_out", "rwkv_mu", "rwkv_w_r", "rwkv_w_k", "rwkv_w_v", "rwkv_w_o",
        "rwkv_w0", "rwkv_w1", "rwkv_w2", "rwkv_a0", "rwkv_a1", "rwkv_a2", "rwkv_g1", "rwkv_g2", "rwkv_k_k", "rwkv_k_a",
        "rwkv_r_k", "rwkv_ln_w", "rwkv_ln_b", "mod_w", "mod_b", "norm_mix", "norm_ffn", "ffn_w_in", "ffn_w_out",
        "norm_final"]


def kernel(**inputs):
    import numpy as np
    import concourse.bacc as bacc
    from concourse.bass_utils import run_bass_kernel_spmd

    nc = bacc.Bacc("TRN2", target_bir_lowering=False, num_devices=1)
    arrays, aps = {}, {}
    for name in _INS:
        arr = np.ascontiguousarray(inputs[name])
        arrays[f"in_{name}"] = arr
        aps[name] = nc.dram_tensor(f"in_{name}", arr.shape, mybir.dt.from_np(arr.dtype), kind="ExternalInput").ap()
    out = nc.dram_tensor("out", (1, S, D), F32, kind="ExternalOutput").ap()
    build(nc, aps, out)
    return run_bass_kernel_spmd(nc, [arrays], core_ids=[0]).results[0]["out"]
```

```python
from contextlib import ExitStack

import concourse.bass as bass
from concourse import mybir

F32 = mybir.dt.float32
F32R = mybir.dt.float32r
BF16 = mybir.dt.bfloat16
ALU = mybir.AluOpType
ACT = mybir.ActivationFunctionType
AX_X = mybir.AxisListType.X

P = 128
S = 512
D = 1024
KT = D // P
TT = S // P
HD = 64
NH = 16
NFOX = 8
FF = 2816
FT = FF // P
EPS = 1e-6
GN_EPS = HD * 1e-5
NEG = -1e30
DECAY = -0.6065306597126334
CH = 64
NC = S // CH
GL = 160
LOG_NORM = 6.931471805599453
RAW = 4
SPLIT = 2
NB = 4
OUT_PARTS = ((0, 8), (8, 7), (15, 7))

QKV, AO, FI0, FO0, RKV, WO, FI1, FO1, CHUNKS = 0, 24, 32, 76, 100, 124, 132, 176, 200
T_QKV, T_AO, T_FI0, T_FO0, T_RKV, T_WO, T_FI1, T_FO1 = 0, 24, 32, 76, 84, 108, 116, 160

H_MIX0, H_ATT, H_FFN0, H_R, H_K, H_V, H_WO, H_FFN1 = 0, 8, 16, 24, 32, 40, 48, 56
LAYERS = 2
LAST = 2 * LAYERS
CONSTS = 24
MASKS = 37
COL = (0, 128, 384, 768, 1280)
PT_BANK = (4, 5, 6, 6)
PT_OFF = (0, 0, 0, 256)

A_C, A_MODB, A_NMIX = 0, 8, 104
A_ROWS = 120
B_NFFN, B_NFIN, B_MU, B_W0, B_A0, B_KK, B_KA, B_RK, B_LNW, B_LNB = 0, 16, 24, 72, 80, 88, 96, 104, 112, 120

PAIR_BANK = (4, 5, 1, 2)
PREP = ("prep_lora", "prep_sig", "prep_cum", "prep_prev", "prep_ln", "prep_norm", "prep_decay", "prep_key", "prep_a",
        "prep_b", "prep_r", "prep_k")
GN = ("gn_mean", "gn_center", "gn_sq", "gn_var", "gn_ln", "gn_exp", "gn_norm", "gn_bonus", "gn_gate")


def rwkv_order():
    for part in PREP:
        yield (part, 0)
    for p in range(KT + 2):
        more = {"C": iter([(kind, p - 1, n) for n in range(NC) for kind in ("step", "out")] if 0 < p <= KT else []),
                "P": iter([(part, p + 1) for part in PREP] if p + 1 < KT else []),
                "G": iter([(part, p - 2) for part in GN] if p >= 2 else [])}
        if p < KT:
            own = [(("tok_bk", p), ""), (("w_back", p - 1), ""), (("tok_av", p), ""), (("prep_bonus", p), ""),
                   (("pairs", p, 0), ""), (("pairs", p, 1), ""), (("pairs", p, 2), "C"), (("pairs", p, 3), "C"),
                   (("intra", p, 0), "C"), (("intra", p, 1), "CP"), (("first", p), "CP"),
                   (("join", p, 1), "CPG"), (("grow", p, 1), "CPG"),
                   (("join", p, 2), "G"), (("turn", p, 1), "CGPG"), (("grow", p, 2), "CPG"),
                   (("join", p, 3), ""), (("turn", p, 2), "CPG"), (("grow", p, 3), "CP"),
                   (("join", p, 4), ""), (("turn", p, 3), "CPG"), (("grow", p, 4), "CP"),
                   (("join", p, 5), ""), (("turn", p, 4), "CPG"), (("grow_t", p, 5), "CCP"), (("wu", p), "")]
        else:
            own = [(("w_back", p - 1) if p == KT else None, "CCCCCCCG" + "CG" * 9)]
        for seg, letters in own:
            if seg and seg[1] >= 0:
                yield seg
            for letter in letters:
                yield from (s for s in [next(more[letter], None)] if s)


def build(nc, a, out):
    with ExitStack() as ctx:
        program(nc, a, out, ctx)


def program(nc, a, out, ctx):
    def sb(name, shape, dt=F32, scope=ctx):
        return scope.enter_context(nc.sbuf_tensor(name, shape, dt))

    def sem(name):
        return ctx.enter_context(nc.semaphore(name))

    bank = [ctx.enter_context(nc.psum_tensor(f"bank{i}", [P, S], F32)) for i in range(8)]

    x = sb("x", [P, KT, S])
    raw = sb("raw", [P, RAW, KT, P])
    w_hi = sb("w_hi", [P, SPLIT, KT, P], F32R)
    w_lo = sb("w_lo", [P, SPLIT, KT, P], F32R)
    ident = sb("ident", [P, P])
    ident_b = sb("ident_b", [P, P], BF16)
    causal = sb("causal", [P, P], BF16)
    ones = sb("ones", [P, P])
    cst = sb("cst", [P, 8])
    par_a = sb("par_a", [P, A_ROWS])
    par_b = sb("par_b", [P, P])
    rows_a = sb("rows_a", [A_ROWS, P])
    rows_b = sb("rows_b", [P, P])
    cond = sb("cond", [P, KT])
    mod_t = sb("mod_t", [P, 2, 6 * KT])
    gain = sb("gain", [P, 4, KT])
    fox_sel = sb("fox_sel", [P, NFOX])
    qkv_scale = sb("qkv_scale", [P, 24])
    ring = sb("ring", [P, 4, S])
    ssq = sb("ssq", [P, S])
    rstd = sb("rstd", [P, S])
    h_scope = ExitStack()
    h_hi = sb("h_hi", [P, KT, S], F32R, h_scope)
    h_lo = sb("h_lo", [P, KT, S], F32R, h_scope)
    mod_scope = ExitStack()
    mod_raw = sb("mod_raw", [P, 2, D], F32, mod_scope)
    mod_acc = sb("mod_acc", [P, D], F32, mod_scope)
    with ExitStack() as s0:
        x_tok = sb("x_tok", [P, TT, D], F32, s0)
        mod_first = sb("mod_first", [P, 2 * KT, D], F32, s0)
    with ExitStack() as s1:
        qkv = sb("qkv", [P, 24, S], F32, s1)
        prob = sb("prob", [P, 2, 1280], F32, s1)
        prob_t = sb("prob_t", [P, 2, 1280], F32, s1)
        q_dec = sb("q_dec", [P, 2, S], F32, s1)
        k_dec = sb("k_dec", [P, 2, S], F32, s1)
        row_stat = sb("row_stat", [P, 2, 3, TT], F32, s1)
        with ExitStack() as s2:
            v_tok = sb("v_tok", [P, TT, D], F32, s2)
        with ExitStack() as s2:
            sb("start_up_tiles", [P, 2048], F32, s2)
            wf_raw = sb("wf_raw", [P, KT, NFOX], F32, s2)
            wf_hi = sb("wf_hi", [P, KT, P], F32R, s2)
            wf_lo = sb("wf_lo", [P, KT, P], F32R, s2)
            decay_l = sb("decay_l", [P, S], F32, s2)
            decay_r = sb("decay_r", [P, S], F32, s2)
            b_f = sb("b_f", [P, 1], F32, s2)
    with ExitStack() as s1:
        y_tok = sb("y_tok", [P, TT, D], F32, s1)
    with ExitStack() as s1:
        g_hi = sb("g_hi", [P, FT, S], F32R, s1)
        g_lo = sb("g_lo", [P, FT, S], F32R, s1)
    mod_scope.close()
    rw_scope = ExitStack()
    rkv = sb("rkv", [P, 3 * KT, S], F32, rw_scope)
    wa_mid = sb("wa_mid", [P, S], F32, rw_scope)
    g_mid = sb("g_mid", [P, 2, S], F32, rw_scope)
    wa2 = sb("wa2", [P, D], F32, rw_scope)
    levels = sb("levels", [P, 6, P], F32, rw_scope)
    before = sb("before", [P, 2, CH], F32, rw_scope)
    heads2 = sb("heads2", [P, P], F32, rw_scope)
    restart = sb("restart", [P, S], F32, rw_scope)
    with ExitStack() as s1:
        h_f = sb("h_f", [P, KT, S + 4], F32, s1)
        xx = sb("xx", [P, KT, S], F32, s1)
        w1 = sb("w1", [P, KT, HD], F32, s1)
        a1 = sb("a1", [P, KT, HD], F32, s1)
        g1 = sb("g1", [P, KT, GL], F32, s1)
    rkv_flat = rkv[:, :, :].rearrange("p k s -> p (k s)")
    with ExitStack() as s1:
        ax_tok = sb("ax_tok", [P, TT, 2, P], F32, s1)
        w_tok = sb("w_tok", [P, TT, P], F32, s1)
        bk_f = sb("bk_f", [P, TT, 4, CH], F32, s1)
        ar_f = sb("ar_f", [P, 2, S], F32, s1)
        bk_tok = sb("bk_tok", [P, 2, NC, P], F32, s1)
        uv = sb("uv", [P, 2, 2, TT, P], F32, s1)
        u0 = sb("u0", [P, TT, P], F32, s1)
        w_f = sb("w_f", [P, S], F32, s1)
        inv = sb("inv", [P, 8, P], F32, s1)
        key = sb("key", [P, S], F32, s1)
        state = sb("state", [P, 2, P], F32, s1)
        state_t = sb("state_t", [P, P], F32, s1)
        bonus_w = sb("bonus_w", [P, P], F32, s1)
        bonus = sb("bonus", [P, S], F32, s1)
        chunk_decay = sb("chunk_decay", [P, 3, NC], F32, s1)
    rw_scope.close()
    h_scope.close()
    with ExitStack() as s1:
        ar = sb("ar", [P, 2, 2, NC, 2, CH], F32, s1)
        inv_t = sb("inv_t", [P, 8, P], F32, s1)
        prod = sb("prod", [P, 8, P], F32, s1)
        join_t = sb("join_t", [P, 2, 8, P], F32, s1)

    s_rows_a = sem("s_rows_a")
    s_rows_b = sem("s_rows_b")
    s_x_tok = sem("s_x_tok")
    s_mod_first = [sem(f"s_mod_first{i}") for i in range(8)]
    s_wf = sem("s_wf")
    s_raw = [sem(f"s_raw{i}") for i in range(RAW)]
    s_mod_raw = [sem(f"s_mod_raw{i}") for i in range(2)]
    s_hi = sem("s_hi")
    s_lo = sem("s_lo")
    s_mm = sem("s_mm")
    s_bank = sem("s_bank")
    s_const = sem("s_const")
    s_par_t = sem("s_par_t")
    s_par = sem("s_par")
    s_cond = sem("s_cond")
    s_xt = sem("s_xt")
    s_x0 = sem("s_x0")
    s_mod_used = sem("s_mod_used")
    s_mod0 = sem("s_mod0")
    s_mod_sum = sem("s_mod_sum")
    s_mod = sem("s_mod")
    s_gain = sem("s_gain")
    s_sq = sem("s_sq")
    s_ssq = sem("s_ssq")
    s_ssq0 = sem("s_ssq0")
    s_ssum = sem("s_ssum")
    s_ln = sem("s_ln")
    s_rstd = sem("s_rstd")
    s_u = sem("s_u")
    s_h_hi = sem("s_h_hi")
    s_h = sem("s_h")
    s_v_t = sem("s_v_t")
    s_v_tok = sem("s_v_tok")
    s_v_tokv = sem("s_v_tokv")
    s_wf_split = sem("s_wf_split")
    s_f = sem("s_f")
    s_fa = sem("s_fa")
    s_fv = sem("s_fv")
    s_fv0 = sem("s_fv0")
    s_wf_lo = sem("s_wf_lo")
    s_dh = sem("s_dh")
    s_qk = sem("s_qk")
    s_score = sem("s_score")
    s_max = sem("s_max")
    s_exp = sem("s_exp")
    s_rinv = sem("s_rinv")
    s_norm = sem("s_norm")
    s_pt = sem("s_pt")
    s_pt_a = sem("s_pt_a")
    s_pt_v = sem("s_pt_v")
    s_pv = sem("s_pv")
    s_silu = sem("s_silu")
    s_g_hi = sem("s_g_hi")
    s_g = sem("s_g")
    s_y_t = sem("s_y_t")
    s_y = sem("s_y")
    s_out = sem("s_out")

    r_lora_w = sem("r_lora_w")
    r_wa2 = sem("r_wa2")
    r_mix = sem("r_mix")
    r_lora = sem("r_lora")
    r_mid = sem("r_mid")
    r_hf = sem("r_hf")
    r_xx = sem("r_xx")
    r_xxv = sem("r_xxv")
    r_hf0 = sem("r_hf0")
    r_mask = sem("r_mask")
    r_zero = sem("r_zero")
    r_lora_mm = sem("r_lora_mm")
    r_sig = sem("r_sig")
    r_cum = sem("r_cum")
    r_cprev = sem("r_cprev")
    r_sqk = sem("r_sqk")
    r_ss = sem("r_ss")
    r_ssm = sem("r_ssm")
    r_rn = sem("r_rn")
    r_dec = sem("r_dec")
    r_kk = sem("r_kk")
    r_b = sem("r_b")
    r_t = sem("r_t")
    r_k1 = sem("r_k1")
    r_prd = sem("r_prd")
    r_bwt = sem("r_bwt")
    r_feat = sem("r_feat")
    r_rt = sem("r_rt")
    r_br = sem("r_br")
    r_brc = sem("r_brc")
    r_bon = sem("r_bon")
    r_tm = sem("r_tm")
    r_tma = sem("r_tma")
    r_tmv = sem("r_tmv")
    r_pm = sem("r_pm")
    r_pe = sem("r_pe")
    r_xm = sem("r_xm")
    r_xv = sem("r_xv")
    r_m = sem("r_m")
    r_l0 = sem("r_l0")
    r_i0 = sem("r_i0")
    r_i0m = sem("r_i0m")
    r_i0c = sem("r_i0c")
    r_zm = sem("r_zm")
    r_zb = sem("r_zb")
    r_gm = sem("r_gm")
    r_inv = sem("r_inv")
    r_tt = sem("r_tt")
    r_tta = sem("r_tta")
    r_ttv = sem("r_ttv")
    r_lm = sem("r_lm")
    r_last = sem("r_last")
    r_wm = sem("r_wm")
    r_wt = sem("r_wt")
    r_wtm = sem("r_wtm")
    r_w = sem("r_w")
    r_u0 = sem("r_u0")
    r_s0 = sem("r_s0")
    r_um = sem("r_um")
    r_u = sem("r_u")
    r_sm = sem("r_sm")
    r_s1 = sem("r_s1")
    r_s2 = sem("r_s2")
    r_ym = sem("r_ym")
    r_y = sem("r_y")
    r_mean = sem("r_mean")
    r_yc = sem("r_yc")
    r_ysq = sem("r_ysq")
    r_var = sem("r_var")
    r_gmm = sem("r_gmm")
    r_grs = sem("r_grs")
    r_yn = sem("r_yn")
    r_z1 = sem("r_z1")
    r_z2 = sem("r_z2")
    r_g2 = sem("r_g2")

    w_rkv = [a[f"rwkv_w_{n}"][0].rearrange("(k p) n -> p k n", p=P) for n in "rkv"]
    w_wo = a["rwkv_w_o"][0].rearrange("(k p) n -> p k n", p=P)
    w_in = a["attn_w_in"][0].rearrange("(k p) n -> p k n", p=P)
    w_ao = a["attn_w_out"][0].rearrange("(k p) n -> p k n", p=P)
    w_fi = [a["ffn_w_in"][l].rearrange("(k p) n -> p k n", p=P) for l in range(2)]
    w_fo = [a["ffn_w_out"][l].rearrange("(k p) n -> p k n", p=P) for l in range(2)]
    w_mod = [a["mod_w"][l].rearrange("(k p) n -> p k n", p=P) for l in range(2)]
    x_dram = a["x"][0].rearrange("(t p) d -> p t d", p=P)
    out_dram = out[0].rearrange("(t p) d -> p t d", p=P)

    score_of = lambda qt: bank[qt][:, 0:(qt + 1) * P]
    h_of = (lambda k: h_hi[:, k, :], lambda k: h_lo[:, k, :])
    g_of = (lambda k: g_hi[:, k, :], lambda k: g_lo[:, k, :])


    block = ctx.enter_context(nc.Block())

    @block.sync
    def _(sp):
        def load(base, per, i, j, src, tiles=KT):
            sp.wait_ge(s_lo, per * i + (base + j + 1))
            sp.dma_start(raw[:, j % RAW, 0:tiles, :], src).then_inc(s_raw[j % RAW], 16)

        def load_mod(layer, i, k, v):
            sp.wait_ge(s_mod_used, KT * i + (k + 1))
            sp.dma_start(mod_raw[:, k % 2, :], w_mod[layer][:, k, bass.ts(v, D)]).then_inc(s_mod_raw[k % 2], 16)

        sp.dma_start(x_tok[:, :, :], x_dram).then_inc(s_x_tok, 16)
        sp.wait_ge(s_rows_a, 16 * 3)
        for n in range(8):
            v, k = n // 4, 2 * (n % 4)
            sp.dma_start(mod_first[:, 2 * n:2 * n + 2, :],
                         w_mod[0][:, k:k + 2, v * D:(v + 1) * D]).then_inc(s_mod_first[n], 16)

        def four(base, i, w):
            for j in range(4):
                load(base, 4, i, j, w[:, :, bass.ts(i * 4 + j, P)])

        with sp.Fori(0, 3) as i:
            for j in range(8):
                load(QKV, 8, i, j, w_in[:, :, bass.ts(i * 8 + j, P)])
                load_mod(0, i, j, i + 2)

        def swiglu(layer, base_in, base_out):
            def weights(i, j):
                for half in range(2):
                    load(base_in, 8, i, 2 * j + half, w_fi[layer][:, :, bass.ds((i * 4 + j + FT * half) * P, P)])

            with sp.Fori(0, 5) as i:
                for j in range(4):
                    weights(i, j)
                    if layer == 0:
                        load_mod(1, i + 4, 2 * j, i)
                        load_mod(1, i + 4, 2 * j + 1, i)
            weights(5, 0)
            weights(5, 1)
            if layer == 0:
                for k in range(KT):
                    load_mod(1, 9, k, 5)
            with sp.Fori(0, 2) as i:
                for j in range(4):
                    for c, (k0, kn) in enumerate(OUT_PARTS):
                        load(base_out, 12, i, 3 * j + c, w_fo[layer][:, k0:k0 + kn, bass.ts(i * 4 + j, P)], kn)

        four(AO, 0, w_ao)
        for k in range(KT):
            load_mod(0, 3, k, 5)
            if k % 2:
                load(AO, 4, 1, k // 2, w_ao[:, :, (4 + k // 2) * P:(5 + k // 2) * P])
        swiglu(0, FI0, FO0)
        if LAYERS == 2:
            four(RKV, 0, w_rkv[0])
            sp.wait_ge(s_mm, SPLIT + RKV)
            sp.dma_start(w1[:, :, :], a["rwkv_w1"][0].rearrange("(k p) n -> p k n", p=P)).then_inc(r_lora_w, 16)
            sp.dma_start(a1[:, :, :], a["rwkv_a1"][0].rearrange("(k p) n -> p k n", p=P)).then_inc(r_lora_w, 16)
            sp.dma_start(g1[:, :, :], a["rwkv_g1"][0].rearrange("(k p) n -> p k n", p=P)).then_inc(r_lora_w, 16)
            sp.dma_start(wa2[0:HD, :], a["rwkv_w2"][0]).then_inc(r_wa2, 16)
            sp.dma_start(wa2[HD:P, :], a["rwkv_a2"][0]).then_inc(r_wa2, 16)
            four(RKV, 1, w_rkv[0])
            for n in (1, 2):
                with sp.Fori(0, 2) as i:
                    four(RKV + 8 * n, i, w_rkv[n])
            sp.wait_ge(s_lo, WO + RAW)
            sp.dma_start(raw[:, 2, :, :], a["rwkv_g2"][0, 0:P, :].rearrange("r (k n) -> r k n", n=P)).then_inc(r_g2, 16)
            sp.dma_start(raw[0:GL - P, 3, :, :], a["rwkv_g2"][0, P:GL, :].rearrange("r (k n) -> r k n", n=P)).then_inc(r_g2, 16)
            for j in range(4):
                if j == 2:
                    sp.wait_ge(r_gmm, KT)
                load(WO, 4, 0, j, w_wo[:, :, j * P:(j + 1) * P])
            four(WO, 1, w_wo)
            swiglu(1, FI1, FO1)
        for part in range(4):
            sp.wait_ge(s_y, 2 * part + 2)
            cols = slice(part * D // 4, (part + 1) * D // 4)
            sp.dma_start(out_dram[:, :, cols], y_tok[:, :, cols]).then_inc(s_out, 16)
        sp.wait_ge(s_out, 64)

    @block.gpsimd
    def _(pool):
        const = [0]

        def step(ins):
            const[0] += 1
            ins.then_inc(s_const, 1)
            pool.wait_ge(s_const, const[0])

        step(pool.memset(ident[:, :], 0.0))
        step(pool.affine_select(out=ident[:, :], in_=ident[:, :], pattern=[[-1, P]], compare_op=ALU.not_equal,
                                fill=1.0, base=0, channel_multiplier=1))
        step(pool.memset(ones[:, :], 1.0))
        step(pool.tensor_copy(ident_b[:, :], ident[:, :]))
        step(pool.memset(causal[:, :], 0.0))
        step(pool.affine_select(out=causal[:, :], in_=causal[:, :], pattern=[[-1, P]], compare_op=ALU.is_ge,
                                fill=NEG, base=0, channel_multiplier=1))
        step(pool.memset(cst[:, 0:1], EPS))
        step(pool.memset(cst[:, 1:2], 1.0))
        step(pool.memset(cst[:, 2:3], GN_EPS))
        step(pool.memset(cst[:, 3:4], LOG_NORM))
        step(pool.memset(qkv_scale[:, :], 1.0))
        step(pool.memset(qkv_scale[:, 0:4], HD ** -0.5))
        step(pool.memset(qkv_scale[:, 12:16], HD ** -0.5))
        step(pool.memset(wf_hi[:, :, :].bitcast(F32), 0.0))
        step(pool.memset(wf_lo[:, :, :].bitcast(F32), 0.0))
        step(pool.memset(fox_sel[:, :], 0.0))
        for row in (0, 32, 64, 96):
            step(pool.affine_select(out=fox_sel[:, :], in_=fox_sel[:, :], pattern=[[-1, NFOX]],
                                    compare_op=ALU.not_equal, fill=1.0, base=-row, channel_multiplier=1))
        step(pool.memset(decay_l[:, :], 0.0))
        step(pool.memset(decay_l[0:NFOX, :], -1.0))
        step(pool.memset(decay_l[HD:HD + NFOX, :], -1.0))
        step(pool.memset(b_f[:, :], 0.0))
        pool.memset(cst[:, 4:5], 0.0).then_inc(s_lo, RAW)
        pool.memset(cst[:, 5:6], 0.0).then_inc(s_mm, SPLIT)
        pool.memset(cst[:, 6:7], 0.0).then_inc(s_bank, NB)
        pool.memset(cst[:, 7:8], 0.0).then_inc(s_mod_used, 2)
        assert const[0] == CONSTS

        def low_part(i, j):
            pool.wait_ge(s_hi, 4 * i + (j + 1))
            pool.tensor_tensor(w_lo[:, j % SPLIT, :, :], raw[:, j % RAW, :, :],
                               w_hi[:, j % SPLIT, :, :].bitcast(F32), ALU.subtract).then_inc(s_lo, 1)

        def low_parts(lo, hi):
            with pool.Fori(lo // 4, hi // 4) as i:
                for j in range(4):
                    low_part(i, j)

        low_parts(0, AO)
        pool.wait_ge(s_bank, NB + T_QKV + 24)
        for h in range(NFOX):
            rows, pair = slice(HD * (h % 2), HD * (h % 2) + HD), h // 2
            if h >= 2:
                pool.wait_ge(s_score, TT * (h - 1))
            for n, tile in enumerate((q_dec, k_dec)):
                pool.tensor_copy(tile[rows, h % 2, :], qkv[rows, pair + 4 * n, :]).then_inc(s_qk, 1)
                pool.wait_ge(s_qk, 2 * h + n + 1)
        low_parts(AO, RKV)
        if LAYERS == 2:
            low_part(RKV // 4, 0)
            low_part(RKV // 4, 1)
            pool.wait_ge(s_mm, SPLIT + RKV)
            pool.wait_ge(r_hf0, 1)
            for k in range(0, KT, 2):
                pool.wait_ge(r_hf, k + 1)
                pool.tensor_tensor(xx[:, k, :], h_f[:, k, 3:3 + S], h_f[:, k, 4:4 + S], ALU.subtract).then_inc(r_xx, 1)
            mask = [0]

            def mstep(ins):
                mask[0] += 1
                ins.then_inc(r_mask, 1)
                pool.wait_ge(r_mask, mask[0])

            def blocks(dst, size):
                v = dst.rearrange("p (n b) -> p n b", b=size)
                mstep(pool.affine_select(out=v, in_=v, pattern=[[-size, P // size], [0, size]], compare_op=ALU.is_ge,
                                         fill=0.0, base=0, channel_multiplier=1))
                mstep(pool.affine_select(out=v, in_=v, pattern=[[size, P // size], [0, size]], compare_op=ALU.is_ge,
                                         fill=0.0, base=size - 1, channel_multiplier=-1))

            mstep(pool.memset(levels[:, :, :], 1.0))
            mstep(pool.memset(join_t[:, 0, 0:2, :], 1.0))
            mstep(pool.memset(heads2[:, :], 1.0))
            mstep(pool.memset(restart[:, :], 1.0))
            mstep(pool.memset(restart[:, :].rearrange("p (n c) -> p n c", c=CH)[:, :, 0:1], 0.0))
            for l in range(6):
                blocks(levels[:, l, :], 2 << l)
            blocks(heads2[:, :], HD)
            for l in range(5, 0, -1):
                mstep(pool.tensor_tensor(levels[:, l, :], levels[:, l, :], levels[:, l - 1, :], ALU.subtract))
            for l in range(6):
                mstep(pool.affine_select(out=levels[:, l, :], in_=levels[:, l, :], pattern=[[1, P]], compare_op=ALU.is_gt,
                                         fill=0.0, base=0, channel_multiplier=-1))
            for q, op in enumerate((ALU.is_gt, ALU.is_ge)):
                blocks(join_t[:, 0, q, :], CH)
                mstep(pool.affine_select(out=join_t[:, 0, q, :], in_=join_t[:, 0, q, :], pattern=[[1, P]], compare_op=op,
                                         fill=0.0, base=0, channel_multiplier=-1))
            mstep(pool.tensor_tensor(before[:, :, :], join_t[:, 0, 0:2, 0:CH], join_t[:, 0, 0:2, CH:P], ALU.add))
            assert mask[0] == MASKS
            low_part(RKV // 4, 2)
            low_part(RKV // 4, 3)
            low_parts(RKV + 4, WO)
            pool.wait_ge(s_mm, SPLIT + WO)
            pool.memset(inv_t[:, :, :], 0.0).then_inc(r_zero, 1)
            pool.memset(join_t[:, :, :, :], 0.0).then_inc(r_zero, 1)
            pool.wait_ge(r_zero, 2)
            for seg in rwkv_order():
                kind, p = seg[0], seg[1]

                def level_part(l, e, src, dst):
                    rows = slice(CH * e, CH * e + CH)
                    n = dst.shape[1] // TT
                    pool.tensor_tensor(dst[rows, :, rows].rearrange("s (h c) t -> s h c t", h=n), src[rows, :, e::2, 0, :],
                                       levels[rows, l, rows].unsqueeze(1).unsqueeze(1).broadcast_to((CH, n, TT, CH)),
                                       ALU.mult).then_inc(r_m, 1)

                if kind == "prep_prev":
                    pool.wait_ge(r_cum, p + 1)
                    pool.tensor_tensor(rstd[:, :], ring[:, 2, :], ring[:, 0, :], ALU.subtract).then_inc(r_cprev, 1)
                    pool.wait_ge(r_cprev, p + 1)
                elif kind == "prep_a":
                    pool.wait_ge(r_kk, p + 1)
                    pool.tensor_tensor(ssq[:, :], key[:, :], ring[:, 1, :], ALU.mult).then_inc(r_b, 1)
                    pool.wait_ge(r_b, p + 1)
                elif kind == "prep_k":
                    pool.wait_ge(r_feat, 5 * p + 3)
                    pool.tensor_copy(rkv[:, p, :], ar_f[:, 1, :]).then_inc(r_rt, 1)
                    pool.wait_ge(r_rt, p + 1)
                elif kind == "first":
                    for hd in range(2):
                        pool.wait_ge(r_pe, 4 * p + 2 * hd + 2)
                        if p and hd == 0:
                            pool.wait_ge(r_wm, 2 * p)
                        level_part(0, 1, ar[:, p % 2, hd:hd + 1, :, :, :], inv_t[:, 4 * hd:4 * hd + 4, :])
                        pool.wait_ge(r_m, 12 * p + hd + 1)
                if kind == "first" or kind == "join" and seg[2] < 5:
                    l = seg[2] + 1 if kind == "join" else 1
                    if 5 * p + l > 2:
                        pool.wait_ge(r_zm, 10 * p + 2 * (l - 2))
                    for e in range(2):
                        level_part(l, e, ar[:, p % 2, :, :, :, :], join_t[:, (p + l) % 2, :, :])
                        pool.wait_ge(r_m, 12 * p + 2 * l + e + 1)
                    if l == 2:
                        pool.wait_ge(r_brc, p + 1)
                        pool.wait_ge(r_tm, 4 * p + 4)
                        pool.tensor_tensor(rkv[:, 2 * KT + p, :], rkv[:, 2 * KT + p, :], bonus[:, :], ALU.mult).then_inc(r_bon, 1)
                        pool.wait_ge(r_bon, p + 1)
            low_parts(WO, CHUNKS)

    @block.scalar
    def _(act):
        def split(base, per, i, j):
            if isinstance(i, int) and base + per * i + j + 2 >= total:
                return
            act.wait_ge(s_raw[(j + 2) % RAW], 4 * per * i + 16 * (base // 4 + (j + 2) // 4 + 1))
            act.wait_ge(s_mm, per * i + (base + j + 3))
            act.activation(w_hi[:, j % SPLIT, :, :], raw[:, (j + 2) % RAW, :, :], ACT.Copy).then_inc(s_hi, 1)

        total = CHUNKS if LAYERS == 2 else FO0 + 24
        row = 0
        for src in (a["c"].rearrange("b (k p) -> (b k) p", p=P), a["mod_b"].rearrange("l (k p) -> (l k) p", p=P),
                    a["norm_mix"].rearrange("l (k p) -> (l k) p", p=P)):
            act.dma_start(rows_a[row:row + src.shape[0], :], src).then_inc(s_rows_a, 16)
            row += src.shape[0]
        row = 0
        for src in (a["norm_ffn"].rearrange("l (k p) -> (l k) p", p=P), a["norm_final"].rearrange("(k p) -> k p", p=P),
                    a["rwkv_mu"][0].rearrange("i (k p) -> (i k) p", p=P), a["rwkv_w0"].rearrange("l (k p) -> (l k) p", p=P),
                    a["rwkv_a0"].rearrange("l (k p) -> (l k) p", p=P), a["rwkv_k_k"].rearrange("l (k p) -> (l k) p", p=P),
                    a["rwkv_k_a"].rearrange("l (k p) -> (l k) p", p=P),
                    a["rwkv_r_k"][0].rearrange("(k g) j -> k (g j)", g=2),
                    a["rwkv_ln_w"].rearrange("l (k p) -> (l k) p", p=P), a["rwkv_ln_b"].rearrange("l (k p) -> (l k) p", p=P)):
            act.dma_start(rows_b[row:row + src.shape[0], :], src).then_inc(s_rows_b, 16)
            row += src.shape[0]
        act.dma_start(wf_raw[:, :, :], w_in[:, :, 24 * P:24 * P + NFOX]).then_inc(s_wf, 16)
        act.wait_ge(s_const, CONSTS)
        for r0 in (0, 32, 64, 96):
            act.dma_start(b_f[r0:r0 + NFOX, :], a["attn_b_f"].rearrange("l h -> h l")).then_inc(s_wf, 16)

        act.wait_ge(s_par, 1)
        act.activation(cond[:, :], par_a[:, A_C:A_C + KT], ACT.Silu).then_inc(s_cond, 1)
        def norm_rstd(n):
            if n:
                act.wait_ge(s_ssum, n)
            else:
                act.wait_ge(s_ssq, KT)
            act.activation(rstd[:, :], bank[7 if n else 6][:, :], ACT.Ln, bias=cst[:, 0:1], scale=1.0 / D).then_inc(s_ln, 1)
            act.wait_ge(s_ln, n + 1)
            act.activation(rstd[:, :], rstd[:, :], ACT.Exp, scale=-0.5).then_inc(s_rstd, 1)

        for k in range(KT):
            act.wait_ge(s_xt, k + 1)
            if k >= 2:
                act.wait_ge(s_ssq, k - 1)
            act.activation(ring[:, k % 2, :], bank[k % 4][:, :], ACT.Square).then_inc(s_sq, 1)
            act.activation(x[:, k, :], bank[k % 4][:, :], ACT.Copy).then_inc(s_x0, 1)
        norm_rstd(0)
        act.wait_ge(s_mm, SPLIT)
        split(0, 4, 0, -2)
        split(0, 4, 0, -1)
        act.wait_ge(s_wf, 80)
        for r0 in (0, 32, 64, 96):
            act.activation(wf_hi[:, :, r0:r0 + NFOX], wf_raw[:, :, :], ACT.Copy).then_inc(s_wf_split, 1)

        def norm_hi(n, h0, layer, v):
            if n:
                norm_rstd(n)
            for k in range(KT):
                act.wait_ge(s_u, KT * n + k + 1)
                act.activation(h_hi[:, k, :], ring[:, k % 4, :], ACT.Identity,
                               bias=mod_t[:, layer, v * KT + k:v * KT + k + 1]).then_inc(s_h_hi, 1)

        norm_hi(0, H_MIX0, 0, 0)
        act.wait_ge(s_fv, 2)
        act.activation(ring[:, 2, :], ring[:, 1, :], ACT.Exp).then_inc(s_fa, 1)
        act.wait_ge(s_fa, 1)
        act.activation(ring[:, 3, :], ring[:, 2, :], ACT.Ln, bias=cst[:, 1:2]).then_inc(s_fa, 1)

        def four(base, i):
            for j in range(4):
                split(base, 4, i, j)

        with act.Fori(0, 6) as i:
            four(QKV, i)

        for n in range(0, 8, 2):
            act.wait_ge(s_v_t, n + 1)
            act.activation(v_tok[:, n // 2, (n % 2) * S:(n % 2 + 1) * S], bank[4 + n % 2][:, :], ACT.Copy).then_inc(s_v_tok, 1)
        for h in range(NH + 2):
            if h < NH:
                for qt in range(TT):
                    act.wait_ge(s_max, TT * h + qt + 1)
                    if h >= 2:
                        act.wait_ge(s_pt, h - 1)
                    act.activation(prob[:, h % 2, COL[qt]:COL[qt + 1]], score_of(qt), ACT.Exp,
                                   bias=row_stat[:, h % 2, 0, qt:qt + 1],
                                   accum_out=row_stat[:, h % 2, 1, qt:qt + 1]).then_inc(s_exp, 1)
            g = h - 2
            if g >= 0 and g % 2:
                pair = g // 2
                act.wait_ge(s_pv, g + 1)
                act.activation(h_hi[:, pair, :], bank[7][:, :], ACT.Copy).then_inc(s_h_hi, 1)
            g = h - 1
            if 0 <= g < NH:
                act.wait_ge(s_pt, g + 1)
                if g >= 2:
                    act.wait_ge(s_pv, g - 1)
                act.activation(prob_t[:, g % 2, 0:S], bank[4][:, :], ACT.Copy).then_inc(s_pt_a, 1)

        def square_x(n, t0, i, j):
            act.wait_ge(s_bank, 4 * i + (NB + t0 + j + 1))
            act.wait_ge(s_ssq, 4 * i + (KT * n + j - 1))
            act.activation(ring[:, j % 2, :], x[:, i * 4 + j, :], ACT.Square).then_inc(s_sq, 1)

        def square(base, t0, n):
            with act.Fori(0, 2) as i:
                for j in range(4):
                    square_x(n, t0, i, j)
                    split(base, 4, i, j)

        def swiglu(layer, base_in, base_out, t_in, t_out):
            def pairs(i, tiles):
                for j in range(tiles):
                    split(base_in, 8, i, 2 * j)
                    act.wait_ge(s_mm, 8 * i + (SPLIT + base_in + 2 * j + 1))
                    act.activation(ring[:, j % 2, :], bank[2 * j % 4][:, :], ACT.Silu).then_inc(s_silu, 1)
                    split(base_in, 8, i, 2 * j + 1)
                    act.wait_ge(s_bank, 8 * i + (NB + t_in + 2 * j + 2))
                    act.activation(g_hi[:, i * 4 + j, :], ring[:, 2 + j % 2, :], ACT.Copy).then_inc(s_g_hi, 1)

            with act.Fori(0, 5) as i:
                pairs(i, 4)
            pairs(5, 2)

            def out(i):
                for j in range(4):
                    split(base_out, 12, i, 3 * j)
                    split(base_out, 12, i, 3 * j + 1)
                    square_x(2 + 2 * layer, t_out, i, j)
                    split(base_out, 12, i, 3 * j + 2)

            with act.Fori(0, 1) as i:
                out(i)
            out(1)

        square(AO, T_AO, 1)
        norm_hi(1, H_FFN0, 0, 3)
        swiglu(0, FI0, FO0, T_FI0, T_FO0)
        if LAYERS == 2:
            norm_rstd(2)
            for k in range(KT):
                act.wait_ge(s_u, KT * 2 + k + 1)
                act.activation(h_f[:, k, 4:4 + S], ring[:, k % 4, :], ACT.Identity,
                               bias=mod_t[:, 1, k:k + 1]).then_inc(r_hf, 1)
            act.wait_ge(r_lora, 8)
            act.activation(wa_mid[0:HD, :], bank[0][0:HD, :], ACT.Tanh).then_inc(r_mid, 1)
            act.wait_ge(r_lora, 16)
            act.activation(wa_mid[HD:P, :], bank[1][HD:P, :], ACT.Copy).then_inc(r_mid, 1)
            def mix_hi(n, k):
                act.wait_ge(r_mix, 24 + 8 * n + k + 1)
                act.activation(h_hi[:, k, :], ring[:, k % 4, :], ACT.Copy).then_inc(s_h_hi, 1)

            for k in range(3):
                mix_hi(0, k)
            act.wait_ge(r_lora, 24)
            act.activation(g_mid[:, 0, :], bank[2][:, :], ACT.Sigmoid).then_inc(r_mid, 1)
            act.activation(g_mid[0:GL - P, 1, :], bank[3][0:GL - P, :], ACT.Sigmoid).then_inc(r_mid, 1)
            for n in range(3):
                if n:
                    act.wait_ge(s_mm, SPLIT + RKV + 8 * n)
                    mix_hi(n, 0)
                    split(RKV + 8 * (n - 1), 4, 1, 3)
                for k in range(1 if n else 3, KT):
                    mix_hi(n, k)
                four(RKV + 8 * n, 0)
                for j in range(4 if n == 2 else 3):
                    split(RKV + 8 * n, 4, 1, j)
            par = lambda b, p: par_b[:, b + p:b + p + 1]
            for seg in rwkv_order():
                kind, p = seg[0], seg[1]
                kp = rkv[:, KT + p, :]
                if kind == "prep_lora":
                    if p:
                        act.wait_ge(r_feat, 5 * p)
                        act.wait_ge(r_br, p)
                    act.activation(ring[:, 3, :], kp, ACT.Square, scale=par(B_KK, p)).then_inc(r_sqk, 1)
                elif kind == "prep_sig":
                    act.wait_ge(r_lora_mm, 2 * p + 2)
                    act.activation(ring[:, 0, :], bank[0][:, :], ACT.Sigmoid, bias=par(B_W0, p)).then_inc(r_sig, 1)
                    act.activation(ring[:, 1, :], bank[1][:, :], ACT.Sigmoid, bias=par(B_A0, p)).then_inc(r_sig, 1)
                elif kind == "prep_ln":
                    act.wait_ge(r_ssm, p + 1)
                    act.activation(ring[:, 3, :], ring[:, 3, :], ACT.Ln, scale=2.0 ** 20).then_inc(r_rn, 1)
                elif kind == "prep_norm":
                    act.wait_ge(r_rn, 2 * p + 1)
                    act.activation(ring[:, 3, :], ring[:, 3, :], ACT.Exp, scale=-0.5, bias=cst[:, 3:4]).then_inc(r_rn, 1)
                elif kind == "prep_decay":
                    act.wait_ge(r_cprev, p + 1)
                    act.activation(ring[:, 0, :], ring[:, 2, :], ACT.Exp, scale=DECAY).then_inc(r_dec, 1)
                    act.activation(ring[:, 2, :], ring[:, 2, :], ACT.Exp, scale=-DECAY).then_inc(r_dec, 1)
                elif kind == "prep_key":
                    act.activation(rstd[:, :], rstd[:, :], ACT.Exp, scale=DECAY).then_inc(r_dec, 1)
                elif kind == "prep_bonus":
                    act.wait_ge(r_br, p + 1)
                    if p:
                        act.wait_ge(r_bon, p)
                    act.activation(bonus[:, :], bank[0][:, :], ACT.Copy).then_inc(r_brc, 1)
                elif kind == "gn_sq":
                    act.wait_ge(r_yc, p + 1)
                    act.activation(ssq[:, :], kp, ACT.Square).then_inc(r_ysq, 1)
                elif kind == "gn_ln":
                    act.wait_ge(r_var, p + 1)
                    act.activation(ssq[:, :], bank[1][:, :], ACT.Ln, scale=1.0 / HD, bias=cst[:, 2:3]).then_inc(r_grs, 1)
                elif kind == "gn_exp":
                    act.wait_ge(r_grs, 2 * p + 1)
                    act.activation(ssq[:, :], ssq[:, :], ACT.Exp, scale=-0.5).then_inc(r_grs, 1)
                elif kind == "tok_bk":
                    act.wait_ge(r_tm, 4 * p + 1)
                    act.activation(bk_tok[:, p % 2, 0:4, :], bank[4][:, :], ACT.Copy).then_inc(r_tma, 1)
                elif kind == "tok_av":
                    act.wait_ge(r_tm, 4 * p + 3)
                    act.activation(ax_tok[:, :, 0, :], bank[2][:, :].rearrange("p (c f) -> p c f", c=TT), ACT.Copy).then_inc(r_tma, 1)
                    act.wait_ge(r_tm, 4 * p + 4)
                    act.activation(uv[CH:P, p % 2, 0, :, :], bank[3][CH:P, :], ACT.Copy).then_inc(r_tma, 1)
                    act.activation(uv[0:CH, p % 2, 1, :, :], bank[3][0:CH, :], ACT.Copy).then_inc(r_tma, 1)
                elif kind == "intra":
                    e = seg[2]
                    rows = slice(CH * e, CH * e + CH)
                    act.wait_ge(r_xm, 2 * p + e + 1)
                    act.activation(ax_tok[rows, :, 1, :], bank[(3, 5)[e]][rows, :].rearrange("p (c f) -> p c f", c=TT),
                                   ACT.Copy).then_inc(r_xv, 1)
                elif kind == "first":
                    for g in range(2):
                        act.wait_ge(r_i0m, 2 * p + g + 1)
                        act.activation(inv[:, 4 * g:4 * g + 4, :], bank[4 + g][:, :], ACT.Copy).then_inc(r_i0c, 1)
                elif kind == "join":
                    for g in range(2):
                        act.wait_ge(r_zm, 2 * (5 * p + seg[2] - 1) + g + 1)
                        act.activation(prod[:, 4 * g:4 * g + 4, :], bank[2 + g][:, :], ACT.Copy).then_inc(r_zb, 1)
                elif kind == "turn":
                    act.wait_ge(r_tt, 8 * p + 2 * seg[2])
                    act.activation(inv_t[:, 4:8, :], bank[5][:, :], ACT.Copy).then_inc(r_tta, 1)
                elif kind == "wu":
                    for hd in range(2):
                        act.wait_ge(r_wm, 2 * p + hd + 1)
                        act.activation(w_tok[:, :, HD * hd:HD * hd + HD],
                                       bank[2 + hd][:, :].rearrange("p (c a f) -> p c a f", c=TT, a=2)[:, :, 0, :],
                                       ACT.Copy).then_inc(r_wt, 1)
                    for hd in range(2):
                        act.activation(u0[:, :, HD * hd:HD * hd + HD],
                                       bank[2 + hd][:, :].rearrange("p (c a f) -> p c a f", c=TT, a=2)[:, :, 1, :],
                                       ACT.Copy).then_inc(r_u0, 1)
                elif kind == "w_back":
                    act.wait_ge(r_wtm, p + 1)
                    act.activation(w_f[:, :], bank[1][:, :], ACT.Copy).then_inc(r_w, 1)
                elif kind == "out":
                    n = seg[2]
                    act.wait_ge(r_ym, NC * p + n + 1)
                    act.activation(kp[:, n * CH:(n + 1) * CH], bank[6][:, 256:256 + CH], ACT.Copy).then_inc(r_y, 1)
            act.wait_ge(r_y, NC * KT)
            for k in range(KT):
                act.wait_ge(r_z2, k + 1)
                act.activation(h_hi[:, k, :], rkv[:, KT + k, :], ACT.Copy).then_inc(s_h_hi, 1)
            square(WO, T_WO, 3)
            norm_hi(3, H_FFN1, 1, 3)
            swiglu(1, FI1, FO1, T_FI1, T_FO1)
        norm_rstd(LAST)
        for k in range(KT):
            act.wait_ge(s_y_t, k + 1)
            act.activation(y_tok[:, :, k * P:(k + 1) * P], bank[k % 4][:, :].rearrange("p (t f) -> p t f", t=TT),
                           ACT.Copy).then_inc(s_y, 1)

    @block.vector
    def _(dve):
        def gate_col(layer, v, k):
            return mod_t[:, layer, v * KT + k:v * KT + k + 1]

        dve.wait_ge(s_par_t, 1)
        dve.tensor_copy(par_a[:, :], bank[4][:, 0:A_ROWS]).then_inc(s_par, 1)
        dve.memset(decay_r[:, :], 1.0).then_inc(s_fv0, 1)
        dve.wait_ge(s_cond, 1)
        dve.wait_ge(s_par, 1)
        for v in range(2):
            for k in range(KT):
                n = KT * v + k
                dve.wait_ge(s_mod_first[n // 2], 16)
                if k == 0:
                    dve.tensor_scalar(mod_first[:, n, :], mod_first[:, n, :], cond[:, 0:1], None, ALU.mult).then_inc(s_mod0, 1)
                else:
                    dve.wait_ge(s_mod0, n)
                    dve.scalar_tensor_tensor(out=mod_first[:, KT * v, :], in0=mod_first[:, n, :], scalar=cond[:, k:k + 1],
                                             in1=mod_first[:, KT * v, :], op0=ALU.mult, op1=ALU.add).then_inc(s_mod0, 1)

        def mod_chunk(i, k):
            dve.wait_ge(s_mod_raw[k % 2], 64 * i + 16 * (k // 2 + 1))
            if k == 0:
                dve.wait_ge(s_mod_sum, i + 2)
                dve.tensor_scalar(mod_acc[:, :], mod_raw[:, 0, :], cond[:, 0:1], None, ALU.mult).then_inc(s_mod_used, 1)
            else:
                dve.wait_ge(s_mod_used, 8 * i + (2 + k))
                dve.scalar_tensor_tensor(out=mod_acc[:, :], in0=mod_raw[:, k % 2, :], scalar=cond[:, k:k + 1],
                                         in1=mod_acc[:, :], op0=ALU.mult, op1=ALU.add).then_inc(s_mod_used, 1)

        def mod_finish(layer, v, group, at):
            dve.wait_ge(s_mod_sum, group + 1)
            dve.tensor_tensor(mod_t[:, layer, bass.ts(v, KT)], bank[at][:, 0:KT],
                              par_a[:, bass.ds(v * KT + (A_MODB + 6 * KT * layer), KT)], ALU.add).then_inc(s_mod, 1)

        def set_gain(n, layer, v, norm):
            dve.scalar_tensor_tensor(out=gain[:, n, :], in0=mod_t[:, layer, v * KT:(v + 1) * KT], scalar=1.0, in1=norm,
                                     op0=ALU.add, op1=ALU.mult).then_inc(s_gain, 1)

        dve.wait_ge(s_par_t, 2)
        dve.tensor_copy(par_b[:, :], bank[5][:, 0:P]).then_inc(s_par, 1)
        mod_finish(0, 0, 0, 7)
        mod_finish(0, 1, 1, 7)
        dve.wait_ge(s_mod, 2)
        set_gain(0, 0, 1, par_a[:, A_NMIX:A_NMIX + KT])
        dve.wait_ge(s_x0, KT)
        dve.wait_ge(s_wf_split, 4)
        for r0 in (0, 32, 64, 96):
            dve.tensor_tensor(wf_lo[:, :, r0:r0 + NFOX], wf_raw[:, :, :], wf_hi[:, :, r0:r0 + NFOX].bitcast(F32),
                              ALU.subtract).then_inc(s_wf_lo, 1)

        def norm_u(n, k, gcol):
            dve.scalar_tensor_tensor(out=ring[:, k % 4, :], in0=x[:, k, :], scalar=gcol, in1=rstd[:, :],
                                     op0=ALU.mult, op1=ALU.mult).then_inc(s_u, 1)

        def norm_split(n, h0, layer, v):
            dve.wait_ge(s_gain, n + 1)
            dve.wait_ge(s_rstd, n + 1)
            for k in range(KT + 1):
                if k < KT:
                    if k >= 4:
                        dve.wait_ge(s_h_hi, h0 + k - 3)
                    norm_u(n, k, gain[:, n, k:k + 1])
                if k >= 1:
                    q = k - 1
                    dve.wait_ge(s_u, KT * n + q + 1)
                    dve.wait_ge(s_h_hi, h0 + q + 1)
                    dve.scalar_tensor_tensor(out=h_lo[:, q, :], in0=ring[:, q % 4, :], scalar=gate_col(layer, v, q),
                                             in1=h_hi[:, q, :].bitcast(F32), op0=ALU.add, op1=ALU.subtract).then_inc(s_h, 1)

        norm_split(0, H_MIX0, 0, 0)
        dve.wait_ge(s_f, 1)
        dve.tensor_scalar(ring[:, 0, :], bank[6][:, :], b_f[:, 0:1], None, ALU.add).then_inc(s_fv, 1)
        dve.wait_ge(s_fv, 1)
        dve.scalar_tensor_tensor(out=ring[:, 1, :], in0=ring[:, 0, :], scalar=-1.0, in1=ring[:, 0, :],
                                 op0=ALU.mult, op1=ALU.min).then_inc(s_fv, 1)
        dve.wait_ge(s_fa, 2)
        dve.scalar_tensor_tensor(out=ring[:, 1, :], in0=ring[:, 0, :], scalar=0.0, in1=ring[:, 3, :],
                                 op0=ALU.min, op1=ALU.subtract).then_inc(s_fv, 1)
        dve.wait_ge(s_fv, 3)
        dve.wait_ge(s_fv0, 1)
        dve.tensor_tensor_scan(ring[:, 2, :], decay_r[:, :], ring[:, 1, :], 0.0, ALU.mult, ALU.add).then_inc(s_fv, 1)
        dve.wait_ge(s_fv, 4)
        for r0 in (0, HD):
            dve.tensor_copy(decay_l[r0 + 32:r0 + 32 + NFOX, :], ring[r0 + 32:r0 + 32 + NFOX, 2, :]).then_inc(s_fv, 1)
            dve.tensor_copy(decay_r[r0:r0 + NFOX, :], ring[r0:r0 + NFOX, 2, :]).then_inc(s_fv, 1)
        dve.wait_ge(s_fv, 8)
        for parity in range(2):
            rows = slice(HD * (1 - parity), HD * (1 - parity) + HD)
            dve.tensor_copy(k_dec[rows, parity, :], decay_r[rows, :]).then_inc(s_fv, 1)

        def select_decay(h):
            rows = slice(HD * (1 - h % 2), HD * (1 - h % 2) + HD)
            dve.tensor_scalar(q_dec[rows, h % 2, :], decay_l[rows, :], fox_sel[rows, h:h + 1], None, ALU.mult).then_inc(s_dh, 1)

        select_decay(0)
        select_decay(1)

        def evict_qkv(i, j):
            dve.wait_ge(s_mm, 8 * i + (SPLIT + QKV + j + 1))
            dve.tensor_scalar(qkv[:, i * 8 + j, :], bank[j % 4][:, :], qkv_scale[:, bass.ds(i * 8 + j, 1)], None,
                              ALU.mult).then_inc(s_bank, 1)

        with dve.Fori(0, 3) as i:
            for j in range(8):
                mod_chunk(i, j)
                evict_qkv(i, j)
            mod_finish(0, i + 2, i + 2, 7)

        for n in range(1, 8, 2):
            dve.wait_ge(s_v_t, n + 1)
            dve.tensor_copy(v_tok[:, n // 2, (n % 2) * S:(n % 2 + 1) * S], bank[4 + n % 2][:, :]).then_inc(s_v_tokv, 1)
        dve.wait_ge(s_mod, 5)
        set_gain(1, 0, 4, par_b[:, B_NFFN:B_NFFN + KT])
        for h in range(NH + 2):
            g = h - 1
            if 0 <= g < NH:
                for qt in range(TT):
                    dve.wait_ge(s_exp, TT * g + qt + 1)
                    dve.reciprocal(row_stat[:, g % 2, 2, qt:qt + 1], row_stat[:, g % 2, 1, qt:qt + 1]).then_inc(s_rinv, 1)
                for qt in range(TT):
                    dve.wait_ge(s_rinv, TT * g + qt + 1)
                    dve.tensor_scalar(prob[:, g % 2, COL[qt]:COL[qt + 1]], prob[:, g % 2, COL[qt]:COL[qt + 1]],
                                      row_stat[:, g % 2, 2, qt:qt + 1], None, ALU.mult).then_inc(s_norm, 1)
            if h < NH:
                for qt in range(TT):
                    dve.wait_ge(s_score, TT * h + qt + 1)
                    dve.tensor_reduce(row_stat[:, h % 2, 0, qt:qt + 1], score_of(qt), AX_X, ALU.max,
                                      negate=True).then_inc(s_max, 1)
            if h < NFOX - 2:
                select_decay(h + 2)
            if h >= 2 and (h - 2) % 2:
                pair = (h - 2) // 2
                dve.wait_ge(s_h_hi, H_ATT + pair + 1)
                dve.tensor_tensor(h_lo[:, pair, :], bank[7][:, :], h_hi[:, pair, :].bitcast(F32),
                                  ALU.subtract).then_inc(s_h, 1)
            if 0 <= g < NH:
                dve.wait_ge(s_pt, g + 1)
                if g >= 2:
                    dve.wait_ge(s_pv, g - 1)
                dve.tensor_copy(prob_t[:, g % 2, S:S + 384], bank[5][:, 0:384]).then_inc(s_pt_v, 1)
                dve.tensor_copy(prob_t[:, g % 2, S + 384:1280], bank[6][:, 0:384]).then_inc(s_pt_v, 1)

        def residual(base, per, last, layer, v, n, t0, i, j):
            dve.wait_ge(s_mm, per * i + (SPLIT + base + last + 1))
            dve.scalar_tensor_tensor(out=x[:, i * 4 + j, :], in0=bank[j][:, :],
                                     scalar=mod_t[:, layer, bass.ds(i * 4 + (v * KT + j), 1)], in1=x[:, i * 4 + j, :],
                                     op0=ALU.mult, op1=ALU.add).then_inc(s_bank, 1)
            dve.wait_ge(s_sq, 4 * i + (KT * n + j + 1))
            dve.wait_ge(s_ssq, 4 * i + (KT * n + j))
            dve.tensor_tensor(ssq[:, :], ssq[:, :], ring[:, j % 2, :], ALU.add).then_inc(s_ssq, 1)

        def clear_ssq(n):
            if n >= 2:
                dve.wait_ge(s_ssum, n - 1)
            dve.memset(ssq[:, :], 0.0).then_inc(s_ssq0, 1)
            dve.wait_ge(s_ssq0, n)

        def square(base, layer, t0, n):
            clear_ssq(n)
            if layer == 0:
                for k in range(KT):
                    mod_chunk(3, k)
                    residual(base, 4, k % 4, layer, 2, n, t0, k // 4, k % 4)
            else:
                with dve.Fori(0, 2) as i:
                    for j in range(4):
                        residual(base, 4, j, layer, 2, n, t0, i, j)

        def swiglu(layer, base_in, base_out, t_in):
            def pairs(i, tiles):
                for j in range(tiles):
                    at = FT * layer + j + 1
                    if layer == 0:
                        per = KT // tiles
                        for k in range(per * j, per * j + per):
                            mod_chunk(i + 4, k)
                    dve.wait_ge(s_silu, 4 * i + at)
                    dve.wait_ge(s_mm, 8 * i + (SPLIT + base_in + 2 * j + 2))
                    dve.tensor_tensor(ring[:, 2 + j % 2, :], ring[:, j % 2, :], bank[(2 * j + 1) % 4][:, :],
                                      ALU.mult).then_inc(s_bank, 2)
                    dve.wait_ge(s_g_hi, 4 * i + at)
                    dve.tensor_tensor(g_lo[:, i * 4 + j, :], ring[:, 2 + j % 2, :], g_hi[:, i * 4 + j, :].bitcast(F32),
                                      ALU.subtract).then_inc(s_g, 1)
                if layer == 0:
                    mod_finish(1, i, i + 6, 7)

            with dve.Fori(0, 5) as i:
                pairs(i, 4)
            pairs(5, 2)
            n = 2 + 2 * layer
            clear_ssq(n)
            with dve.Fori(0, 2) as i:
                for j in range(4):
                    residual(base_out, 12, 3 * j + 2, layer, 5, n, 0, i, j)

        square(AO, 0, T_AO, 1)
        norm_split(1, H_FFN0, 0, 3)
        mod_finish(0, 5, 5, 6)
        dve.wait_ge(s_mod, 6)
        swiglu(0, FI0, FO0, T_FI0)
        dve.wait_ge(s_mod, 12)
        set_gain(2, 1, 1, par_a[:, A_NMIX + KT:A_NMIX + 2 * KT])
        set_gain(3, 1, 4, par_b[:, B_NFFN + KT:B_NFFN + 2 * KT])
        if LAYERS == 2:
            dve.wait_ge(s_mm, SPLIT + RKV)
            dve.memset(h_f[:, :, 3:4], 0.0).then_inc(r_hf0, 1)
            dve.wait_ge(s_gain, 4)
            dve.wait_ge(s_rstd, 3)
            for k in range(KT):
                if k >= 4:
                    dve.wait_ge(r_hf, k - 3)
                norm_u(2, k, gain[:, 2, k:k + 1])
            mus = (1, 4, 5, 0, 2, 3)

            def mix(n, k):
                m = KT * n + k
                dve.wait_ge(r_xxv if k % 2 else r_xx, k // 2 + 1)
                if m < 4:
                    dve.wait_ge(r_hf, KT)
                elif m < 28:
                    dve.wait_ge(r_lora, m - 3)
                else:
                    dve.wait_ge(s_h, H_R + m - 27)
                dve.scalar_tensor_tensor(out=ring[:, k % 4, :], in0=xx[:, k, :],
                                         scalar=par_b[:, B_MU + 8 * mus[n] + k:B_MU + 8 * mus[n] + k + 1],
                                         in1=h_f[:, k, 4:4 + S], op0=ALU.mult, op1=ALU.add).then_inc(r_mix, 1)

            for n in range(3):
                for k in range(KT):
                    if n == 0 and k % 2:
                        dve.tensor_tensor(xx[:, k, :], h_f[:, k, 3:3 + S], h_f[:, k, 4:4 + S], ALU.subtract).then_inc(r_xxv, 1)
                    mix(n, k)
            dve.wait_ge(r_mask, MASKS)
            for n in range(3, 6):
                for k in range(KT + 1):
                    if k < KT and (n == 3 or k >= 4):
                        mix(n, k)
                    if k >= 1:
                        q = 8 * (n - 3) + k
                        dve.wait_ge(r_mix, 24 + q)
                        dve.wait_ge(s_h_hi, H_R + q)
                        dve.tensor_tensor(h_lo[:, k - 1, :], ring[:, (k - 1) % 4, :], h_hi[:, k - 1, :].bitcast(F32),
                                          ALU.subtract).then_inc(s_h, 1)
                if n < 5:
                    for k in range(4):
                        mix(n + 1, k)
                with dve.Fori(0, 2) as i:
                    for j in range(4):
                        dve.wait_ge(s_mm, 4 * i + (SPLIT + RKV + 8 * (n - 3) + j + 1))
                        dve.tensor_copy(rkv[:, i * 4 + (8 * (n - 3) + j), :], bank[j][:, :]).then_inc(s_bank, 1)
            for seg in rwkv_order():
                kind, p = seg[0], seg[1]
                rp, kp, vp = rkv[:, p, :], rkv[:, KT + p, :], rkv[:, 2 * KT + p, :]
                par = lambda b: par_b[:, b + p:b + p + 1]
                if kind == "prep_cum":
                    dve.wait_ge(r_sig, 2 * p + 1)
                    dve.tensor_tensor_scan(ring[:, 2, :], restart[:, :], ring[:, 0, :], 0.0, ALU.mult, ALU.add).then_inc(r_cum, 1)
                elif kind == "prep_prev":
                    dve.wait_ge(r_ss, p + 1)
                    dve.tensor_scalar(ring[:, 3, :], bank[0][:, :], 1e-24, None, ALU.max).then_inc(r_ssm, 1)
                elif kind == "prep_key":
                    dve.wait_ge(r_rn, 2 * p + 2)
                    dve.scalar_tensor_tensor(out=key[:, :], in0=kp, scalar=par(B_KK), in1=ring[:, 3, :],
                                             op0=ALU.mult, op1=ALU.mult).then_inc(r_kk, 1)
                    dve.tensor_scalar(bonus_w[:, :], heads2[:, :], par(B_RK), None, ALU.mult).then_inc(r_bwt, 1)
                elif kind == "prep_a":
                    dve.wait_ge(r_kk, p + 1)
                    dve.wait_ge(r_dec, 3 * p + 3)
                    dve.scalar_tensor_tensor(out=ar_f[:, 0, :], in0=key[:, :], scalar=-1.0, in1=rstd[:, :], op0=ALU.mult,
                                             op1=ALU.mult).then_inc(r_feat, 1)
                elif kind in ("prep_b", "prep_r", "prep_k"):
                    bk = lambda slots: bk_f[:, :, slots, :]
                    by_chunk = lambda t: t.rearrange("p (c e t) -> p c e t", e=2, t=CH)
                if kind == "prep_b":
                    dve.wait_ge(r_b, p + 1)
                    dve.tensor_scalar(ring[:, 1, :], ring[:, 1, :], -1.0, par(B_KA), ALU.add, ALU.mult).then_inc(r_t, 1)
                    dve.tensor_tensor(bk(slice(0, 4, 3)), by_chunk(ssq[:, :]), by_chunk(ring[:, 2, :]), ALU.mult).then_inc(r_feat, 1)
                    dve.wait_ge(r_t, p + 1)
                    dve.scalar_tensor_tensor(out=kp, in0=ring[:, 1, :], scalar=1.0, in1=kp, op0=ALU.add,
                                             op1=ALU.mult).then_inc(r_k1, 1)
                elif kind == "prep_r":
                    dve.wait_ge(r_k1, p + 1)
                    dve.tensor_tensor(ring[:, 3, :], rp, kp, ALU.mult).then_inc(r_prd, 1)
                    dve.tensor_tensor(ar_f[:, 1, :], rp, ring[:, 0, :], ALU.mult).then_inc(r_feat, 1)
                elif kind == "prep_k":
                    dve.tensor_tensor(bk(slice(1, 3)), by_chunk(kp), by_chunk(ring[:, 2, :]), ALU.mult).then_inc(r_feat, 1)
                    dve.tensor_copy(chunk_decay[:, p % 3, :],
                                    ring[:, 0, :].rearrange("p (n c) -> p n c", c=CH)[:, :, CH - 1]).then_inc(r_feat, 1)
                elif kind == "gn_center":
                    dve.wait_ge(r_mean, p + 1)
                    dve.scalar_tensor_tensor(out=kp, in0=bank[1][:, :], scalar=-1.0 / HD, in1=kp, op0=ALU.mult,
                                             op1=ALU.add).then_inc(r_yc, 1)
                elif kind == "gn_norm":
                    dve.wait_ge(r_grs, 2 * p + 2)
                    dve.scalar_tensor_tensor(out=kp, in0=kp, scalar=par(B_LNW), in1=ssq[:, :],
                                             op0=ALU.mult, op1=ALU.mult).then_inc(r_yn, 1)
                elif kind == "gn_bonus":
                    dve.wait_ge(r_yn, p + 1)
                    dve.scalar_tensor_tensor(out=kp, in0=kp, scalar=par(B_LNB), in1=vp, op0=ALU.add,
                                             op1=ALU.add).then_inc(r_z1, 1)
                elif kind == "gn_gate":
                    dve.wait_ge(r_z1, p + 1)
                    dve.wait_ge(r_gmm, p + 1)
                    dve.tensor_tensor(kp, kp, bank[1][:, :], ALU.mult).then_inc(r_z2, 1)
                elif kind == "tok_bk":
                    dve.wait_ge(r_tm, 4 * p + 2)
                    dve.tensor_copy(bk_tok[:, p % 2, 4:8, :], bank[5][:, :]).then_inc(r_tmv, 1)
                elif kind == "pairs":
                    g = seg[2]
                    dve.wait_ge(r_pm, 4 * p + g + 1)
                    dve.tensor_tensor(ar[:, p % 2, g // 2, 4 * (g % 2):4 * (g % 2) + 4, :, :],
                                      bank[PAIR_BANK[g]][:, :].rearrange("p (n a t) -> p n a t", n=4, a=2),
                                      before[:, :, :].unsqueeze(1).broadcast_to((P, 4, 2, CH)), ALU.mult).then_inc(r_pe, 1)
                elif kind == "first":
                    if p:
                        dve.wait_ge(r_wm, 2 * p)
                    else:
                        dve.wait_ge(r_zero, 2)
                    for hd in range(2):
                        half = slice(4 * hd, 4 * hd + 4)
                        dve.wait_ge(r_pe, 4 * p + 2 * hd + 2)
                        even = slice(0, CH)
                        dve.tensor_tensor(inv_t[even, half, even], ar[even, p % 2, hd, 0::2, 0, :],
                                          levels[even, 0, even].unsqueeze(1).broadcast_to((CH, TT, CH)),
                                          ALU.mult).then_inc(r_l0, 1)
                        dve.wait_ge(r_l0, 2 * p + hd + 1)
                        dve.wait_ge(r_m, 12 * p + hd + 1)
                        dve.tensor_tensor(inv_t[:, half, :], inv_t[:, half, :], ident[:, :].unsqueeze(1).broadcast_to((P, 4, P)),
                                          ALU.add).then_inc(r_i0, 1)
                elif kind == "grow":
                    for g in range(2):
                        half = slice(4 * g, 4 * g + 4)
                        dve.wait_ge(r_gm, 8 * p + 2 * (seg[2] - 1) + g + 1)
                        dve.tensor_tensor(inv[:, half, :], inv[:, half, :],
                                          bank[4 + g][:, :].rearrange("p (q t) -> p q t", q=4), ALU.add).then_inc(r_inv, 1)
                elif kind == "turn":
                    dve.wait_ge(r_tt, 8 * p + 2 * seg[2] - 1)
                    dve.tensor_copy(inv_t[:, 0:4, :], bank[4][:, :]).then_inc(r_ttv, 1)
                elif kind == "grow_t":
                    for g in range(2):
                        half = slice(4 * g, 4 * g + 4)
                        dve.wait_ge(r_lm, 2 * p + g + 1)
                        dve.tensor_tensor(inv_t[:, half, :], inv_t[:, half, :],
                                          bank[4 + g][:, :].rearrange("p (q t) -> p q t", q=4), ALU.add).then_inc(r_last, 1)
                elif kind == "wu":
                    if p:
                        dve.wait_ge(r_s2, NC * p)
                    dve.memset(state[:, 0, :], 0.0).then_inc(r_s0, 1)
                elif kind == "step":
                    n = seg[2]
                    c, e, rows = n // 2, n % 2, slice(CH * (n % 2), CH * (n % 2) + CH)
                    dve.wait_ge(r_um, NC * p + n + 1)
                    dve.tensor_tensor(uv[rows, p % 2, e, (c + e) % TT, :], bank[6][rows, 0:P], u0[rows, c, :],
                                      ALU.add).then_inc(r_u, 1)
                elif kind == "out":
                    n = seg[2]
                    dve.wait_ge(r_sm, NC * p + n + 1)
                    dve.tensor_tensor(state_t[:, :], bank[7][:, 0:P], state[:, n % 2, :], ALU.add).then_inc(r_s1, 1)
                    dve.wait_ge(r_s1, NC * p + n + 1)
                    dve.scalar_tensor_tensor(out=state[:, (n + 1) % 2, :], in0=state_t[:, :],
                                             scalar=chunk_decay[:, p % 3, n:n + 1], in1=heads2[:, :], op0=ALU.mult,
                                             op1=ALU.mult).then_inc(r_s2, 1)
            for k in range(KT):
                dve.wait_ge(r_z2, k + 1)
                dve.wait_ge(s_h_hi, H_WO + k + 1)
                dve.tensor_tensor(h_lo[:, k, :], rkv[:, KT + k, :], h_hi[:, k, :].bitcast(F32), ALU.subtract).then_inc(s_h, 1)
            square(WO, 1, T_WO, 3)
            norm_split(3, H_FFN1, 1, 3)
            swiglu(1, FI1, FO1, T_FI1)
        dve.wait_ge(s_rstd, LAST + 1)
        for k in range(KT):
            if k >= 4:
                dve.wait_ge(s_y_t, k - 3)
            norm_u(LAST, k, par_b[:, B_NFIN + k:B_NFIN + k + 1])

    @block.tensor
    def _(pe):
        def multiply(base, per, i, j, psum, rhs, tiles=KT, k0=0, first=True, last=True, ready=None):
            pe.wait_ge(s_lo, per * i + (base + j + 1 + RAW))
            for t in range(tiles):
                if ready is not None:
                    pe.wait_ge(ready[0], ready[1] + k0 + t + 1)
                hi, lo = rhs[0](k0 + t), rhs[1](k0 + t)
                for q, (w, r) in enumerate(((w_hi, hi), (w_hi, lo), (w_lo, hi))):
                    mm = pe.matmul(psum[:, :], w[:, j % SPLIT, t, :], r, start=first and t == 0 and q == 0,
                                   stop=last and t == tiles - 1 and q == 2)
            mm.then_inc(s_mm, 1)

        def start(base, t0, ready, rest=None):
            lag = 3
            for j in range(2):
                pe.wait_ge(s_bank, t0 + j + 1)
                pe.wait_ge(s_hi, base + j + 1)
            pe.wait_ge(s_lo, base + 1 + RAW)
            for k in range(KT + lag):
                if k < KT:
                    pe.wait_ge(ready[0], ready[1] + k + 1)
                    for j in range(2):
                        pe.matmul(bank[j][:, :], w_hi[:, j, k, :], h_hi[:, k, :], start=k == 0, stop=False)
                        pe.matmul(bank[j][:, :], w_hi[:, j, k, :], h_lo[:, k, :], start=False, stop=False)
                    mm = pe.matmul(bank[0][:, :], w_lo[:, 0, k, :], h_hi[:, k, :], start=False, stop=k == KT - 1)
                    if k == KT - 1:
                        mm.then_inc(s_mm, 1)
                if k == lag:
                    pe.wait_ge(s_lo, base + 2 + RAW)
                if k >= lag:
                    mm = pe.matmul(bank[1][:, :], w_lo[:, 1, k - lag, :], h_hi[:, k - lag, :], start=False,
                                   stop=k == KT + lag - 1)
            mm.then_inc(s_mm, 1)
            if rest is not None:
                pe.wait_ge(rest[0], rest[1])
            pe.wait_ge(s_bank, t0 + 3)
            pe.wait_ge(s_hi, base + 3)
            for k in range(KT):
                pe.matmul(bank[2][:, :], w_hi[:, 0, k, :], h_hi[:, k, :], start=k == 0, stop=False)
                pe.matmul(bank[2][:, :], w_hi[:, 0, k, :], h_lo[:, k, :], start=False, stop=False)
            pe.wait_ge(s_lo, base + 3 + RAW)
            for k in range(KT):
                mm = pe.matmul(bank[2][:, :], w_lo[:, 0, k, :], h_hi[:, k, :], start=False, stop=k == KT - 1)
            mm.then_inc(s_mm, 1)
            pe.wait_ge(s_bank, t0 + 4)
            multiply(base, 4, 0, 3, bank[3], h_of)

        def mod_sum(acc, group, at=7):
            pe.wait_ge(s_mod, group)
            for c in range(KT):
                mm = pe.matmul(bank[at][:, c:c + 1], acc[:, c * P:(c + 1) * P], ones[:, 0:1], start=True, stop=True)
            mm.then_inc(s_mod_sum, 1)

        def norm_sum(n):
            pe.wait_ge(s_ssq, KT * (n + 1))
            pe.matmul(bank[7][:, :], ones[:, :], ssq[:, :], start=True, stop=True).then_inc(s_ssum, 1)

        pe.wait_ge(s_const, CONSTS)
        pe.wait_ge(s_rows_a, 16 * 3)
        pe.transpose(bank[4][:, 0:A_ROWS], rows_a[:, :], ident[0:A_ROWS, 0:A_ROWS]).then_inc(s_par_t, 1)
        pe.wait_ge(s_x_tok, 16)

        def square_sum(k):
            pe.wait_ge(s_sq, k + 1)
            mm = pe.matmul(bank[6][:, :], ones[:, :], ring[:, k % 2, :], start=k == 0, stop=k == KT - 1)
            mm.then_inc(s_ssq, 1)

        for k in range(KT):
            if k >= 4:
                pe.wait_ge(s_x0, k - 3)
                pe.wait_ge(s_sq, k - 3)
            for t in range(TT):
                mm = pe.transpose(bank[k % 4][:, t * P:(t + 1) * P], x_tok[:, t, k * P:(k + 1) * P], ident[:, :])
            mm.then_inc(s_xt, 1)
            if k >= 1:
                square_sum(k - 1)
        square_sum(KT - 1)
        pe.wait_ge(s_rows_b, 16 * 10)
        pe.transpose(bank[5][:, 0:P], rows_b[:, :], ident[:, :]).then_inc(s_par_t, 1)
        pe.wait_ge(s_mod0, KT)
        for c in range(KT):
            mm = pe.matmul(bank[7][:, c:c + 1], mod_first[:, 0, c * P:(c + 1) * P], ones[:, 0:1], start=True, stop=True)
        mm.then_inc(s_mod_sum, 1)
        pe.wait_ge(s_mod0, 2 * KT)
        mod_sum(mod_first[:, KT, :], 1)
        pe.wait_ge(s_wf_lo, 4)
        for k in range(KT):
            pe.wait_ge(s_h, H_MIX0 + k + 1)
            for q, (w, r) in enumerate(((wf_hi, h_hi), (wf_hi, h_lo), (wf_lo, h_hi))):
                mm = pe.matmul(bank[6][:, :], w[:, k, :], r[:, k, :], start=k == 0 and q == 0, stop=k == KT - 1 and q == 2)
        mm.then_inc(s_f, 1)

        with pe.Fori(0, 3) as i:
            for j in range(8):
                pe.wait_ge(s_bank, 8 * i + (T_QKV + j + 1))
                multiply(QKV, 8, i, j, bank[j % 4], h_of)
            pe.wait_ge(s_mod_used, 8 * i + 10)
            mod_sum(mod_acc, i + 2)

        pe.wait_ge(s_bank, NB + T_QKV + 24)
        for n in range(8):
            if n >= 2:
                pe.wait_ge(s_v_tok if n % 2 == 0 else s_v_tokv, n // 2)
            for f in range(4):
                mm = pe.transpose(bank[4 + n % 2][:, f * P:(f + 1) * P], qkv[:, 8 + 12 * (n % 2) + f, (n // 2) * P:(n // 2 + 1) * P],
                                  ident[:, :])
            mm.then_inc(s_v_t, 1)
        pe.wait_ge(s_v_tok, 4)
        pe.wait_ge(s_v_tokv, 4)
        pe.wait_ge(s_mod, 5)
        pe.wait_ge(s_fv, 10)
        for h in range(NH + 2):
            if h < NH:
                pair, rows = (h % NFOX) // 2, slice(HD * (h % 2), HD * (h % 2) + HD)
                if h < NFOX:
                    pe.wait_ge(s_dh, h + 1)
                    pe.wait_ge(s_qk, 2 * h + 2)
                for qt in range(TT):
                    if h >= 1:
                        pe.wait_ge(s_exp, TT * (h - 1) + qt + 1)
                    cols = slice(qt * P, (qt + 1) * P)
                    psum = score_of(qt)
                    if h < NFOX:
                        pe.matmul(psum, q_dec[:, h % 2, cols], k_dec[:, h % 2, 0:(qt + 1) * P], start=True, stop=False)
                    else:
                        pe.matmul(psum, qkv[rows, 12 + pair, cols], qkv[rows, 16 + pair, 0:(qt + 1) * P], start=True,
                                  stop=False)
                    pe.matmul(psum[:, qt * P:(qt + 1) * P], ident_b[:, :], causal[:, :], start=False,
                              stop=True).then_inc(s_score, 1)
            g = h - 2
            if g >= 0:
                pair = g // 2
                if g % 2 == 0 and pair >= 1:
                    pe.wait_ge(s_h, H_ATT + pair)
                pe.wait_ge(s_pt_a, g + 1)
                pe.wait_ge(s_pt_v, 2 * g + 2)
                rows = slice(HD * (g % 2), HD * (g % 2) + HD)
                for kt in range(TT):
                    o = (0, S, S + 384, S + 640)[kt]
                    mm = pe.matmul(bank[7][rows, kt * P:S], v_tok[:, kt, g * HD:(g + 1) * HD],
                                   prob_t[:, g % 2, o:o + S - kt * P], start=kt == 0, stop=kt == TT - 1)
                mm.then_inc(s_pv, 1)
            g = h - 1
            if 0 <= g < NH:
                if g >= 1:
                    pe.wait_ge(s_pt_a, g)
                    pe.wait_ge(s_pt_v, 2 * g)
                for qt in range(TT):
                    pe.wait_ge(s_norm, TT * g + qt + 1)
                    for kt in range(qt + 1):
                        dst = bank[PT_BANK[kt]][:, PT_OFF[kt] + (qt - kt) * P:PT_OFF[kt] + (qt - kt + 1) * P]
                        mm = pe.transpose(dst, prob[:, g % 2, COL[qt] + kt * P:COL[qt] + (kt + 1) * P], ident[:, :])
                mm.then_inc(s_pt, 1)

        def square(base, t0, h0, rest=None):
            start(base, t0, (s_h, h0), rest)
            for j in range(4):
                pe.wait_ge(s_bank, t0 + 4 + j + 1)
                multiply(base, 4, 1, j, bank[j], h_of)

        def swiglu(layer, base_in, base_out, t_in, t_out, h0):
            def pairs(i, tiles, done=0):
                for j in range(done, 2 * tiles):
                    pe.wait_ge(s_bank, 8 * i + (t_in + j + 1))
                    multiply(base_in, 8, i, j, bank[j % 4], h_of)
                if layer == 0:
                    pe.wait_ge(s_mod_used, 8 * i + 42)
                    mod_sum(mod_acc, i + 6)

            start(base_in, t_in, (s_h, h0))
            pairs(0, 4, 4)
            with pe.Fori(1, 5) as i:
                pairs(i, 4)
            pairs(5, 2)
            with pe.Fori(0, 2) as i:
                for j in range(4):
                    pe.wait_ge(s_bank, 4 * i + (t_out + j + 1))
                    for c, (k0, kn) in enumerate(OUT_PARTS):
                        multiply(base_out, 12, i, 3 * j + c, bank[j], g_of, kn, k0, c == 0, c == 2,
                                 ready=(s_g, FT * layer) if j == 0 else None)

        square(AO, T_AO, H_ATT)
        norm_sum(1)
        pe.wait_ge(s_mod_used, 34)
        mod_sum(mod_acc, 5, 6)
        swiglu(0, FI0, FO0, T_FI0, T_FO0, H_FFN0)
        norm_sum(2)
        if LAYERS == 2:
            pe.wait_ge(s_bank, NB + T_RKV)
            pe.wait_ge(r_lora_w, 48)
            for m in range(24):
                k, x_mix = m % KT, ring[:, m % 4, :]
                pe.wait_ge(r_mix, m + 1)
                if m < 8:
                    mm = pe.matmul(bank[0][0:HD, :], w1[:, k, :], x_mix, start=k == 0, stop=k == KT - 1)
                elif m < 16:
                    mm = pe.matmul(bank[1][HD:P, :], a1[:, k, :], x_mix, start=k == 0, stop=k == KT - 1)
                else:
                    pe.matmul(bank[2][:, :], g1[:, k, 0:P], x_mix, start=k == 0, stop=k == KT - 1)
                    mm = pe.matmul(bank[3][0:GL - P, :], g1[:, k, P:GL], x_mix, start=k == 0, stop=k == KT - 1)
                mm.then_inc(r_lora, 1)
            pe.wait_ge(r_mid, 2)
            for n in range(3):
                square(RKV + 8 * n, T_RKV + 8 * n, H_R + 8 * n, None if n else (r_mid, 4))
            pe.wait_ge(s_bank, NB + T_WO)
            pe.wait_ge(r_mask, MASKS)
            pe.wait_ge(r_g2, 32)
            pe.wait_ge(r_wa2, 32)
            for seg in rwkv_order():
                kind, p = seg[0], seg[1]
                rp, vp = rkv[:, p, :], rkv[:, 2 * KT + p, :]
                blocks = [(hd, c, 4 * hd + c) for hd in range(2) for c in range(TT)]
                if kind == "prep_lora":
                    if p:
                        pe.wait_ge(r_pe, 4 * p)
                        pe.wait_ge(r_brc, p)
                    cols = slice(p * P, (p + 1) * P)
                    pe.matmul(bank[0][:, :], wa2[0:HD, cols], wa_mid[0:HD, :], start=True, stop=True).then_inc(r_lora_mm, 1)
                    pe.matmul(bank[1][:, :], wa2[HD:P, cols], wa_mid[HD:P, :], start=True, stop=True).then_inc(r_lora_mm, 1)
                elif kind == "prep_cum":
                    pe.wait_ge(r_sqk, p + 1)
                    pe.wait_ge(r_sig, 2 * p + 1)
                    pe.matmul(bank[0][:, :], heads2[:, :], ring[:, 3, :], start=True, stop=True).then_inc(r_ss, 1)
                elif kind == "prep_k":
                    pe.wait_ge(r_bwt, p + 1)
                    pe.wait_ge(r_prd, p + 1)
                    pe.matmul(bank[0][:, :], bonus_w[:, :], ring[:, 3, :], start=True, stop=True).then_inc(r_br, 1)
                elif kind == "gn_mean":
                    pe.wait_ge(r_y, NC * (p + 1))
                    pe.wait_ge(r_sig, 2 * min(p + 4, KT))
                    if p:
                        pe.wait_ge(r_z2, p)
                    pe.matmul(bank[1][:, :], heads2[:, :], rkv[:, KT + p, :], start=True, stop=True).then_inc(r_mean, 1)
                elif kind == "gn_var":
                    pe.wait_ge(r_ysq, p + 1)
                    pe.matmul(bank[1][:, :], heads2[:, :], ssq[:, :], start=True, stop=True).then_inc(r_var, 1)
                elif kind == "gn_norm":
                    pe.wait_ge(r_grs, 2 * p + 1)
                    pe.matmul(bank[1][:, :], raw[:, 2, p, :], g_mid[:, 0, :], start=True, stop=False)
                    pe.matmul(bank[1][:, :], raw[0:GL - P, 3, p, :], g_mid[0:GL - P, 1, :], start=False,
                              stop=True).then_inc(r_gmm, 1)
                elif kind == "tok_bk":
                    pe.wait_ge(r_feat, 5 * p + 4)
                    if p:
                        pe.wait_ge(r_last, 2 * p)
                    for g, b in enumerate((4, 5)):
                        for n in range(4):
                            mm = pe.transpose(bank[b][:, n * P:(n + 1) * P],
                                              bk_f[:, 2 * g + n // 2, 2 * (n % 2):2 * (n % 2) + 2, :], ident[:, :])
                        mm.then_inc(r_tm, 1)
                elif kind == "tok_av":
                    if p:
                        pe.wait_ge(r_u0, 2 * p)
                    for c in range(TT):
                        mm = pe.transpose(bank[2][:, c * P:(c + 1) * P], ar_f[:, 0, c * P:(c + 1) * P], ident[:, :])
                    mm.then_inc(r_tm, 1)
                    for c in range(TT):
                        t = (2 * KT + p) * S + c * P - CH
                        pe.transpose(bank[3][:, c * P:(c + 1) * P], rkv_flat[:, t:t + P], ident[:, :])
                    mm = pe.transpose(bank[3][0:CH, 0:P], vp[:, S - CH:S], ident[:, :])
                    mm.then_inc(r_tm, 1)
                elif kind == "pairs":
                    g = seg[2]
                    if g == 0:
                        pe.wait_ge(r_tma, 4 * p + 1)
                    elif g == 1:
                        pe.wait_ge(r_tmv, p + 1)
                    elif g == 2 and p:
                        pe.wait_ge(r_w, p)
                    elif g == 3:
                        pe.wait_ge(r_tma, 4 * p + 2)
                    rows = slice(HD * (g // 2), HD * (g // 2) + HD)
                    for m in range(4):
                        n = 4 * (g % 2) + m
                        mm = pe.matmul(bank[PAIR_BANK[g]][:, m * P:(m + 1) * P],
                                       bk_f[rows, n // 2, 2 * (n % 2):2 * (n % 2) + 2, :],
                                       ar_f[rows, :, n * CH:(n + 1) * CH], start=True, stop=True)
                    mm.then_inc(r_pm, 1)
                elif kind == "intra":
                    e = seg[2]
                    pe.wait_ge(r_pe, 4 * p + 4)
                    if e == 0:
                        pe.wait_ge(r_tma, 4 * p + 4)
                    rows, krows = slice(CH * e, CH * e + CH), slice(CH * (1 - e), CH * (1 - e) + CH)
                    for hd, c, _ in blocks:
                        f = slice(HD * hd, HD * hd + HD)
                        mm = pe.matmul(bank[(3, 5)[e]][rows, c * P + HD * hd:c * P + HD * hd + HD],
                                       ar[krows, p % 2, hd, 2 * c + e, 0, :], uv[krows, p % 2, e, (c + e) % TT, f],
                                       start=True, stop=True)
                    mm.then_inc(r_xm, 1)
                elif kind == "first":
                    for g in range(2):
                        pe.wait_ge(r_i0, 2 * p + g + 1)
                        if g == 1:
                            pe.wait_ge(r_xv, 2 * p + 2)
                        for q in range(4 * g, 4 * g + 4):
                            mm = pe.transpose(bank[4 + g][:, q % 4 * P:(q % 4 + 1) * P], inv_t[:, q, :], ident[:, :])
                        mm.then_inc(r_i0m, 1)
                elif kind == "join":
                    l = seg[2]
                    pe.wait_ge(r_m, 12 * p + 2 * l + 2)
                    for g in range(2):
                        if l == 1:
                            pe.wait_ge(r_i0c, 2 * p + g + 1)
                        else:
                            pe.wait_ge(r_inv, 8 * p + 2 * (l - 2) + g + 1)
                        for q in range(4 * g, 4 * g + 4):
                            mm = pe.matmul(bank[2 + g][:, q % 4 * P:(q % 4 + 1) * P], join_t[:, (p + l) % 2, q, :], inv[:, q, :],
                                           start=True, stop=True)
                        mm.then_inc(r_zm, 1)
                elif kind in ("grow", "grow_t"):
                    l = seg[2]
                    for g in range(2):
                        pe.wait_ge(r_zb, 2 * (5 * p + l - 1) + g + 1)
                        if l > 1:
                            pe.wait_ge((r_ttv, r_tta)[g], 4 * p + l - 1)
                        for q in range(4 * g, 4 * g + 4):
                            left, right = (inv_t, prod) if l < 5 else (prod, inv_t)
                            mm = pe.matmul(bank[4 + g][:, q % 4 * P:(q % 4 + 1) * P], left[:, q, :], right[:, q, :],
                                           start=True, stop=True)
                        mm.then_inc(r_gm if l < 5 else r_lm, 1)
                elif kind == "turn":
                    for g in range(2):
                        pe.wait_ge(r_inv, 8 * p + 2 * (seg[2] - 1) + g + 1)
                        for q in range(4 * g, 4 * g + 4):
                            mm = pe.transpose(bank[4 + g][:, q % 4 * P:(q % 4 + 1) * P], inv[:, q, :], ident[:, :])
                        mm.then_inc(r_tt, 1)
                elif kind == "wu":
                    pe.wait_ge(r_xv, 2 * p + 2)
                    for hd in range(2):
                        pe.wait_ge(r_last, 2 * p + hd + 1)
                        for c in range(TT):
                            mm = pe.matmul(bank[2 + hd][:, c * P:(c + 1) * P], inv_t[:, 4 * hd + c, :],
                                           ax_tok[:, c, :, HD * hd:HD * hd + HD], start=True, stop=True)
                        mm.then_inc(r_wm, 1)
                elif kind == "w_back":
                    pe.wait_ge(r_wt, 2 * p + 2)
                    if p >= 2:
                        pe.wait_ge(r_z2, p - 1)
                    for c in range(TT):
                        mm = pe.transpose(bank[1][:, c * P:(c + 1) * P], w_tok[:, c, :], ident[:, :])
                    mm.then_inc(r_wtm, 1)
                elif kind == "step":
                    n = seg[2]
                    at_, rows = NC * p + n, slice(CH * (n % 2), CH * (n % 2) + CH)
                    if n == 0:
                        pe.wait_ge(r_s0, p + 1)
                        pe.wait_ge(r_w, p + 1)
                        pe.wait_ge(r_u0, 2 * p + 2)
                    if at_:
                        pe.wait_ge(r_s2, at_)
                        pe.wait_ge(r_y, at_)
                    pe.matmul(bank[6][rows, 0:P], w_f[:, n * CH:(n + 1) * CH], state[:, n % 2, :], start=True,
                              stop=True).then_inc(r_um, 1)
                elif kind == "out":
                    n = seg[2]
                    c, e, toks = n // 2, n % 2, slice(n * CH, (n + 1) * CH)
                    pe.wait_ge(r_u, NC * p + n + 1)
                    pe.matmul(bank[7][:, 0:P], bk_tok[:, p % 2, n, :], uv[:, p % 2, e, (c + e) % TT, :], start=True,
                              stop=True).then_inc(r_sm, 1)
                    pe.wait_ge(r_rt, p + 1)
                    y = bank[6][:, 256:256 + CH]
                    pe.matmul(y, state[:, n % 2, :], rp[:, toks], start=True, stop=False)
                    for hd in range(2):
                        f = slice(HD * hd, HD * hd + HD)
                        mm = pe.matmul(y[f, :], uv[:, p % 2, e, (c + e) % TT, f], ar[:, p % 2, hd, n, 1, :], start=False, stop=True)
                    mm.then_inc(r_ym, 1)
            square(WO, T_WO, H_WO)
            norm_sum(3)
            swiglu(1, FI1, FO1, T_FI1, T_FO1, H_FFN1)
            norm_sum(4)
        for k in range(KT):
            pe.wait_ge(s_u, KT * LAST + k + 1)
            if k >= 4:
                pe.wait_ge(s_y, k - 3)
            for t in range(TT):
                mm = pe.transpose(bank[k % 4][:, t * P:(t + 1) * P], ring[:, k % 4, t * P:(t + 1) * P], ident[:, :])
            mm.then_inc(s_y_t, 1)


_INS = ["x", "c", "attn_w_in", "attn_b_f", "attn_w_out", "rwkv_mu", "rwkv_w_r", "rwkv_w_k", "rwkv_w_v", "rwkv_w_o",
        "rwkv_w0", "rwkv_w1", "rwkv_w2", "rwkv_a0", "rwkv_a1", "rwkv_a2", "rwkv_g1", "rwkv_g2", "rwkv_k_k", "rwkv_k_a",
        "rwkv_r_k", "rwkv_ln_w", "rwkv_ln_b", "mod_w", "mod_b", "norm_mix", "norm_ffn", "ffn_w_in", "ffn_w_out",
        "norm_final"]


def kernel(**inputs):
    import numpy as np
    import concourse.bacc as bacc
    from concourse.bass_utils import run_bass_kernel_spmd

    nc = bacc.Bacc("TRN2", target_bir_lowering=False, num_devices=1)
    arrays, aps = {}, {}
    for name in _INS:
        arr = np.ascontiguousarray(inputs[name])
        arrays[f"in_{name}"] = arr
        aps[name] = nc.dram_tensor(f"in_{name}", arr.shape, mybir.dt.from_np(arr.dtype), kind="ExternalInput").ap()
    out = nc.dram_tensor("out", (1, S, D), F32, kind="ExternalOutput").ap()
    build(nc, aps, out)
    return run_bass_kernel_spmd(nc, [arrays], core_ids=[0]).results[0]["out"]
```
